# Optimizing a Trainium2 kernel written in Bass

```python
import jax, jax.numpy as jnp
from jax import lax
import numpy as np
import math

D_MODEL = 1024
BATCH = 1
SEQ = 256
DEPTH = 2

D_CONV_A = 512
CONV_A_WIDTH = 3
D_CONV_B = 512
CONV_B_WIDTH = 31
N_HEADS = 16
HEAD_DIM = 64
D_ATTN = N_HEADS * HEAD_DIM
BLOCK_Q = 128
N_GROUPS = 4
EXPERTS_PER_GROUP = 8
N_EXPERTS = N_GROUPS * EXPERTS_PER_GROUP
TOP_K = 2
D_EXPERT = 512
ROW_CHUNK = 256
LN_EPS = 1e-5
DEEPNORM_ALPHA = (2 * DEPTH) ** 0.25
DEEPNORM_BETA = (8 * DEPTH) ** -0.25

N_EVEN = (DEPTH + 1) // 2
N_ODD = DEPTH // 2
D_IN_EVEN = 3 * D_CONV_A + 2 * D_CONV_B
D_MIX_EVEN = D_CONV_A + D_CONV_B


def layer_norm(x, g, b):
    xf = x.astype(jnp.float32)
    mu = jnp.mean(xf, axis=-1, keepdims=True)
    var = jnp.mean(jnp.square(xf - mu), axis=-1, keepdims=True)
    y = (xf - mu) * lax.rsqrt(var + LN_EPS)
    return (y * g + b).astype(x.dtype)

def causal_depthwise_conv(x, w):
    k = w.shape[0]
    return lax.conv_general_dilated(
        x, w[:, None, :].astype(x.dtype), window_strides=(1,), padding=[(k - 1, 0)],
        dimension_numbers=("NWC", "WIO", "NWC"), feature_group_count=x.shape[-1])

def conv_mixers(x, w_in, conv_a, conv_b_w, conv_b_bias, norm_b_g, norm_b_b, w_out):
    u = jnp.einsum("bsd,de->bse", x, w_in)
    a_b, a_c, a_v, b_val, b_gate = jnp.split(
        u, [D_CONV_A, 2 * D_CONV_A, 3 * D_CONV_A, 3 * D_CONV_A + D_CONV_B], axis=-1)
    y_a = a_b * causal_depthwise_conv(a_c * a_v, conv_a)
    g = b_val * jax.nn.sigmoid(b_gate)
    g = causal_depthwise_conv(g, conv_b_w) + conv_b_bias
    y_b = jax.nn.silu(layer_norm(g, norm_b_g, norm_b_b))
    return jnp.einsum("bse,ed->bsd", jnp.concatenate([y_a, y_b], axis=-1), w_out)

def stick_breaking_attention(x, w_qkv, w_o):
    b, s, _ = x.shape
    qkv = jnp.einsum("bsd,de->bse", x, w_qkv).reshape(b, s, 3, N_HEADS, HEAD_DIM)
    q = qkv[:, :, 0].transpose(0, 2, 1, 3)
    k = qkv[:, :, 1].transpose(0, 2, 1, 3)
    v = qkv[:, :, 2].transpose(0, 2, 1, 3)
    scale = HEAD_DIM ** -0.5
    outs = []
    for blk in range(s // BLOCK_Q):
        q0 = blk * BLOCK_Q
        kv_len = q0 + BLOCK_Q
        qb = q[:, :, q0:kv_len]
        kb = k[:, :, :kv_len]
        vb = v[:, :, :kv_len]
        z = jnp.einsum("bhqd,bhkd->bhqk", qb, kb,
                       preferred_element_type=jnp.float32) * scale
        t_idx = q0 + jnp.arange(BLOCK_Q)[:, None]
        s_idx = jnp.arange(kv_len)[None, :]
        causal = s_idx < t_idx
        log_keep = jnp.where(causal, jax.nn.log_sigmoid(-z), 0.0)
        later = lax.cumsum(log_keep, axis=3, reverse=True) - log_keep
        a = jnp.where(causal, jnp.exp(jax.nn.log_sigmoid(z) + later), 0.0)
        outs.append(jnp.einsum("bhqk,bhkd->bhqd", a.astype(vb.dtype), vb))
    o = jnp.concatenate(outs, axis=2).transpose(0, 2, 1, 3).reshape(b, s, D_ATTN)
    return jnp.einsum("bse,ed->bsd", o, w_o)

def hierarchical_moe(x, rg_w, rg_b, re_w, re_b, w_up, w_down):
    b, s, d = x.shape
    h = x.reshape(-1, d)
    t = h.shape[0]
    g_logits = jnp.matmul(h, rg_w).astype(jnp.float32) + rg_b
    grp = jnp.argmax(g_logits, axis=-1)
    g_gate = jnp.take_along_axis(jax.nn.softmax(g_logits, axis=-1), grp[:, None], axis=-1)
    e_logits = (jnp.matmul(h, re_w).astype(jnp.float32) + re_b).reshape(t, N_GROUPS, EXPERTS_PER_GROUP)
    e_logits = jnp.take_along_axis(e_logits, grp[:, None, None], axis=1)[:, 0]
    top_val, top_idx = lax.top_k(e_logits, TOP_K)
    weights = (g_gate * jax.nn.softmax(top_val, axis=-1)).reshape(-1)
    ids = (grp[:, None] * EXPERTS_PER_GROUP + top_idx).reshape(-1).astype(jnp.int32)
    n_assign = t * TOP_K
    order = jnp.argsort(ids)
    sorted_ids = ids[order]
    tok = order // TOP_K
    sizes = jnp.bincount(ids, length=N_EXPERTS)
    padded = (sizes + ROW_CHUNK - 1) // ROW_CHUNK * ROW_CHUNK
    pad_end = jnp.cumsum(padded)
    pad_start = pad_end - padded
    start = jnp.cumsum(sizes) - sizes
    dest = pad_start[sorted_ids] + jnp.arange(n_assign) - start[sorted_ids]
    n_chunks = -(-n_assign // ROW_CHUNK) + N_EXPERTS
    rows = jnp.zeros((n_chunks * ROW_CHUNK, d), h.dtype).at[dest].set(h[tok])
    chunk_expert = jnp.minimum(
        jnp.searchsorted(pad_end, jnp.arange(n_chunks) * ROW_CHUNK, side="right"), N_EXPERTS - 1)

    def expert_chunk(args):
        xc, e = args
        gate, up = jnp.split(jnp.matmul(xc, w_up[e]), 2, axis=-1)
        return jnp.matmul(jax.nn.silu(gate) * up, w_down[e])

    y_rows = lax.map(expert_chunk, (rows.reshape(n_chunks, ROW_CHUNK, d), chunk_expert))
    y = y_rows.reshape(-1, d)[dest] * weights[order][:, None].astype(h.dtype)
    out = jnp.zeros((t, d), h.dtype).at[tok].add(y)
    return out.reshape(b, s, d)

def first_inputs(seed: int = 0) -> dict:
    key = jax.random.key(seed)
    ks = jax.random.split(key, 24)
    nrm = jax.random.normal
    f32 = jnp.float32
    x = nrm(ks[0], (BATCH, SEQ, D_MODEL), f32)
    even_w_in = nrm(ks[1], (N_EVEN, D_MODEL, D_IN_EVEN), f32) * D_MODEL ** -0.5
    even_conv_a = nrm(ks[2], (N_EVEN, CONV_A_WIDTH, D_CONV_A), f32) * CONV_A_WIDTH ** -0.5
    even_conv_b_w = nrm(ks[3], (N_EVEN, CONV_B_WIDTH, D_CONV_B), f32) * CONV_B_WIDTH ** -0.5
    even_conv_b_bias = nrm(ks[4], (N_EVEN, D_CONV_B), f32) * 0.02
    even_norm_b_g = 1.0 + 0.1 * nrm(ks[5], (N_EVEN, D_CONV_B), f32)
    even_norm_b_b = 0.02 * nrm(ks[6], (N_EVEN, D_CONV_B), f32)
    even_w_out = nrm(ks[7], (N_EVEN, D_MIX_EVEN, D_MODEL), f32) * (D_MIX_EVEN ** -0.5 * DEEPNORM_BETA)
    v_scale = jnp.concatenate([jnp.ones((2 * D_ATTN,), f32), jnp.full((D_ATTN,), DEEPNORM_BETA, f32)])
    odd_w_qkv = nrm(ks[8], (N_ODD, D_MODEL, 3 * D_ATTN), f32) * D_MODEL ** -0.5 * v_scale
    odd_w_o = nrm(ks[9], (N_ODD, D_ATTN, D_MODEL), f32) * (D_ATTN ** -0.5 * DEEPNORM_BETA)
    ln_mix_g = 1.0 + 0.1 * nrm(ks[10], (DEPTH, D_MODEL), f32)
    ln_mix_b = 0.02 * nrm(ks[11], (DEPTH, D_MODEL), f32)
    ln_ffn_g = 1.0 + 0.1 * nrm(ks[12], (DEPTH, D_MODEL), f32)
    ln_ffn_b = 0.02 * nrm(ks[13], (DEPTH, D_MODEL), f32)
    router_group_w = nrm(ks[14], (DEPTH, D_MODEL, N_GROUPS), f32) * D_MODEL ** -0.5
    router_group_b = 0.01 * nrm(ks[15], (DEPTH, N_GROUPS), f32)
    router_expert_w = nrm(ks[16], (DEPTH, D_MODEL, N_EXPERTS), f32) * D_MODEL ** -0.5
    router_expert_b = 0.01 * nrm(ks[17], (DEPTH, N_EXPERTS), f32)
    expert_w_up = nrm(ks[18], (DEPTH, N_EXPERTS, D_MODEL, 2 * D_EXPERT), f32) * D_MODEL ** -0.5
    expert_w_down = nrm(ks[19], (DEPTH, N_EXPERTS, D_EXPERT, D_MODEL), f32) * (D_EXPERT ** -0.5 * DEEPNORM_BETA)
    return {"x": x, "even_w_in": even_w_in, "even_conv_a": even_conv_a,
            "even_conv_b_w": even_conv_b_w, "even_conv_b_bias": even_conv_b_bias,
            "even_norm_b_g": even_norm_b_g, "even_norm_b_b": even_norm_b_b,
            "even_w_out": even_w_out, "odd_w_qkv": odd_w_qkv, "odd_w_o": odd_w_o,
            "ln_mix_g": ln_mix_g, "ln_mix_b": ln_mix_b, "ln_ffn_g": ln_ffn_g, "ln_ffn_b": ln_ffn_b,
            "router_group_w": router_group_w, "router_group_b": router_group_b,
            "router_expert_w": router_expert_w, "router_expert_b": router_expert_b,
            "expert_w_up": expert_w_up, "expert_w_down": expert_w_down}

def first_block(x, even_w_in, even_conv_a, even_conv_b_w, even_conv_b_bias, even_norm_b_g,
              even_norm_b_b, even_w_out, odd_w_qkv, odd_w_o, ln_mix_g, ln_mix_b, ln_ffn_g,
              ln_ffn_b, router_group_w, router_group_b, router_expert_w, router_expert_b,
              expert_w_up, expert_w_down):
    for layer in range(DEPTH):
        i = layer // 2
        if layer % 2 == 0:
            mix = conv_mixers(x, even_w_in[i], even_conv_a[i], even_conv_b_w[i],
                              even_conv_b_bias[i], even_norm_b_g[i], even_norm_b_b[i],
                              even_w_out[i])
        else:
            mix = stick_breaking_attention(x, odd_w_qkv[i], odd_w_o[i])
        x = layer_norm(DEEPNORM_ALPHA * x + mix, ln_mix_g[layer], ln_mix_b[layer])
        ffn = hierarchical_moe(x, router_group_w[layer], router_group_b[layer],
                               router_expert_w[layer], router_expert_b[layer],
                               expert_w_up[layer], expert_w_down[layer])
        x = layer_norm(DEEPNORM_ALPHA * x + ffn, ln_ffn_g[layer], ln_ffn_b[layer])
    return x


MEM_LEN = 256
MLA_HEADS = 6
MLA_NOPE = 64
MLA_ROPE = 32
MLA_V = 64
MLA_Q_RANK = 256
MLA_KV_RANK = 128
ROPE_THETA = 10000.0
DIFF_HEADS = 6
DIFF_HD = 32
MOBA_HEADS = 4
MOBA_HD = 64
MOBA_BLOCK = 256
MOBA_TOPK = 3
MOBA_Q_CHUNK = 32
Q_BLOCK = 128
CROSS_HEADS = 4
CROSS_HD = D_MODEL // CROSS_HEADS
D_FF = 4 * D_MODEL
EPS = 1e-6
NEG = -1e30
N_ALIBI = DIFF_HEADS + MOBA_HEADS

C_Q = MLA_Q_RANK
C_KV = MLA_KV_RANK
C_KR = MLA_ROPE
C_DIFF = DIFF_HEADS * 2 * DIFF_HD
C_MOBA = MOBA_HEADS * MOBA_HD
D_IN = C_Q + C_KV + C_KR + 3 * C_DIFF + 3 * C_MOBA
D_MIX = MLA_HEADS * MLA_V + DIFF_HEADS * 2 * DIFF_HD + MOBA_HEADS * MOBA_HD


def rmsnorm(x, g):
    xf = x.astype(jnp.float32)
    y = xf * lax.rsqrt(jnp.mean(xf * xf, axis=-1, keepdims=True) + EPS)
    return (y * g.astype(jnp.float32)).astype(x.dtype)

def alibi_slopes():
    return jnp.asarray([2.0 ** (-8.0 * (h + 1) / N_ALIBI) for h in range(N_ALIBI)], jnp.float32)

def apply_rope(x, pos):
    half = x.shape[-1] // 2
    inv = ROPE_THETA ** (-jnp.arange(half, dtype=jnp.float32) / half)
    ang = pos.astype(jnp.float32)[:, None, :, None] * inv
    cos, sin = jnp.cos(ang), jnp.sin(ang)
    xf = x.astype(jnp.float32)
    x1, x2 = xf[..., :half], xf[..., half:]
    return jnp.concatenate([x1 * cos - x2 * sin, x1 * sin + x2 * cos], axis=-1).astype(x.dtype)

def to_heads(t, hd):
    B, S, _ = t.shape
    return t.reshape(B, S, -1, hd).transpose(0, 2, 1, 3)

def from_heads(t):
    B, H, S, d = t.shape
    return t.transpose(0, 2, 1, 3).reshape(B, S, H * d)

def sweep_query_blocks(body, B, H, S, dv):
    out = lax.map(body, jnp.arange(S // Q_BLOCK, dtype=jnp.int32) * Q_BLOCK)
    return jnp.moveaxis(out, 0, 2).reshape(B, H, S, dv)

def mla_causal_attention(q, k, v):
    B, H, S, dqk = q.shape
    scale = dqk ** -0.5
    kidx = jnp.arange(S)

    def body(start):
        qc = lax.dynamic_slice_in_dim(q, start, Q_BLOCK, axis=2)
        s = jnp.einsum('bhqd,bhkd->bhqk', qc, k, preferred_element_type=jnp.float32) * scale
        qidx = start + jnp.arange(Q_BLOCK)
        s = jnp.where(kidx[None, :] <= qidx[:, None], s, NEG)
        p = jax.nn.softmax(s, axis=-1)
        return jnp.einsum('bhqk,bhkd->bhqd', p.astype(v.dtype), v)

    return sweep_query_blocks(body, B, H, S, v.shape[-1])

def diff_causal_attention(q1, q2, k1, k2, v, pos, slopes, lam):
    B, H, S, d = q1.shape
    scale = d ** -0.5
    kidx = jnp.arange(S)

    def body(start):
        pq = lax.dynamic_slice_in_dim(pos, start, Q_BLOCK, axis=1)
        qidx = start + jnp.arange(Q_BLOCK)
        causal = kidx[None, :] <= qidx[:, None]
        dist = jnp.abs(pq[:, :, None] - pos[:, None, :]).astype(jnp.float32)
        bias = -slopes[None, :, None, None] * dist[:, None]

        def probs(qf, k):
            qc = lax.dynamic_slice_in_dim(qf, start, Q_BLOCK, axis=2)
            s = jnp.einsum('bhqd,bhkd->bhqk', qc, k, preferred_element_type=jnp.float32) * scale + bias
            return jax.nn.softmax(jnp.where(causal, s, NEG), axis=-1)

        p = probs(q1, k1) - lam * probs(q2, k2)
        return jnp.einsum('bhqk,bhkd->bhqd', p.astype(v.dtype), v)

    return sweep_query_blocks(body, B, H, S, v.shape[-1])

def moba_causal_attention(q, k, v, pos, slopes):
    B, H, S, dh = q.shape
    NB = -(-S // MOBA_BLOCK)
    pad = NB * MOBA_BLOCK - S
    kb = jnp.pad(k, ((0, 0), (0, 0), (0, pad), (0, 0))).reshape(B, H, NB, MOBA_BLOCK, dh)
    vb = jnp.pad(v, ((0, 0), (0, 0), (0, pad), (0, 0))).reshape(B, H, NB, MOBA_BLOCK, dh)
    pb = jnp.pad(pos, ((0, 0), (0, pad)), mode='edge').reshape(B, NB, MOBA_BLOCK)
    kmean = jnp.mean(kb.astype(jnp.float32), axis=3)
    K = min(MOBA_TOPK, NB)
    scale = dh ** -0.5
    bi = jnp.arange(B)[:, None, None, None]
    hi = jnp.arange(H)[None, :, None, None]
    m5 = slopes[None, :, None, None, None]

    def body(start):
        qc = lax.dynamic_slice_in_dim(q, start, MOBA_Q_CHUNK, axis=2)
        pq = lax.dynamic_slice_in_dim(pos, start, MOBA_Q_CHUNK, axis=1)
        qidx = start + jnp.arange(MOBA_Q_CHUNK)
        ob = start // MOBA_BLOCK
        gate = jnp.einsum('bhqd,bhnd->bhqn', qc.astype(jnp.float32), kmean)
        gate = jnp.where(jnp.arange(NB) < ob, gate, NEG)
        _, sel = lax.top_k(gate, K)
        valid = jnp.arange(K) < ob
        kg = kb[bi, hi, sel]
        vg = vb[bi, hi, sel]
        pg = pb[bi, sel]
        s_sel = jnp.einsum('bhqd,bhqkjd->bhqkj', qc, kg, preferred_element_type=jnp.float32) * scale
        s_sel = s_sel - m5 * jnp.abs(pq[:, None, :, None, None] - pg).astype(jnp.float32)
        s_sel = jnp.where(valid[None, None, None, :, None], s_sel, NEG)
        s_sel = s_sel.reshape(B, H, MOBA_Q_CHUNK, K * MOBA_BLOCK)
        ko = lax.dynamic_index_in_dim(kb, ob, axis=2, keepdims=False)
        vo = lax.dynamic_index_in_dim(vb, ob, axis=2, keepdims=False)
        po = lax.dynamic_index_in_dim(pb, ob, axis=1, keepdims=False)
        s_own = jnp.einsum('bhqd,bhjd->bhqj', qc, ko, preferred_element_type=jnp.float32) * scale
        s_own = s_own - slopes[None, :, None, None] * jnp.abs(pq[:, None, :, None] - po[:, None, None, :]).astype(jnp.float32)
        kidx = ob * MOBA_BLOCK + jnp.arange(MOBA_BLOCK)
        s_own = jnp.where(kidx[None, :] <= qidx[:, None], s_own, NEG)
        p = jax.nn.softmax(jnp.concatenate([s_sel, s_own], axis=-1), axis=-1).astype(v.dtype)
        p_sel = p[..., :K * MOBA_BLOCK].reshape(B, H, MOBA_Q_CHUNK, K, MOBA_BLOCK)
        return (jnp.einsum('bhqkj,bhqkjd->bhqd', p_sel, vg)
                + jnp.einsum('bhqj,bhjd->bhqd', p[..., K * MOBA_BLOCK:], vo))

    out = lax.map(body, jnp.arange(S // MOBA_Q_CHUNK, dtype=jnp.int32) * MOBA_Q_CHUNK)
    return jnp.moveaxis(out, 0, 2).reshape(B, H, S, dh)

def hybrid_mixer(n, pos, layer_idx, w_in, q_norm, w_uq, kv_norm, w_ukv,
                 lq1, lk1, lq2, lk2, sub_norm, w_out):
    B, S, _ = n.shape
    proj = n @ w_in
    cuts = [int(c) for c in np.cumsum([C_Q, C_KV, C_KR, C_DIFF, C_DIFF, C_DIFF, C_MOBA, C_MOBA])]
    c_q, c_kv, k_r, dq, dk, dv, mq, mk, mv = jnp.split(proj, cuts, axis=-1)
    slopes = alibi_slopes()

    qh = to_heads(rmsnorm(c_q, q_norm) @ w_uq, MLA_NOPE + MLA_ROPE)
    kvh = to_heads(rmsnorm(c_kv, kv_norm) @ w_ukv, MLA_NOPE + MLA_V)
    q_rope = apply_rope(qh[..., MLA_NOPE:], pos)
    k_rope = apply_rope(k_r[:, None], pos)
    q_a = jnp.concatenate([qh[..., :MLA_NOPE], q_rope], axis=-1)
    k_a = jnp.concatenate([kvh[..., :MLA_NOPE],
                           jnp.broadcast_to(k_rope, (B, MLA_HEADS, S, MLA_ROPE))], axis=-1)
    o_a = mla_causal_attention(q_a, k_a, kvh[..., MLA_NOPE:])

    dqh, dkh, dvh = to_heads(dq, 2 * DIFF_HD), to_heads(dk, 2 * DIFF_HD), to_heads(dv, 2 * DIFF_HD)
    lam_init = 0.8 - 0.6 * math.exp(-0.3 * layer_idx)
    lam = (jnp.exp(jnp.sum(lq1.astype(jnp.float32) * lk1.astype(jnp.float32)))
           - jnp.exp(jnp.sum(lq2.astype(jnp.float32) * lk2.astype(jnp.float32))) + lam_init)
    o_b = diff_causal_attention(dqh[..., :DIFF_HD], dqh[..., DIFF_HD:],
                                dkh[..., :DIFF_HD], dkh[..., DIFF_HD:],
                                dvh, pos, slopes[:DIFF_HEADS], lam)
    o_b = rmsnorm(o_b, sub_norm) * (1.0 - lam_init)

    o_c = moba_causal_attention(to_heads(mq, MOBA_HD), to_heads(mk, MOBA_HD),
                                to_heads(mv, MOBA_HD), pos, slopes[DIFF_HEADS:])

    o = jnp.concatenate([from_heads(o_a), from_heads(o_b), from_heads(o_c)], axis=-1)
    return o @ w_out

def memory_cross_attention(n, mem_n, wq, wkv, wo):
    q = to_heads(n @ wq, CROSS_HD)
    kv = mem_n @ wkv
    k = to_heads(kv[..., :D_MODEL], CROSS_HD)
    v = to_heads(kv[..., D_MODEL:], CROSS_HD)
    s = jnp.einsum('bhqd,bhmd->bhqm', q, k, preferred_element_type=jnp.float32) * (CROSS_HD ** -0.5)
    p = jax.nn.softmax(s, axis=-1).astype(v.dtype)
    return from_heads(jnp.einsum('bhqm,bhmd->bhqd', p, v)) @ wo

def squared_relu_mlp(n, w1, w2):
    return jnp.square(jax.nn.relu(n @ w1)) @ w2

def second_inputs(seed: int = 0) -> dict:
    key = jax.random.key(seed)
    k = jax.random.split(key, 24)
    L = DEPTH
    f32 = jnp.float32
    nrm = lambda kk, shape, scale: jax.random.normal(kk, shape, f32) * scale
    gain = lambda kk, shape: 1.0 + 0.02 * jax.random.normal(kk, shape, f32)
    offset = jax.random.randint(k[2], (BATCH, 1), 0, 1024, dtype=jnp.int32)
    positions = offset + jnp.arange(SEQ, dtype=jnp.int32)[None, :]
    return {
        "x": nrm(k[0], (BATCH, SEQ, D_MODEL), 1.0),
        "mem": nrm(k[1], (BATCH, MEM_LEN, D_MODEL), 1.0),
        "positions": positions,
        "attn_norm": gain(k[3], (L, D_MODEL)),
        "w_in": nrm(k[4], (L, D_MODEL, D_IN), D_MODEL ** -0.5),
        "mla_q_norm": gain(k[5], (L, MLA_Q_RANK)),
        "mla_w_uq": nrm(k[6], (L, MLA_Q_RANK, MLA_HEADS * (MLA_NOPE + MLA_ROPE)), MLA_Q_RANK ** -0.5),
        "mla_kv_norm": gain(k[7], (L, MLA_KV_RANK)),
        "mla_w_ukv": nrm(k[8], (L, MLA_KV_RANK, MLA_HEADS * (MLA_NOPE + MLA_V)), MLA_KV_RANK ** -0.5),
        "diff_lambda_q1": nrm(k[9], (L, DIFF_HD), 0.1),
        "diff_lambda_k1": nrm(k[10], (L, DIFF_HD), 0.1),
        "diff_lambda_q2": nrm(k[11], (L, DIFF_HD), 0.1),
        "diff_lambda_k2": nrm(k[12], (L, DIFF_HD), 0.1),
        "diff_sub_norm": gain(k[13], (L, 2 * DIFF_HD)),
        "w_out": nrm(k[14], (L, D_MIX, D_MODEL), D_MIX ** -0.5),
        "cross_norm": gain(k[15], (L, D_MODEL)),
        "mem_norm": gain(k[16], (L, D_MODEL)),
        "cross_wq": nrm(k[17], (L, D_MODEL, D_MODEL), D_MODEL ** -0.5),
        "cross_wkv": nrm(k[18], (L, D_MODEL, 2 * D_MODEL), D_MODEL ** -0.5),
        "cross_wo": nrm(k[19], (L, D_MODEL, D_MODEL), D_MODEL ** -0.5),
        "mlp_norm": gain(k[20], (L, D_MODEL)),
        "mlp_w1": nrm(k[21], (L, D_MODEL, D_FF), D_MODEL ** -0.5),
        "mlp_w2": nrm(k[22], (L, D_FF, D_MODEL), D_FF ** -0.5),
        "final_norm": gain(k[23], (D_MODEL,)),
    }

def second_block(x, mem, positions, attn_norm, w_in, mla_q_norm, mla_w_uq, mla_kv_norm, mla_w_ukv,
              diff_lambda_q1, diff_lambda_k1, diff_lambda_q2, diff_lambda_k2, diff_sub_norm, w_out,
              cross_norm, mem_norm, cross_wq, cross_wkv, cross_wo, mlp_norm, mlp_w1, mlp_w2, final_norm):
    h = x
    for l in range(DEPTH):
        h = h + hybrid_mixer(rmsnorm(h, attn_norm[l]), positions, l, w_in[l],
                             mla_q_norm[l], mla_w_uq[l], mla_kv_norm[l], mla_w_ukv[l],
                             diff_lambda_q1[l], diff_lambda_k1[l], diff_lambda_q2[l], diff_lambda_k2[l],
                             diff_sub_norm[l], w_out[l])
        h = h + memory_cross_attention(rmsnorm(h, cross_norm[l]), rmsnorm(mem, mem_norm[l]),
                                       cross_wq[l], cross_wkv[l], cross_wo[l])
        h = h + squared_relu_mlp(rmsnorm(h, mlp_norm[l]), mlp_w1[l], mlp_w2[l])
    return rmsnorm(h, final_norm)


def setup_inputs(seed=0):
    out = dict(first_inputs(seed))
    for name, value in second_inputs(seed + 1).items():
        if name != "x":
            out[name + "_2"] = value
    return out


def reference(
    x, even_w_in, even_conv_a, even_conv_b_w, even_conv_b_bias, even_norm_b_g, even_norm_b_b,
    even_w_out, odd_w_qkv, odd_w_o, ln_mix_g, ln_mix_b, ln_ffn_g, ln_ffn_b, router_group_w,
    router_group_b, router_expert_w, router_expert_b, expert_w_up, expert_w_down, mem_2,
    positions_2, attn_norm_2, w_in_2, mla_q_norm_2, mla_w_uq_2, mla_kv_norm_2, mla_w_ukv_2,
    diff_lambda_q1_2, diff_lambda_k1_2, diff_lambda_q2_2, diff_lambda_k2_2, diff_sub_norm_2,
    w_out_2, cross_norm_2, mem_norm_2, cross_wq_2, cross_wkv_2, cross_wo_2, mlp_norm_2,
    mlp_w1_2, mlp_w2_2, final_norm_2,
):
    x = first_block(
        x, even_w_in, even_conv_a, even_conv_b_w, even_conv_b_bias, even_norm_b_g,
        even_norm_b_b, even_w_out, odd_w_qkv, odd_w_o, ln_mix_g, ln_mix_b, ln_ffn_g, ln_ffn_b,
        router_group_w, router_group_b, router_expert_w, router_expert_b, expert_w_up,
        expert_w_down,
    )
    return second_block(
        x, mem_2, positions_2, attn_norm_2, w_in_2, mla_q_norm_2, mla_w_uq_2, mla_kv_norm_2,
        mla_w_ukv_2, diff_lambda_q1_2, diff_lambda_k1_2, diff_lambda_q2_2, diff_lambda_k2_2,
        diff_sub_norm_2, w_out_2, cross_norm_2, mem_norm_2, cross_wq_2, cross_wkv_2, cross_wo_2,
        mlp_norm_2, mlp_w1_2, mlp_w2_2, final_norm_2,
    )


_drawn_inputs = setup_inputs


def setup_inputs(seed=0):
    import zlib

    import numpy as np

    out = dict(_drawn_inputs(seed))
    spreads = {}
    factors = {'even_conv_b_bias': 3.222,
     'even_norm_b_b': 6.25,
     'router_group_b': 8.0,
     'router_expert_b': 6.47,
     'attn_norm_2': 3.2,
     'mla_q_norm_2': 8.0,
     'mla_kv_norm_2': 8.0,
     'diff_lambda_q1_2': 3.32,
     'diff_lambda_k1_2': 8.0,
     'diff_sub_norm_2': 5.436,
     'cross_norm_2': 8.0,
     'mem_norm_2': 8.0,
     'final_norm_2': 2.86}
    for name, (base, spread) in spreads.items():
        noise = np.random.default_rng([zlib.crc32(name.encode()), seed]).standard_normal(out[name].shape)
        drawn = base * np.exp(spread * noise) if base else spread * noise
        out[name] = __import__('jax').numpy.asarray(drawn.astype(out[name].dtype))
    for name, factor in factors.items():
        out[name] = (out[name] * factor).astype(out[name].dtype)
    return out
```

```python
import math
from contextlib import ExitStack

import concourse.bass as bass
from concourse import mybir

F32 = mybir.dt.float32
F32R = mybir.dt.float32r
I32 = mybir.dt.int32
ALU = mybir.AluOpType
ACT = mybir.ActivationFunctionType
AX = mybir.AxisListType.X

P = 128
D = 1024
KT = D // P
T = 256
NH2 = T // P
DEPTH = 2
ALPHA = (2 * DEPTH) ** 0.25
LN_EPS, RMS_EPS = 1e-5, 1e-6
NEG = -1e30

E_IN, CONV_A, CONV_B = 2560, 3, 31
SB_HEADS, HD = 16, 64
NG, EPG = 4, 8
NE = NG * EPG
DE = 512
NR = NG + NE
CAP = 64

MLA_H, MLA_QK, MLA_NOPE, MLA_ROPE = 6, 96, 64, 32
QR, KVR = 256, 128
DIFF_H, DIFF_HD = 6, 32
MOBA_H = 4
CROSS_H, CROSS_HD = 4, 256
FF = 4096
N_ALIBI = DIFF_H + MOBA_H
SLOPES = [2.0 ** (-8.0 * (h + 1) / N_ALIBI) for h in range(N_ALIBI)]
BLK = 3 * P

TK = 4
TW = 512
RAW = 6
CNV = 3
EXPERT_TILES = 6

ROW_ATTN, ROW_CROSS, ROW_MEM, ROW_MLP, ROW_Q, ROW_KV, ROWS_LAYER = 0, 8, 16, 24, 32, 34, 35
ROW_CONVA = DEPTH * ROWS_LAYER
ROW_BIAS = ROW_CONVA + 4 * CONV_A
ROW_NBG = ROW_BIAS + 4
ROW_NBB = ROW_NBG + 4
ROWS_A = ROW_NBB + 4

PROJ = [(0, 416, False), (416, 384, True), (800, 384, True), (1184, 384, False), (1568, 512, True), (2080, 256, False)]


class Lane:

    def __init__(self, eng, link_sem=None):
        self.e, self.link_sem = eng, link_sem
        self.seen, self.loop = {}, None

    def wait(self, sem, k=1):
        self.seen[sem.name] = self.seen.get(sem.name, 0) + k
        if self.loop is None:
            self.e.wait_ge(sem, self.seen[sem.name])
        else:
            i, per, _ = self.loop
            self.e.wait_ge(sem, self.seen[sem.name] + per[sem.name] * i)

    def link(self, ins):
        ins.then_inc(self.link_sem, 1)
        self.wait(self.link_sem)

    def enter(self, i, per):
        self.loop = (i, per, dict(self.seen))

    def leave(self, rounds):
        _, per, before = self.loop
        for name, n in per.items():
            assert self.seen.get(name, 0) - before.get(name, 0) == n, (name, n, self.seen.get(name, 0) - before.get(name, 0))
            self.seen[name] = before.get(name, 0) + n * rounds
        self.loop = None


def weight_tiles(a):
    def cut(w, kg, c0, width, k=TK):
        return w[kg * TK * P:kg * TK * P + k * P, c0:c0 + width].rearrange("(k p) c -> p k c", p=P)

    def whole(w, kgs, width):
        return [cut(w, kg, c0, TW) for c0 in range(0, width, TW) for kg in range(kgs)]

    before = whole(a["even_w_in"][0], 2, E_IN) + whole(a["even_w_out"][0], 2, D)
    middle = whole(a["odd_w_qkv"][0], 2, 3 * D) + whole(a["odd_w_o"][0], 2, D)
    after = []
    for l in range(DEPTH):
        for c0, width, _ in PROJ:
            after += [cut(a["w_in_2"][l], kg, c0, width) for kg in range(2)]
        after += [cut(a["mla_w_uq_2"][l], 0, 0, 576, 2), cut(a["mla_w_ukv_2"][l], 0, 0, 768, 1)]
        after += whole(a["w_out_2"][l], 2, D)
        after += whole(a["cross_wkv_2"][l], 2, 2 * D) + whole(a["cross_wq_2"][l], 2, D)
        after += whole(a["cross_wo_2"][l], 2, D)
        for f in range(2):
            after += whole(a["mlp_w1_2"][l][:, f * FF // 2:(f + 1) * FF // 2], 2, FF // 2)
            after += whole(a["mlp_w2_2"][l][f * FF // 2:(f + 1) * FF // 2, :], FF // 2 // (TK * P), D)
    return before, middle, after


def build(nc, a, out):
    before, middle, after = weight_tiles(a)
    n_moe = NE * EXPERT_TILES
    moe_start = [len(before), len(before) + n_moe + len(middle)]
    n_total = len(before) + len(middle) + len(after) + 2 * n_moe
    shapes = {}
    for first, tiles in ((0, before), (moe_start[0] + n_moe, middle), (moe_start[1] + n_moe, after)):
        for j, ap in enumerate(tiles):
            shapes[first + j] = (ap.shape[1], ap.shape[2])

    def shape_of(n):
        return shapes.get(n, (TK, TW))

    ctx = ExitStack()
    with ctx:
        def sb(name, shape, dt=F32, scope=ctx):
            return scope.enter_context(nc.sbuf_tensor(name, shape, dt))

        def sem(name):
            return ctx.enter_context(nc.semaphore(name))

        PS = ctx.enter_context(nc.psum_tensor("PS", [P, 8, 512], F32))
        PSf = PS[:, :, :].rearrange("p b c -> p (b c)")

        raw = sb("raw", [P, RAW, TK * TW])
        w_hi = sb("w_hi", [P, CNV, TK * TW], F32R)
        w_lo = sb("w_lo", [P, CNV, TK * TW], F32R)
        x = sb("x", [P, NH2, D])
        ah = sb("ah", [P, KT, T], F32R)
        al = sb("al", [P, KT, T], F32R)
        ident = sb("ident", [P, P])
        ones = sb("ones", [P, P])
        tri_after = sb("tri_after", [P, P])
        tri_before = sb("tri_before", [P, P])
        keep_t = sb("keep_t", [P, P])
        drop_t = sb("drop_t", [P, P])
        causal = sb("causal", [P, BLK])
        fold = sb("fold", [P, CAP])
        slot_no = sb("slot_no", [P, 2 * CAP])
        prio = sb("prio", [P, EPG])
        colA = sb("colA", [P, P])
        colB = sb("colB", [P, 4 * CONV_B])
        inv_freq = sb("inv_freq", [P, MLA_ROPE // 2])
        stat = sb("stat", [P, 256])
        subn = sb("subn", [P, DEPTH, HD])
        flag = sb("flag", [P, DEPTH], I32)
        lam_rows = sb("lam_rows", [P, DEPTH * 4, DIFF_HD])
        lnp = sb("lnp", [P, 2, D])

        def scoped(specs):
            scope = ExitStack()
            got = [sb(name, shape, dt, scope) for name, shape, dt in specs]
            scope.close()
            return got

        prmA, prmB, xt0 = scoped([("prmA", [P, P], F32), ("prmB", [P, P], F32), ("xt0", [P, 4], F32)])
        uT, pa, pb, ya, gb, tc = scoped([
            ("uT", [P, 20, T], F32), ("pa", [P, 4, CONV_A - 1 + T], F32), ("pb", [P, 4, CONV_B - 1 + T], F32),
            ("ya", [P, 4, T], F32), ("gb", [P, 4, T], F32), ("tc", [P, 4, T], F32)])
        (xT, xh, xl, xe, hs, sil, af, aT, yh, yl, SS, Pm, rw, rbias, lg, rs, Mt, Wt, slot, wc, ovf_w, ovf_h, ovf_a, ovf_wt) = scoped([
            ("xT", [P, KT, T], F32), ("xh", [P, NH2, D], F32R), ("xl", [P, NH2, D], F32R),
            ("xe", [P, KT, 2 * CAP], F32R), ("hs", [P, 2 * DE], F32), ("sil", [P, 4, CAP], F32),
            ("af", [P, 4, CAP], F32), ("aT", [P, 4, 2 * CAP], F32R), ("yh", [P, D], F32R), ("yl", [P, D], F32R),
            ("SS", [P, NH2, 2 * CAP], F32R), ("Pm", [P, T], F32R), ("rw", [P, KT, NR], F32), ("rbias", [P, NR], F32),
            ("lg", [P, NH2, NR], F32), ("rs", [P, NH2, 64], F32), ("Mt", [P, NH2, NE], F32), ("Wt", [P, NH2, NE], F32),
            ("slot", [P, NH2, NE + 1], F32), ("wc", [P, 1], F32),
            ("ovf_w", [P, DE], F32), ("ovf_h", [P, 2 * DE], F32), ("ovf_a", [P, 4, P], F32), ("ovf_wt", [P, NH2, NE], F32)])
        qT1, kT1, v1, zs, sp_a, sp_l, aa = scoped([
            ("qT1", [P, KT, T], F32), ("kT1", [P, KT, T], F32), ("v1", [P, NH2, D], F32),
            ("zs", [P, 2, BLK], F32), ("sp_a", [P, 2, BLK], F32), ("sp_l", [P, 2, BLK], F32), ("aa", [P, 2, BLK], F32)])
        tabs = ExitStack()
        alibi = sb("alibi", [P, N_ALIBI, BLK], F32, tabs)
        cosT = sb("cosT", [P, NH2, MLA_ROPE // 2], F32, tabs)
        sinT = sb("sinT", [P, NH2, MLA_ROPE // 2], F32, tabs)
        posq = sb("posq", [P, NH2], F32, tabs)
        posk, posi, posqi, dist, ang, angk = scoped([
            ("posk", [P, T], F32), ("posi", [P, T], I32), ("posqi", [P, NH2], I32), ("dist", [P, BLK], F32),
            ("ang", [P, NH2, 16], F32), ("angk", [P, NH2, 16], F32)])
        (cq, dqT, dkT, mqT, mkT, dv, mv, qrow, krow, v2, qa, ka, sc, o2) = scoped([
            ("cq", [P, NH2, 416], F32), ("dqT", [P, 3, T], F32), ("dkT", [P, 3, T], F32), ("mqT", [P, 2, T], F32),
            ("mkT", [P, 2, T], F32), ("dv", [P, NH2, 384], F32), ("mv", [P, NH2, 256], F32),
            ("qrow", [P, NH2, 576], F32), ("krow", [P, NH2, 576], F32), ("v2", [P, NH2, 384], F32),
            ("qa", [P, MLA_H, T], F32), ("ka", [P, MLA_H, T], F32), ("sc", [P, 2, BLK], F32), 
            ("o2", [P, NH2, D], F32)])
        pT = cq[:, :, :].rearrange("p h c -> p (h c)")[:, 0:2 * BLK].rearrange("p (i c) -> p i c", i=2)
        o3 = qrow[:, :, 0:384]
        cqT, ckT, cv, csc, cpT, co, memx = scoped([
            ("cqT", [P, KT, T], F32), ("ckT", [P, KT, T], F32), ("cv", [P, NH2, D], F32), ("csc", [P, 2, 512], F32),
            ("cpT", [P, 2, 512], F32), ("co", [P, NH2, D], F32), ("memx", [P, NH2, D], F32)])
        rT, fh, fl = scoped([("rT", [P, 2, 1024], F32), ("fh", [P, FF // P // 2, T], F32R), ("fl", [P, FF // P // 2, T], F32R)])
        tabs.close()

        raw_loaded = [sem(f"raw_loaded{s}") for s in range(RAW)]
        hi_ready = sem("hi_ready")
        lo_ready = sem("lo_ready")
        w_used = sem("w_used")
        params = sem("params")
        consts = sem("consts")
        ln_loaded = sem("ln_loaded")
        ln_used = sem("ln_used")
        mem_loaded = sem("mem_loaded")
        pos_loaded = sem("pos_loaded")
        part_done = sem("part_done")
        gemm_free = [sem("gemm_free0"), sem("gemm_free1")]
        moe_done = sem("moe_done")
        router_loaded = sem("router_loaded")
        turned = sem("turned")
        turn_hi = sem("turn_hi")
        turn_ready = sem("turn_ready")
        rows_ready = sem("rows_ready")
        root_in, root_out = sem("root_in"), sem("root_out")
        ssq_done = sem("ssq_done")
        pe_stage, act_stage, dve_stage = sem("pe_stage"), sem("act_stage"), sem("dve_stage")
        pe_link, act_link, dve_link = sem("pe_link"), sem("act_link"), sem("dve_link")
        gate_sig = sem("gate_sig")
        conv_b_done = sem("conv_b_done")
        chan_mean = sem("chan_mean")
        sq_ready = sem("sq_ready")
        normed = sem("normed")
        yb_ready = sem("yb_ready")
        mix_hi = sem("mix_hi")
        logits_done = sem("logits_done")
        rexp_in, rexp_out = sem("rexp_in"), sem("rexp_out")
        member_ready = sem("member_ready")
        rank_done = sem("rank_done")
        xh_ready, xl_ready = sem("xh_ready"), sem("xl_ready")
        ss_ready = sem("ss_ready")
        t_done = sem("t_done")
        p_copied = sem("p_copied")
        g0_done, g1_done = sem("g0_done"), sem("g1_done")
        xe0, xe1 = sem("xe0"), sem("xe1")
        hs_gate, hs_up = sem("hs_gate"), sem("hs_up")
        f_done = sem("f_done")
        silu_done, act_ready = sem("silu_done"), sem("act_ready")
        yh0, yh1, yl0, yl1 = sem("yh0"), sem("yh1"), sem("yl0"), sem("yl1")
        score_done = sem("score_done")
        score_read = sem("score_read")
        shifted = sem("shifted")
        exp_done = sem("exp_done")
        prob_ready = sem("prob_ready")
        prob_turned = sem("prob_turned")
        prob_copied = sem("prob_copied")
        pv_done = sem("pv_done")
        pv_read = sem("pv_read")
        soft_abs = sem("soft_abs")
        soft_ready = sem("soft_ready")
        later_done = sem("later_done")
        logit_ready = sem("logit_ready")
        share_ready = sem("share_ready")
        sb_scored, sb_read, sb_pv = sem("sb_scored"), sem("sb_read"), sem("sb_pv")
        heads_copied = sem("heads_copied")
        x_scored, x_max, x_exp, x_prob = sem("x_scored"), sem("x_max"), sem("x_exp"), sem("x_prob")
        x_turned, x_copied, x_pv = sem("x_turned"), sem("x_copied"), sem("x_pv")
        sin_in, sin_out = sem("sin_in"), sem("sin_out")
        sq_in, fh_done = sem("sq_in"), sem("fh_done")
        qk_rows, dve_half = sem("qk_rows"), sem("dve_half")
        h_ready = sem("h_ready")
        lam_in, lam_out = sem("lam_in"), sem("lam_out")
        stored = sem("stored")
        ov = [{k: sem(f"ov{l}_{k}") for k in ("w", "mm", "copied", "act", "turn", "tcopy", "down", "add", "link", "alink", "wt", "silu")}
              for l in range(DEPTH)]

        xn = lnp

        items = []
        for h in range(MLA_H):
            items.append((qa[0:MLA_QK, h, :], ka[0:MLA_QK, h, :], causal, MLA_QK ** -0.5, v2[:, :, h * HD:(h + 1) * HD], 4, h * HD))
        for j in range(2):
            for h in range(DIFF_H):
                r = slice(64 * (h % 2) + DIFF_HD * j, 64 * (h % 2) + DIFF_HD * (j + 1))
                items.append((dqT[r, h // 2, :], dkT[r, h // 2, :], alibi[:, h, :], DIFF_HD ** -0.5, dv[:, :, h * HD:(h + 1) * HD], 6 - 2 * j, h * HD))
        for h in range(MOBA_H):
            r = slice(HD * (h % 2), HD * (h % 2) + HD)
            items.append((mqT[r, h // 2, :], mkT[r, h // 2, :], alibi[:, DIFF_H + h, :], HD ** -0.5, mv[:, :, h * HD:(h + 1) * HD], 6, h * HD))
        N_MAPS = len(items)
        GROUP_ENDS = (MLA_H, MLA_H + DIFF_H, MLA_H + 2 * DIFF_H, N_MAPS)
        GROUP_REUSES = (MLA_H + DIFF_H, MLA_H + 2 * DIFF_H)
        LAM_INIT = [0.8 - 0.6 * math.exp(-0.3 * l) for l in range(DEPTH)]
        TWO_PI_PARTS = (6.28125, 0.0019350051879882812, 3.019915981956753e-07)

        def tile_view(buf, slot, n):
            kts, width = shape_of(n)
            return buf[:, slot, 0:kts * width].rearrange("p (k c) -> p k c", k=kts)

        class Engine(Lane):

            def __init__(self, eng, link_sem, own_stage, stages, convert=None):
                super().__init__(eng, link_sem)
                self.n = self.g = self.converted = 0
                self.own_stage, self.stages, self.convert = own_stage, stages, convert
                self.k = 0

            def pump(self, upto):
                while self.converted <= min(upto, n_total - 1):
                    self.convert(self.converted)
                    self.converted += 1

            def barrier(self):
                self.e.drain().then_inc(self.own_stage, 1)
                self.k += 1
                for s in self.stages:
                    if s is not self.own_stage:
                        self.e.wait_ge(s, self.k)

            def gemm_pair(self, tiles, mine, part=False):
                self.n += tiles
                self.pump(self.n - 1 + CNV - 1)
                g = self.g
                self.g += 1
                if mine:
                    self.e.wait_ge(w_used, self.n)
                return g

            def wide_half(self, tiles, mine):
                self.n += tiles
                self.pump(self.n - 1 + CNV - 1)
                if mine:
                    self.e.wait_ge(w_used, self.n)

        STAGES = (pe_stage, act_stage, dve_stage)
        PARAM_LOADS = 6 * DEPTH + 5 + 1 + 4 + 1
        OVF_HALF, OVF_LOADS = 2 * KT + 8, 2 * (2 * KT + 8)
        ROUTER_FROM, POS_FROM, MEM_FROM, FINAL_FROM = (2, 8), 12, (18, 28), 33

        block = ctx.enter_context(nc.Block())

        @block.sync
        def _(sp):
            count = [0]

            def param(dst, src):
                sp.dma_start(dst, src).then_inc(params, 16)
                count[0] += 16

            sp.dma_start(x[:, :, :], a["x"][0].rearrange("(h p) d -> p h d", p=P)).then_inc(h_ready, 16)

            def load(n, src):
                slot = n % RAW
                if n >= RAW:
                    sp.wait_ge(lo_ready, n - RAW + 1)
                sp.dma_start(tile_view(raw, slot, n), src).then_inc(raw_loaded[slot], 16)

            for n in range(2):
                load(n, before[n])
            sp.wait_ge(consts, 1)
            for l in range(DEPTH):
                for row, name, k in ((ROW_ATTN, "attn_norm_2", 8), (ROW_CROSS, "cross_norm_2", 8), (ROW_MEM, "mem_norm_2", 8),
                                     (ROW_MLP, "mlp_norm_2", 8), (ROW_Q, "mla_q_norm_2", 2), (ROW_KV, "mla_kv_norm_2", 1)):
                    r = l * ROWS_LAYER + row
                    param(prmA[r:r + k, :], a[name][l].rearrange("(k p) -> k p", p=P))
            param(prmA[ROW_CONVA:ROW_CONVA + 4 * CONV_A, :], a["even_conv_a"][0].rearrange("j (k p) -> (j k) p", p=P))
            param(prmA[ROW_BIAS:ROW_BIAS + 4, :], a["even_conv_b_bias"][0].rearrange("(k p) -> k p", p=P))
            param(prmA[ROW_NBG:ROW_NBG + 4, :], a["even_norm_b_g"][0].rearrange("(k p) -> k p", p=P))
            param(prmA[ROW_NBB:ROW_NBB + 4, :], a["even_norm_b_b"][0].rearrange("(k p) -> k p", p=P))
            param(prmB[0:4 * CONV_B, :], a["even_conv_b_w"][0].rearrange("j (k p) -> (j k) p", p=P))
            param(inv_freq[:, :], a["inv_freq"].partition_broadcast(P))
            for j, name in enumerate(("q1", "k1", "q2", "k2")):
                param(lam_rows[:, j * DEPTH:(j + 1) * DEPTH, :], a[f"diff_lambda_{name}_2"].partition_broadcast(P))
            param(subn[:, :, :], a["diff_sub_norm_2"].partition_broadcast(P))
            assert count[0] == 16 * PARAM_LOADS

            for n in range(2, len(before)):
                load(n, before[n])
            for layer, rest in ((0, middle), (1, after)):
                n0 = moe_start[layer]
                w_up, w_down = a["expert_w_up"][layer], a["expert_w_down"][layer]
                with sp.Fori(0, NE) as e:
                    ups = w_up[bass.ds(e, 1)].rearrange("a (k p) c -> p (a k) c", p=P)
                    downs = w_down[bass.ds(e, 1)].rearrange("a (k p) c -> p (a k) c", p=P)
                    for k in range(EXPERT_TILES):
                        if k < 4:
                            src = ups[:, (k % 2) * TK:(k % 2 + 1) * TK, (k // 2) * DE:(k // 2 + 1) * DE]
                        else:
                            src = downs[:, :, (k - 4) * TW:(k - 3) * TW]
                        slot = (n0 + k) % RAW
                        sp.wait_ge(lo_ready, e * EXPERT_TILES + (n0 + k - RAW + 1))
                        sp.dma_start(tile_view(raw, slot, n0), src).then_inc(raw_loaded[slot], 16)
                for j in range(CNV):
                    load(n0 + n_moe + j, rest[j])
                o = ov[layer]
                more = sp.value_load(flag[0:1, layer:layer + 1], min_val=0, max_val=1)
                with sp.If(more > 0):
                    with sp.Fori(0, NE) as e:
                        ups = w_up[bass.ds(e, 1)].rearrange("a (k p) c -> p (a k) c", p=P)
                        downs = w_down[bass.ds(e, 1)].rearrange("a (k p) c -> p (a k) c", p=P)
                        for half in range(NH2):
                            for j in range(OVF_HALF):
                                src = ups[:, j // 2, (j % 2) * DE:(j % 2 + 1) * DE] if j < 2 * KT else \
                                    downs[:, (j - 2 * KT) // 2, (j % 2) * TW:(j % 2 + 1) * TW]
                                sp.wait_ge(o["mm"], e * OVF_LOADS + (half * OVF_HALF + j + 1))
                                sp.dma_start(ovf_w[:, :], src).then_inc(o["w"], 16)
                for j in range(CNV, len(rest)):
                    load(n0 + n_moe + j, rest[j])
            sp.wait_ge(h_ready, 16 + 1)
            sp.dma_start(out[0].rearrange("(h p) d -> p h d", p=P), x[:, :, :]).then_inc(stored, 16)
            sp.wait_ge(stored, 16)

        @block.gpsimd
        def _(pool):
            pool.memset(prmA[:, :], 0.0)
            pool.memset(prmB[:, :], 0.0).then_inc(consts, 1)
            pool.memset(ident[:, :], 0.0)
            pool.memset(ones[:, :], 1.0)
            pool.memset(tri_after[:, :], 1.0)
            pool.memset(tri_before[:, :], 1.0)
            pool.memset(keep_t[:, :], 1.0)
            pool.memset(drop_t[:, :], 0.0)
            pool.memset(causal[:, :], 0.0)
            pool.memset(fold[:, :], 0.0).then_inc(consts, 1)
            pool.wait_ge(consts, 2)
            sel = pool.affine_select
            sel(out=ident[:, :], in_=ident[:, :], pattern=[[-1, P]], compare_op=ALU.not_equal, fill=1.0, base=0, channel_multiplier=1)
            sel(out=tri_after[:, :], in_=tri_after[:, :], pattern=[[-1, P]], compare_op=ALU.is_ge, fill=0.0, base=0, channel_multiplier=1)
            sel(out=tri_before[:, :], in_=tri_before[:, :], pattern=[[1, P]], compare_op=ALU.is_gt, fill=0.0, base=0, channel_multiplier=-1)
            sel(out=keep_t[:, :], in_=keep_t[:, :], pattern=[[1, P]], compare_op=ALU.is_gt, fill=0.0, base=0, channel_multiplier=-1)
            sel(out=drop_t[:, :], in_=drop_t[:, :], pattern=[[1, P]], compare_op=ALU.is_gt, fill=NEG, base=0, channel_multiplier=-1)
            sel(out=causal[:, 0:P], in_=causal[:, 0:P], pattern=[[-1, P]], compare_op=ALU.is_ge, fill=NEG, base=0, channel_multiplier=1)
            sel(out=causal[:, P:BLK], in_=causal[:, P:BLK], pattern=[[-1, T]], compare_op=ALU.is_ge, fill=NEG, base=P, channel_multiplier=1)
            sel(out=fold[:, :], in_=fold[:, :], pattern=[[-1, CAP]], compare_op=ALU.not_equal, fill=1.0, base=0, channel_multiplier=1).then_inc(consts, 1)
            pool.wait_ge(consts, 3)
            sel(out=fold[:, :], in_=fold[:, :], pattern=[[-1, CAP]], compare_op=ALU.not_equal, fill=1.0, base=-CAP, channel_multiplier=1)
            pool.iota(slot_no[:, :], pattern=[[0, 2], [1, CAP]], base=0, channel_multiplier=0, allow_small_or_imprecise_dtypes=True)
            pool.iota(prio[:, :], pattern=[[-1, EPG]], base=EPG, channel_multiplier=0, allow_small_or_imprecise_dtypes=True).then_inc(consts, 1)

            def norm_params(k, names, layer):
                if k:
                    pool.wait_ge(ln_used, k)
                for j, name in enumerate(names):
                    src = a[name][layer] if layer is not None else a[name]
                    pool.dma_start(lnp[:, j, :], src.partition_broadcast(P)).then_inc(ln_loaded, 16)

            for layer in range(DEPTH):
                norm_params(2 * layer, ("ln_mix_g", "ln_mix_b"), layer)
                if layer == 0:
                    pass
                pool.wait_ge(dve_stage, ROUTER_FROM[layer])
                pool.wait_ge(act_stage, ROUTER_FROM[layer])
                pool.wait_ge(pe_stage, ROUTER_FROM[layer])
                pool.dma_start(rw[:, :, 0:NG], a["router_group_w"][layer].rearrange("(k p) n -> p k n", p=P)).then_inc(router_loaded, 16)
                pool.dma_start(rw[:, :, NG:NR], a["router_expert_w"][layer].rearrange("(k p) n -> p k n", p=P)).then_inc(router_loaded, 16)
                pool.dma_start(rbias[:, 0:NG], a["router_group_b"][layer].partition_broadcast(P)).then_inc(router_loaded, 16)
                pool.dma_start(rbias[:, NG:NR], a["router_expert_b"][layer].partition_broadcast(P)).then_inc(router_loaded, 16)
                norm_params(2 * layer + 1, ("ln_ffn_g", "ln_ffn_b"), layer)
            pool.wait_ge(ln_used, 4)
            pool.wait_ge(dve_stage, POS_FROM)
            pool.wait_ge(act_stage, POS_FROM)
            pool.wait_ge(pe_stage, POS_FROM)
            pool.dma_start(posi[:, :], a["positions_2"][0].partition_broadcast(P)).then_inc(pos_loaded, 16)
            pool.dma_start(posqi[:, :], a["positions_2"][0].rearrange("(h p) -> p h", p=P), allow_slow_non_contiguous=True).then_inc(pos_loaded, 16)
            for layer in range(DEPTH):
                for s in STAGES:
                    pool.wait_ge(s, MEM_FROM[layer])
                pool.dma_start(memx[:, :, :], a["mem_2"][0].rearrange("(h p) d -> p h d", p=P)).then_inc(mem_loaded, 16)
            for s in STAGES:
                pool.wait_ge(s, FINAL_FROM)
            pool.dma_start(lnp[:, 0, :], a["final_norm_2"].partition_broadcast(P)).then_inc(ln_loaded, 16)

        @block.tensor
        def _(pe):
            me = Engine(pe, pe_link, pe_stage, STAGES)
            me.pump = lambda upto: None

            def mm(outp, lhsT, rhs, start, stop):
                return pe.matmul(outp, lhsT, rhs, start=start, stop=stop, skip_group_check=True)

            def tile(width_only=None):
                n = me.n
                pe.wait_ge(lo_ready, n + 1)
                me.n += 1
                return tile_view(w_hi, n % CNV, n), tile_view(w_lo, n % CNV, n)

            def three(outp, lh, ll, rh, rl, start, stop):
                mm(outp, lh, rh, start, False)
                mm(outp, ll, rh, False, False)
                return mm(outp, lh, rl, False, stop)

            def open_pair():
                g = me.g
                if g >= 2:
                    pe.wait_ge(gemm_free[g % 2], g // 2)
                me.g += 1
                return 2 * (g % 2)

            def rows_pair(kts, width, halves_cols=None, k0=0):
                b = open_pair()
                for kg in range(0, kts, TK):
                    wh, wl = tile()
                    for half in range(NH2):
                        tok = slice(half * P, half * P + P)
                        for k in range(min(TK, kts - kg)):
                            kt = kg + k
                            last = three(PS[:, b + half, 0:width], ah[:, k0 + kt, tok], al[:, k0 + kt, tok], wh[:, k, :], wl[:, k, :],
                                         kt == 0, kt == kts - 1)
                    last.then_inc(w_used, 1)

            def split_pair(kts, k0, widths):
                wh, wl = tile()
                c0 = 0
                for j, width in enumerate(widths):
                    b = open_pair()
                    for half in range(NH2):
                        tok = slice(half * P, half * P + P)
                        for k in range(kts):
                            last = three(PS[:, b + half, 0:width], ah[:, k0 + k, tok], al[:, k0 + k, tok],
                                         wh[:, k, c0:c0 + width], wl[:, k, c0:c0 + width], k == 0, k == kts - 1)
                    last.then_inc(w_used if j == len(widths) - 1 else part_done, 1)
                    c0 += width

            def cols_pair(width, kts=KT):
                b = open_pair()
                for kg in range(0, kts, TK):
                    wh, wl = tile()
                    for k in range(TK):
                        kt = kg + k
                        for eb in range(width // P):
                            ch = slice(eb * P, eb * P + P)
                            o = PS[:, b + eb // 2, (eb % 2) * T:(eb % 2 + 1) * T]
                            first, stop = kt == 0 and eb % 2 == 0, kt == kts - 1
                            mm(o, wh[:, k, ch], ah[:, kt, :], first, False)
                            mm(o, wh[:, k, ch], al[:, kt, :], False, False)
                            last = mm(o, wl[:, k, ch], ah[:, kt, :], False, stop)
                    last.then_inc(w_used, 1)

            def wide(actsh, actsl, kts, first=True, final=True):
                for nb in range(2):
                    for kg in range(0, kts, TK):
                        wh, wl = tile()
                        for half in range(NH2):
                            tok = slice(half * P, half * P + P)
                            for k in range(TK):
                                kt = kg + k
                                last = three(PS[:, 4 + 2 * nb + half, :], actsh[:, kt, tok], actsl[:, kt, tok], wh[:, k, :], wl[:, k, :],
                                             first and kt == 0, final and kt == kts - 1)
                        last.then_inc(w_used, 1)

            def turn(src, kts=KT, wait=True, c0=0):
                if wait:
                    me.wait(rows_ready)
                for b in range((kts + 1) // 2):
                    for kt in range(2 * b, min(2 * b + 2, kts)):
                        for half in range(NH2):
                            c = (kt % 2) * T + half * P
                            last = pe.transpose(PS[:, b, c:c + P], src[:, half, c0 + kt * P:c0 + (kt + 1) * P], ident[:, :])
                    last.then_inc(turned, 1)

            pe.wait_ge(consts, 4)
            pe.wait_ge(params, 16 * PARAM_LOADS)
            pe.wait_ge(h_ready, 16)
            pe.transpose(PS[:, 7, 0:P], prmA[:, :], ident[:, :])
            pe.transpose(PS[:, 7, P:2 * P], prmB[:, :], ident[:, :]).then_inc(turned, 1)
            turn(x, wait=False)
            me.barrier()

            for nb in range(E_IN // TW):
                cols_pair(TW)
            me.wait(conv_b_done)
            for blk in range(4):
                last = mm(PS[:, 4, 0:T], ones[:, :], gb[:, blk, :], blk == 0, blk == 3)
            last.then_inc(chan_mean, 1)
            me.wait(sq_ready)
            for blk in range(4):
                last = mm(PS[:, 5, 0:T], ones[:, :], tc[:, blk, :], blk == 0, blk == 3)
            last.then_inc(chan_mean, 1)
            me.barrier()

            def router_and_experts(layer):
                me.wait(router_loaded, 64)
                for half in range(NH2):
                    for kt in range(KT):
                        last = mm(PS[:, 0, half * 64:half * 64 + NR], xT[:, kt, half * P:half * P + P], rw[:, kt, :], kt == 0, kt == KT - 1)
                last.then_inc(logits_done, 1)
                me.wait(member_ready)
                mm(PS[:, 1, 0:NE], tri_before[:, :], Mt[:, 0, :], True, True)
                mm(PS[:, 1, NE:2 * NE], tri_before[:, :], Mt[:, 1, :], True, False)
                mm(PS[:, 1, NE:2 * NE], ones[:, :], Mt[:, 0, :], False, True)
                mm(PS[:, 1, 2 * NE:3 * NE], ones[:, :], Mt[:, 0, :], True, False)
                mm(PS[:, 1, 2 * NE:3 * NE], ones[:, :], Mt[:, 1, :], False, True).then_inc(rank_done, 1)
                me.barrier()

                def gather(kts, bank):
                    for k in kts:
                        for part, c0 in ((xh, 0), (xl, CAP)):
                            for half in range(NH2):
                                last = mm(PS[:, bank, (k % 4) * 2 * CAP + c0:(k % 4) * 2 * CAP + c0 + CAP], part[:, half, k * P:(k + 1) * P],
                                          SS[:, half, 0:CAP], half == 0, half == 1)
                    return last

                def combine():
                    for nb in range(2):
                        for half in range(NH2):
                            for part in (yh, yl):
                                last = mm(PS[:, 4 + 2 * nb + half, :], Pm[:, half * P:half * P + P], part[:, nb * TW:(nb + 1) * TW], False, False)
                    return last

                me.wait(ss_ready)
                for nb in range(2):
                    for half in range(NH2):
                        mm(PS[:, 4 + 2 * nb + half, :], Pm[:, half * P:half * P + P], yh[:, nb * TW:(nb + 1) * TW], True, False)
                gather(range(0, 4), 3).then_inc(g0_done, 1)
                gather(range(4, 8), 2).then_inc(g1_done, 1)
                n0 = me.n
                one = lambda *s: {q.name: 1 for q in s}
                with pe.Fori(0, NE) as e:
                    me.enter(e, one(xe0, xe1, yl0, yl1, p_copied, ss_ready, hs_gate, hs_up, act_ready))

                    def up(bank, k0):
                        for k in range(k0, k0 + 2):
                            slot = (n0 + k) % CNV
                            pe.wait_ge(lo_ready, e * EXPERT_TILES + (n0 + k + 1))
                            for q in range(TK):
                                kt = (k % 2) * TK + q
                                mm(PS[:, bank, :], xe[:, kt, :], w_hi[:, slot, q * TW:(q + 1) * TW], kt == 0, False)
                                last = mm(PS[:, bank, :], xe[:, kt, :], w_lo[:, slot, q * TW:(q + 1) * TW], False, kt == KT - 1)
                            last.then_inc(w_used, 1)

                    me.wait(xe0)
                    me.wait(xe1)
                    me.wait(yl0)
                    up(0, 0)
                    me.wait(yl1)
                    combine()
                    pe.transpose(PS[:, 2, 0:P], SS[:, 0, :].bitcast(F32), ident[:, :])
                    pe.transpose(PS[:, 2, P:2 * P], SS[:, 1, :].bitcast(F32), ident[:, :])
                    for half in range(NH2):
                        last = mm(PS[:, 2, 2 * P:2 * P + NE], SS[:, half, :].bitcast(F32), Wt[:, half, :], half == 0, half == 1)
                    last.then_inc(t_done, 1)
                    up(1, 2)
                    me.wait(ss_ready)
                    gather(range(0, 4), 3).then_inc(g0_done, 1)
                    me.wait(p_copied)
                    gather(range(4, 8), 2).then_inc(g1_done, 1)
                    me.wait(hs_gate)
                    me.wait(hs_up)
                    pe.wait_ge(xe0, e + (layer * (NE + 1) + 2))
                    for c in range(2 * DE // P):
                        last = mm(PS[:, 3, c * CAP:(c + 1) * CAP], hs[:, c * P:(c + 1) * P], fold[:, :], True, True)
                    last.then_inc(f_done, 1)
                    me.wait(act_ready)
                    for nb in range(2):
                        slot = (n0 + 4 + nb) % CNV
                        pe.wait_ge(lo_ready, e * EXPERT_TILES + (n0 + 4 + nb + 1))
                        for q in range(TK):
                            mm(PS[:, nb, :], aT[:, q, :], w_hi[:, slot, q * TW:(q + 1) * TW], q == 0, False)
                            last = mm(PS[:, nb, :], aT[:, q, :], w_lo[:, slot, q * TW:(q + 1) * TW], False, q == TK - 1)
                        last.then_inc(w_used, 1)
                    me.leave(NE)
                me.n = n0 + n_moe
                me.wait(xe0)
                me.wait(xe1)
                me.wait(yl0)
                me.wait(yl1)
                combine().then_inc(moe_done, 1)
                overflow(layer)
                me.barrier()

            def overflow(layer):
                o = ov[layer]
                more = pe.value_load(flag[0:1, layer:layer + 1], min_val=0, max_val=1)
                with pe.If(more > 0):
                    with pe.Fori(0, NE) as e:
                        for half in range(NH2):
                            tok = slice(half * P, half * P + P)
                            if half == 0:
                                pe.wait_ge(o["add"], e * 2 + 1)
                            else:
                                pe.wait_ge(o["add"], e * 2 + 2)
                            for j in range(2 * KT):
                                pe.wait_ge(o["w"], e * (16 * OVF_LOADS) + 16 * (half * OVF_HALF + j + 1))
                                mm(PS[:, j % 2, :], xT[:, j // 2, tok], ovf_w[:, :], j // 2 == 0, j // 2 == KT - 1).then_inc(o["mm"], 1)
                            pe.wait_ge(o["act"], e * 2 + (half + 1))
                            for c in range(4):
                                last = pe.transpose(PS[:, 2, c * P:(c + 1) * P], ovf_h[:, c * P:(c + 1) * P], ident[:, :])
                            last.then_inc(o["turn"], 1)
                            pe.wait_ge(o["tcopy"], e * 2 + (half + 1))
                            for j in range(8):
                                pe.wait_ge(o["w"], e * (16 * OVF_LOADS) + 16 * (half * OVF_HALF + 2 * KT + j + 1))
                                mm(PS[:, j % 2, :], ovf_a[:, j // 2, :], ovf_w[:, :], j // 2 == 0, j // 2 == 3).then_inc(o["mm"], 1)

            wide(ah, al, KT)
            turn(x)
            me.barrier()
            router_and_experts(0)
            turn(x)
            me.barrier()

            for nb in range(4):
                cols_pair(TW)
            for nb in range(2):
                rows_pair(KT, TW)
            me.barrier()

            def rows_of(h):
                return slice(HD * (h % 2), HD * (h % 2) + HD)

            def sb_scores(h):
                if h >= 2:
                    pe.wait_ge(sb_read, h - 1)
                r, kt = rows_of(h), h // 2
                mm(PS[:, h % 2, 0:T], kT1[r, kt, 0:P], qT1[r, kt, :], True, True)
                mm(PS[:, h % 2, T:BLK], kT1[r, kt, P:T], qT1[r, kt, P:T], True, True).then_inc(sb_scored, 1)

            def sb_later(h):
                pe.wait_ge(soft_ready, h + 1)
                if h >= 2:
                    pe.wait_ge(logit_ready, h - 1)
                b = 2 + h % 2
                mm(PS[:, b, 0:T], tri_after[:, :], sp_l[:, h % 2, 0:T], True, False)
                mm(PS[:, b, P:T], ones[:, :], sp_l[:, h % 2, T:BLK], False, True)
                mm(PS[:, b, T:BLK], tri_after[:, :], sp_l[:, h % 2, T:BLK], True, True).then_inc(later_done, 1)

            def sb_values(h):
                pe.wait_ge(share_ready, h + 1)
                r, kt = rows_of(h), h // 2
                b, c0 = 4 + kt // 2, (kt % 2) * T
                v = v1[:, :, h * HD:(h + 1) * HD]
                mm(PS[r, b, c0:c0 + T], v[:, 0, :], aa[:, h % 2, 0:T], True, False)
                mm(PS[r, b, c0 + P:c0 + T], v[:, 1, :], aa[:, h % 2, T:BLK], False, True).then_inc(sb_pv, 1)

            for step in range(SB_HEADS + 2):
                if step < SB_HEADS:
                    sb_scores(step)
                if 1 <= step <= SB_HEADS:
                    sb_later(step - 1)
                if step >= 2:
                    sb_values(step - 2)
            me.barrier()

            wide(ah, al, KT)
            turn(x)
            me.barrier()
            router_and_experts(1)
            me.barrier()
            me.barrier()

            for layer in range(DEPTH):
                turn(xn)
                me.barrier()
                for c0, width, channel_major in PROJ:
                    cols_pair(width) if channel_major else rows_pair(KT, width)
                me.barrier()
                turn(cq, 3)
                me.wait(turn_ready)
                split_pair(2, 0, (288, 288))
                split_pair(1, 2, (384, 384))
                for rows in (qrow, krow):
                    me.wait(rows_ready)
                    for b in range(3):
                        for h in (2 * b, 2 * b + 1):
                            for half in range(NH2):
                                last = pe.transpose(PS[0:MLA_QK, 4 + b, (h % 2) * T + half * P:(h % 2) * T + half * P + P],
                                                    rows[:, half, h * MLA_QK:(h + 1) * MLA_QK], ident[:, :])
                    last.then_inc(turned, 1)
                    me.wait(heads_copied)
                me.barrier()

                def scores(i):
                    if i >= 2:
                        me.wait(score_read)
                    q, k = items[i][0], items[i][1]
                    mm(PS[:, i % 2, 0:P], q[:, 0:P], k[:, 0:P], True, True)
                    mm(PS[:, i % 2, P:BLK], q[:, P:T], k[:, :], True, True).then_inc(score_done, 1)

                def values(i):
                    v, b, c0 = items[i][4], items[i][5], items[i][6]
                    mm(PS[:, b, c0:c0 + HD], pT[:, i % 2, 0:P], v[:, 0, :], True, True)
                    mm(PS[:, b + 1, c0:c0 + HD], pT[:, i % 2, P:2 * P], v[:, 0, :], True, False)
                    mm(PS[:, b + 1, c0:c0 + HD], pT[:, i % 2, 2 * P:BLK], v[:, 1, :], False, True).then_inc(pv_done, 1)

                for step in range(N_MAPS + 2):
                    if step < N_MAPS:
                        scores(step)
                    if step >= 2:
                        if step - 2 in GROUP_REUSES:
                            me.wait(pv_read)
                        me.wait(prob_copied)
                        values(step - 2)
                    if 1 <= step <= N_MAPS:
                        me.wait(prob_ready)
                        i = step - 1
                        for c in range(3):
                            last = pe.transpose(PS[:, 2 + i % 2, c * P:(c + 1) * P], sc[:, i % 2, c * P:(c + 1) * P], ident[:, :])
                        last.then_inc(prob_turned, 1)
                me.wait(score_read, 2)
                me.wait(pv_read, 4 - len(GROUP_REUSES))
                me.barrier()

                turn(o2)
                me.wait(turn_ready)
                wide(ah, al, KT)
                me.barrier()
                turn(memx)
                me.wait(turn_ready)
                for nb in range(2):
                    cols_pair(TW)
                for nb in range(2):
                    rows_pair(KT, TW)
                me.barrier()
                turn(xn)
                me.wait(turn_ready)
                for nb in range(2):
                    cols_pair(TW)
                me.barrier()
                for step in range(CROSS_H + 1):
                    if step < CROSS_H:
                        h = step
                        if h >= 2:
                            me.wait(x_exp)
                        for half in range(NH2):
                            for q in range(2):
                                last = mm(PS[:, h % 2, half * T:(half + 1) * T], cqT[:, 2 * h + q, half * P:half * P + P], ckT[:, 2 * h + q, :], q == 0, q == 1)
                        last.then_inc(x_scored, 1)
                    if step >= 1:
                        h = step - 1
                        me.wait(x_prob)
                        for m in range(2):
                            for half in range(NH2):
                                last = pe.transpose(PS[:, 2 + h % 2, m * T + half * P:m * T + half * P + P],
                                                    csc[:, h % 2, half * T + m * P:half * T + m * P + P], ident[:, :])
                        last.then_inc(x_turned, 1)
                        me.wait(x_copied)
                        for q in range(2):
                            for m in range(2):
                                c = h * CROSS_HD + q * P
                                last = mm(PS[:, 4 + h, q * T:(q + 1) * T], cv[:, m, c:c + P], cpT[:, h % 2, m * T:(m + 1) * T], m == 0, m == 1)
                        last
                last.then_inc(x_pv, 1)
                me.wait(x_exp, 2)
                me.barrier()
                wide(ah, al, KT)
                me.barrier()
                turn(xn)
                me.wait(turn_ready)
                for f in range(2):
                    for nb in range(FF // 2 // TW):
                        cols_pair(TW)
                    me.wait(fh_done, FF // 2 // TW)
                    wide(fh, fl, FF // 2 // P, first=f == 0, final=f == 1)
                me.barrier()


        @block.scalar
        def _(act):
            def round_tile(n):
                act.wait_ge(raw_loaded[n % RAW], 16 * (n // RAW + 1))
                if n >= CNV:
                    act.wait_ge(w_used, n - CNV + 1)
                act.activation(tile_view(w_hi, n % CNV, n), tile_view(raw, n % RAW, n), ACT.Copy).then_inc(hi_ready, 1)

            me = Engine(act, act_link, act_stage, STAGES, round_tile)

            def f(out_, in_, func, **kw):
                return act.activation(out_, in_, func, **kw)

            def root():
                me.wait(root_in)
                f(stat[:, 16:18], stat[:, 14:16], ACT.Sqrt).then_inc(root_out, 1)

            def split_banks(kts, b0=0, gain=None, wait=True, k0=0):
                for b in range((kts + 1) // 2):
                    if wait:
                        me.wait(turned)
                    for kt in range(2 * b, min(2 * b + 2, kts)) if gain is not None else (2 * b,):
                        if gain is None:
                            m = min(2, kts - kt)
                            last = f(ah[:, k0 + kt:k0 + kt + m, :].rearrange("p k t -> p (k t)"), PS[:, b0 + b, 0:m * T], ACT.Copy)
                        else:
                            last = f(ah[:, k0 + kt, :], PS[:, b0 + b, (kt % 2) * T:(kt % 2 + 1) * T], ACT.Copy, scale=colA[:, gain + kt:gain + kt + 1])
                    last.then_inc(turn_hi, 1)

            def squares(src):
                for half in range(NH2):
                    last = f(PSf[:, half * D:half * D + D], src[:, half, :], ACT.Square, accum_out=stat[:, 12 + half:13 + half])
                last.then_inc(ssq_done, 1)

            me.pump(CNV - 1)
            me.wait(turned)
            split_banks(KT)
            me.barrier()

            for nb in range(E_IN // TW):
                g = me.gemm_pair(2, nb % 2 == 0)
                if nb % 2 == 0:
                    b = 2 * (g % 2)
                    f(uT[:, 4 * nb:4 * nb + 4, :].rearrange("p k t -> p (k t)"), PSf[:, b * 512:b * 512 + 2 * 512], ACT.Copy).then_inc(gemm_free[g % 2], 1)
            me.pump(me.n + CNV - 1)
            act.wait_ge(gemm_free[0], 3)
            me.link(f(gb[:, :, :], uT[:, 16:20, :], ACT.Sigmoid))
            act.drain().then_inc(gate_sig, 1)
            me.wait(root_in)
            f(tc[:, 0, :], tc[:, 1, :], ACT.Sqrt).then_inc(root_out, 1)
            me.wait(normed)
            for blk in range(4):
                last = f(gb[:, blk, :], gb[:, blk, :], ACT.Silu, scale=colA[:, ROW_NBG + blk:ROW_NBG + blk + 1],
                         bias=colA[:, ROW_NBB + blk:ROW_NBB + blk + 1])
            me.link(last)
            f(ah[:, 0:4, :], ya[:, :, :], ACT.Copy)
            f(ah[:, 4:8, :], gb[:, :, :], ACT.Copy).then_inc(mix_hi, 1)
            me.barrier()

            def rows_split():
                me.wait(rows_ready)
                f(xh[:, :, :], x[:, :, :], ACT.Copy).then_inc(xh_ready, 1)
                for b in range(4):
                    me.wait(turned)
                    last = f(xT[:, 2 * b:2 * b + 2, :].rearrange("p k t -> p (k t)"), PS[:, b, :], ACT.Copy)

            def router_and_experts(layer):
                for _ in range(NH2):
                    me.wait(rexp_in)
                    half = _
                    f(rs[:, half, 4:8], rs[:, half, 0:4], ACT.Exp, accum_out=rs[:, half, 8:9]).then_inc(rexp_out, 1)
                me.wait(rexp_in)
                f(rs[:, :, 51:52], rs[:, :, 50:51], ACT.Exp).then_inc(rexp_out, 1)
                me.barrier()

                def xe_copy():
                    me.wait(g0_done)
                    f(xe[:, 0:4, :].rearrange("p k c -> p (k c)"), PS[:, 3, :], ACT.Copy).then_inc(xe0, 1)

                xe_copy()
                n0 = me.n
                me.pump(n0 + CNV - 1)
                one = lambda *s: {q.name: 1 for q in s}
                with act.Fori(0, NE) as e:
                    me.enter(e, one(t_done, g0_done, f_done, p_copied))

                    def convert(k):
                        n = n0 + k
                        act.wait_ge(raw_loaded[n % RAW], e * 16 + 16 * (n // RAW + 1))
                        act.wait_ge(w_used, e * EXPERT_TILES + (n - CNV + 1))
                        act.activation(tile_view(w_hi, n % CNV, n0), tile_view(raw, n % RAW, n0), ACT.Copy).then_inc(hi_ready, 1)

                    def used(k):
                        act.wait_ge(w_used, e * EXPERT_TILES + (n0 + k + 1))

                    convert(3)
                    used(1)
                    f(hs[:, 0:DE], PS[:, 0, :], ACT.Copy).then_inc(hs_gate, 1)
                    convert(4)
                    me.wait(t_done)
                    f(Pm[:, :], PS[:, 2, 0:T], ACT.Copy)
                    f(wc[:, :], PS[:, 2, bass.ds(e + T, 1)], ACT.Copy).then_inc(p_copied, 1)
                    convert(5)
                    convert(6)
                    xe_copy()
                    me.wait(f_done)
                    f(sil[:, :, :].rearrange("p k c -> p (k c)"), PS[:, 3, 0:4 * CAP], ACT.Silu).then_inc(silu_done, 1)
                    me.wait(p_copied)
                    used(4)
                    f(yh[:, 0:TW], PS[:, 0, :], ACT.Copy, scale=wc[:, 0:1]).then_inc(yh0, 1)
                    convert(7)
                    used(5)
                    f(yh[:, TW:D], PS[:, 1, :], ACT.Copy, scale=wc[:, 0:1]).then_inc(yh1, 1)
                    convert(8)
                    me.leave(NE)
                me.n = n0 + n_moe
                me.converted = me.n + CNV
                o = ov[layer]
                more = act.value_load(flag[0:1, layer:layer + 1], min_val=0, max_val=1)
                with act.If(more > 0):
                    with act.Fori(0, NE) as e:
                        for half in range(NH2):
                            act.wait_ge(o["mm"], e * OVF_LOADS + (half * OVF_HALF + 2 * KT + 1))
                            f(ovf_h[:, 0:DE], PS[:, 0, :], ACT.Silu).then_inc(o["silu"], 1)
                            act.wait_ge(o["turn"], e * 2 + (half + 1))
                            f(ovf_a[:, :, :].rearrange("p k t -> p (k t)"), PS[:, 2, :], ACT.Copy).then_inc(o["tcopy"], 1)
                me.barrier()

            for nb in range(2):
                me.wide_half(2, False)
            root()
            rows_split()
            me.barrier()
            router_and_experts(0)
            root()
            me.wait(rows_ready)
            split_banks(KT)
            me.barrier()

            for nb in range(6):
                g = me.gemm_pair(2, nb % 2 == 0)
                b = 2 * (g % 2)
                if nb == 0 or nb == 2:
                    dst = (qT1, kT1)[nb // 2][:, 0:4, :].rearrange("p k t -> p (k t)")
                    f(dst, PSf[:, b * 512:b * 512 + 1024], ACT.Copy).then_inc(gemm_free[g % 2], 1)
                elif nb == 4:
                    f(v1[:, :, 0:TW], PS[:, b:b + 2, :], ACT.Copy).then_inc(gemm_free[g % 2], 1)
            me.barrier()

            for step in range(SB_HEADS + 1):
                if step < SB_HEADS:
                    h, i = step, step % 2
                    act.wait_ge(sb_scored, h + 1)
                    if h >= 2:
                        act.wait_ge(logit_ready, h - 1)
                    if h >= 2:
                        act.wait_ge(soft_ready, h - 1)
                    me.link(f(zs[:, i, :], PS[:, i, 0:BLK], ACT.Copy, scale=HD ** -0.5))
                    act.drain().then_inc(sb_read, 1)
                    me.link(f(sp_a[:, i, :], zs[:, i, :], ACT.Abs))
                    me.link(f(sp_a[:, i, :], sp_a[:, i, :], ACT.Exp, scale=-1.0))
                    f(sp_a[:, i, :], sp_a[:, i, :], ACT.Ln, bias=1.0).then_inc(soft_abs, 1)
                if step >= 1:
                    h, i = step - 1, (step - 1) % 2
                    act.wait_ge(logit_ready, h + 1)
                    f(aa[:, i, :], aa[:, i, :], ACT.Exp).then_inc(share_ready, 1)
            act.wait_ge(sb_pv, SB_HEADS)
            split_banks(KT, 4, wait=False)
            me.barrier()

            for nb in range(2):
                me.wide_half(2, False)
            root()
            rows_split()
            me.barrier()
            router_and_experts(1)
            root()
            me.barrier()
            me.wait(sin_in)
            f(sinT[:, :, :], ang[:, :, :], ACT.Sin)
            f(cosT[:, :, :], ang[:, :, :], ACT.Sin, scale=0.5).then_inc(sin_out, 1)
            me.wait(lam_in)
            f(stat[:, 40:40 + 2 * DEPTH], stat[:, 32:32 + 2 * DEPTH], ACT.Exp).then_inc(lam_out, 1)
            me.barrier()

            for layer in range(DEPTH):
                row = layer * ROWS_LAYER
                squares(x)
                root()
                split_banks(KT, gain=row + ROW_ATTN)
                me.barrier()
                for j, (c0, width, channel_major) in enumerate(PROJ):
                    g = me.gemm_pair(2, j % 2 == 0)
                    b = 2 * (g % 2)
                    if j == 0:
                        f(cq[:, :, :], PS[:, b:b + 2, 0:416], ACT.Copy).then_inc(gemm_free[g % 2], 1)
                    elif j == 2:
                        f(dkT[:, :, :].rearrange("p k t -> p (k t)"), PSf[:, b * 512:b * 512 + 3 * T], ACT.Copy).then_inc(gemm_free[g % 2], 1)
                    elif j == 4:
                        f(mqT[:, :, :].rearrange("p k t -> p (k t)"), PS[:, b, :], ACT.Copy)
                        f(mkT[:, :, :].rearrange("p k t -> p (k t)"), PS[:, b + 1, :], ACT.Copy).then_inc(gemm_free[g % 2], 1)
                me.barrier()
                for half in range(NH2):
                    f(PSf[:, 6 * 512 + half * 256:6 * 512 + half * 256 + QR], cq[:, half, 0:QR], ACT.Square, accum_out=stat[:, 12 + half:13 + half])
                    last = f(PSf[:, 7 * 512 + half * 256:7 * 512 + half * 256 + KVR], cq[:, half, QR:QR + KVR], ACT.Square,
                             accum_out=stat[:, 20 + half:21 + half])
                last.then_inc(ssq_done, 1)
                me.wait(root_in)
                f(stat[:, 22:26], stat[:, 26:30], ACT.Sqrt).then_inc(root_out, 1)
                split_banks(3, gain=row + ROW_Q)
                for j in range(4):
                    if j % 2 == 0:
                        g = me.gemm_pair(1, False)
                        act.wait_ge(part_done, 2 * layer + j // 2 + 1)
                        b = 2 * (g % 2)
                        if j == 0:
                            f(qrow[:, :, 0:288], PS[:, b:b + 2, 0:288], ACT.Copy).then_inc(gemm_free[g % 2], 1)
                        else:
                            for half in range(NH2):
                                kv = PS[:, b + half, 0:384].rearrange("p (h c) -> p h c", c=P)
                                f(krow[:, half, 0:288].rearrange("p (h c) -> p h c", c=MLA_QK)[:, :, 0:MLA_NOPE], kv[:, :, 0:MLA_NOPE], ACT.Copy)
                                last = f(v2[:, half, 0:192].rearrange("p (h c) -> p h c", c=64), kv[:, :, MLA_NOPE:P], ACT.Copy)
                            last.then_inc(gemm_free[g % 2], 1)
                    else:
                        me.gemm_pair(0, False)
                act.drain().then_inc(qk_rows, 1)
                for dst in (qa, ka):
                    me.wait(turned)
                    for b in range(3):
                        last = f(dst[0:MLA_QK, 2 * b:2 * b + 2, :].rearrange("p h t -> p (h t)"), PS[0:MLA_QK, 4 + b, :], ACT.Copy)
                    last.then_inc(heads_copied, 1)
                me.barrier()
                for step in range(N_MAPS + 1):
                    if step < N_MAPS:
                        i = step % 2
                        me.wait(shifted)
                        f(sc[:, i, 0:P], sc[:, i, 0:P], ACT.Exp, bias=stat[:, 52 + 2 * i:53 + 2 * i], accum_out=stat[:, 56 + 2 * i:57 + 2 * i])
                        f(sc[:, i, P:BLK], sc[:, i, P:BLK], ACT.Exp, bias=stat[:, 53 + 2 * i:54 + 2 * i],
                          accum_out=stat[:, 57 + 2 * i:58 + 2 * i]).then_inc(exp_done, 1)
                    if step >= 1:
                        i = (step - 1) % 2
                        me.wait(prob_turned)
                        if step - 1 >= 2:
                            me.wait(pv_done)
                        f(pT[:, i, :], PS[:, 2 + i, 0:BLK], ACT.Copy).then_inc(prob_copied, 1)
                me.wait(pv_done, 2)
                me.wait(root_in)
                f(stat[:, 124:136], stat[:, 112:124], ACT.Sqrt).then_inc(root_out, 1)
                me.barrier()
                split_banks(KT)
                for nb in range(2):
                    me.wide_half(2, False)
                me.barrier()
                me.wait(mem_loaded, 16)
                squares(memx)
                root()
                split_banks(KT, gain=row + ROW_MEM)
                for nb in range(4):
                    g = me.gemm_pair(2, nb % 2 == 0)
                    b = 2 * (g % 2)
                    if nb == 0:
                        f(ckT[:, 0:4, :].rearrange("p k t -> p (k t)"), PSf[:, b * 512:b * 512 + 1024], ACT.Copy).then_inc(gemm_free[g % 2], 1)
                    elif nb == 2:
                        f(cv[:, :, 0:TW], PS[:, b:b + 2, :], ACT.Copy).then_inc(gemm_free[g % 2], 1)
                me.barrier()
                squares(x)
                root()
                split_banks(KT, gain=row + ROW_CROSS)
                for nb in range(2):
                    g = me.gemm_pair(2, nb == 0)
                    b = 2 * (g % 2)
                    if nb == 0:
                        f(cqT[:, 0:4, :].rearrange("p k t -> p (k t)"), PSf[:, b * 512:b * 512 + 1024], ACT.Copy).then_inc(gemm_free[g % 2], 1)
                me.barrier()
                for step in range(CROSS_H + 1):
                    if step < CROSS_H:
                        i = step % 2
                        me.wait(x_max)
                        for half in range(NH2):
                            last = f(csc[:, i, half * T:(half + 1) * T], PS[:, i, half * T:(half + 1) * T], ACT.Exp, scale=CROSS_HD ** -0.5,
                                     bias=stat[:, 52 + 2 * i + half:53 + 2 * i + half], accum_out=stat[:, 56 + 2 * i + half:57 + 2 * i + half])
                        last.then_inc(x_exp, 1)
                    if step >= 1:
                        i = (step - 1) % 2
                        me.wait(x_turned)
                        f(cpT[:, i, :], PS[:, 2 + i, :], ACT.Copy).then_inc(x_copied, 1)
                me.wait(x_pv)
                split_banks(KT, 4, wait=False)
                me.barrier()
                for nb in range(2):
                    me.wide_half(2, False)
                me.barrier()
                squares(x)
                root()
                split_banks(KT, gain=row + ROW_MLP)
                for part in range(2):
                    for nb in range(FF // 2 // TW):
                        g = me.gemm_pair(2, True)
                        b = 2 * (g % 2)
                        me.link(f(rT[:, 0, :], PSf[:, b * 512:b * 512 + 1024], ACT.Relu))
                        act.drain().then_inc(gemm_free[g % 2], 1)
                        if nb + part >= 1:
                            me.wait(fh_done)
                        me.link(f(rT[:, 1, :], rT[:, 0, :], ACT.Square))
                        f(fh[:, 4 * nb:4 * nb + 4, :].rearrange("p k t -> p (k t)"), rT[:, 1, :], ACT.Copy).then_inc(sq_in, 1)
                    for nb in range(2):
                        me.wide_half(4, False)
                me.wait(fh_done)
                me.barrier()
            squares(x)
            root()

        @block.vector
        def _(dve):
            def split_tile(n):
                dve.wait_ge(hi_ready, n + 1)
                dve.tensor_tensor(tile_view(w_lo, n % CNV, n), tile_view(raw, n % RAW, n), tile_view(w_hi, n % CNV, n),
                                  ALU.subtract).then_inc(lo_ready, 1)

            me = Engine(dve, dve_link, dve_stage, STAGES, split_tile)
            tt, ts, stt = dve.tensor_tensor, dve.tensor_scalar, dve.scalar_tensor_tensor

            def root():
                dve.drain().then_inc(root_in, 1)
                me.wait(root_out)
                me.link(dve.reciprocal(stat[:, 18:20], stat[:, 16:18]))

            def split_banks(kts, b0=0, gain=None, k0=0, signal=False):
                for b in range((kts + 1) // 2):
                    me.wait(turn_hi)
                    for kt in range(2 * b, min(2 * b + 2, kts)) if gain is not None else (2 * b,):
                        if gain is None:
                            m = min(2, kts - kt)
                            last = tt(al[:, k0 + kt:k0 + kt + m, :].rearrange("p k t -> p (k t)"), PS[:, b0 + b, 0:m * T],
                                      ah[:, k0 + kt:k0 + kt + m, :].rearrange("p k t -> p (k t)"), ALU.subtract)
                        else:
                            last = stt(out=al[:, k0 + kt, :], in0=PS[:, b0 + b, (kt % 2) * T:(kt % 2 + 1) * T],
                                       scalar=colA[:, gain + kt:gain + kt + 1], in1=ah[:, k0 + kt, :], op0=ALU.mult, op1=ALU.subtract)
                if signal:
                    last.then_inc(turn_ready, 1)

            def add_wide(factor):
                for nb in range(2):
                    me.wide_half(add_wide.tiles, True)
                    for half in range(NH2):
                        last = stt(out=x[:, half, nb * TW:(nb + 1) * TW], in0=x[:, half, nb * TW:(nb + 1) * TW], scalar=factor,
                                   in1=PS[:, 4 + 2 * nb + half, :], op0=ALU.mult, op1=ALU.add)
                me.link(last)
            add_wide.tiles = 2

            def layer_norm():
                for half in range(NH2):
                    for c in range(2):
                        last = dve.bn_stats(stat[:, 64 + 12 * half + 6 * c:70 + 12 * half + 6 * c], x[:, half, c * TW:(c + 1) * TW])
                me.link(last)
                for half in range(NH2):
                    last = dve.bn_aggr(stat[:, 88 + 2 * half:90 + 2 * half], stat[:, 64 + 12 * half:76 + 12 * half])
                me.link(last)
                for half in range(NH2):
                    last = ts(stat[:, 14 + half:15 + half], stat[:, 89 + 2 * half:90 + 2 * half], LN_EPS, None, ALU.add)
                me.link(last)
                root()
                me.wait(ln_loaded, 32)
                for half in range(NH2):
                    me.link(ts(x[:, half, :], x[:, half, :], stat[:, 88 + 2 * half:89 + 2 * half], stat[:, 18 + half:19 + half], ALU.subtract, ALU.mult))
                    me.link(tt(x[:, half, :], x[:, half, :], lnp[:, 0, :], ALU.mult))
                    me.link(tt(x[:, half, :], x[:, half, :], lnp[:, 1, :], ALU.add))
                dve.drain().then_inc(ln_used, 1)

            def rms_rows(src, dst):
                me.wait(ssq_done)
                me.link(ts(stat[:, 14:16], stat[:, 12:14], 1.0 / D, RMS_EPS, ALU.mult, ALU.add))
                root()
                for half in range(NH2):
                    last = ts(dst[:, half, :], src[:, half, :], stat[:, 18 + half:19 + half], None, ALU.mult)
                return last

            me.pump(CNV - 1)
            me.wait(turned)
            tt_copy = dve.tensor_copy
            tt_copy(colA[:, :], PS[:, 7, 0:P])
            tt_copy(colB[:, :], PS[:, 7, P:P + 4 * CONV_B])
            split_banks(KT)
            me.barrier()

            dve.memset(pa[:, :, 0:CONV_A - 1], 0.0)
            dve.memset(pb[:, :, 0:CONV_B - 1], 0.0)
            for nb in range(E_IN // TW):
                g = me.gemm_pair(2, nb % 2 == 1)
                if nb % 2 == 1:
                    b = 2 * (g % 2)
                    tt_copy(uT[:, 4 * nb:4 * nb + 4, :].rearrange("p k t -> p (k t)"), PSf[:, b * 512:b * 512 + 1024]).then_inc(gemm_free[g % 2], 1)
            me.pump(me.n + CNV - 1)
            dve.wait_ge(gemm_free[1], 2)
            me.wait(gate_sig)
            tt(pb[:, :, CONV_B - 1:], uT[:, 12:16, :], gb[:, :, :], ALU.mult)
            me.link(tt(pa[:, :, CONV_A - 1:], uT[:, 4:8, :], uT[:, 8:12, :], ALU.mult))

            def taps(dst, src, col, width, bias=None):
                for j in range(width):
                    for blk in range(4):
                        w = col[:, 4 * j + blk:4 * j + blk + 1]
                        if j == 0:
                            last = ts(dst[:, blk, :], src[:, blk, 0:T], w, None, ALU.mult) if bias is None else \
                                ts(dst[:, blk, :], src[:, blk, 0:T], w, bias[:, blk:blk + 1], ALU.mult, ALU.add)
                        else:
                            last = stt(out=dst[:, blk, :], in0=src[:, blk, j:j + T], scalar=w, in1=dst[:, blk, :], op0=ALU.mult, op1=ALU.add)
                    me.link(last)

            taps(gb, pb, colB, CONV_B, colA[:, ROW_BIAS:ROW_BIAS + 4])
            dve.drain().then_inc(conv_b_done, 1)
            taps(ya, pa, colA[:, ROW_CONVA:ROW_CONVA + 4 * CONV_A], CONV_A)
            me.link(tt(ya[:, :, :], ya[:, :, :], uT[:, 0:4, :], ALU.mult))
            me.wait(chan_mean)
            for blk in range(4):
                last = stt(out=gb[:, blk, :], in0=PS[:, 4, 0:T], scalar=-1.0 / 512, in1=gb[:, blk, :], op0=ALU.mult, op1=ALU.add)
            me.link(last)
            tt(tc[:, :, :], gb[:, :, :], gb[:, :, :], ALU.mult).then_inc(sq_ready, 1)
            me.wait(chan_mean)
            me.link(ts(tc[:, 1, :], PS[:, 5, 0:T], 1.0 / 512, LN_EPS, ALU.mult, ALU.add))
            dve.drain().then_inc(root_in, 1)
            me.wait(root_out)
            me.link(dve.reciprocal(tc[:, 2, :], tc[:, 0, :]))
            for blk in range(4):
                last = tt(gb[:, blk, :], gb[:, blk, :], tc[:, 2, :], ALU.mult)
            last.then_inc(normed, 1)
            me.wait(mix_hi)
            tt(al[:, 0:4, :], ya[:, :, :], ah[:, 0:4, :], ALU.subtract)
            tt(al[:, 4:8, :], gb[:, :, :], ah[:, 4:8, :], ALU.subtract)
            me.barrier()

            def rows_split():
                dve.drain().then_inc(rows_ready, 1)
                me.wait(xh_ready)
                tt(xl[:, :, :], x[:, :, :], xh[:, :, :], ALU.subtract)

            def router_and_experts(layer):
                dve.memset(Pm[:, :].bitcast(F32), 0.0)
                dve.memset(yh[:, :].bitcast(F32), 0.0)
                dve.memset(yl[:, :].bitcast(F32), 0.0)
                me.wait(logits_done)
                for half in range(NH2):
                    last = tt(lg[:, half, :], PS[:, 0, half * 64:half * 64 + NR], rbias[:, :], ALU.add)
                me.link(last)
                GD, GO, ESEL, KEY, O1, O2 = slice(0, 4), slice(12, 16), slice(16, 24), slice(24, 32), slice(32, 40), slice(40, 48)
                for half in range(NH2):
                    r, g4, e32 = rs[:, half, :], lg[:, half, 0:NG], lg[:, half, NG:NR]

                    def col(c, r=r):
                        return r[:, c:c + 1]

                    def first_max(oh, val, top, n):
                        me.link(stt(out=r[:, KEY][:, 0:n], in0=val, scalar=top, in1=prio[:, EPG - n:EPG], op0=ALU.is_equal, op1=ALU.mult))
                        me.link(dve.tensor_reduce(col(49), r[:, KEY][:, 0:n], AX, ALU.max))
                        me.link(ts(oh, r[:, KEY][:, 0:n], col(49), None, ALU.is_equal))

                    me.link(dve.tensor_reduce(col(9), g4, AX, ALU.max))
                    me.link(ts(r[:, GD], g4, col(9), None, ALU.subtract))
                    dve.drain().then_inc(rexp_in, 1)
                    first_max(r[:, GO], g4, col(9), NG)
                    me.link(ts(r[:, ESEL], e32[:, 0:EPG], r[:, 12:13], None, ALU.mult))
                    for j in range(1, NG):
                        me.link(stt(out=r[:, ESEL], in0=e32[:, j * EPG:(j + 1) * EPG], scalar=r[:, 12 + j:13 + j], in1=r[:, ESEL], op0=ALU.mult, op1=ALU.add))
                    me.link(dve.tensor_reduce(col(10), r[:, ESEL], AX, ALU.max))
                    first_max(r[:, O1], r[:, ESEL], col(10), EPG)
                    me.link(stt(out=r[:, ESEL], in0=r[:, O1], scalar=NEG, in1=r[:, ESEL], op0=ALU.mult, op1=ALU.add))
                    me.link(dve.tensor_reduce(col(11), r[:, ESEL], AX, ALU.max))
                    first_max(r[:, O2], r[:, ESEL], col(11), EPG)
                    me.link(tt(col(50), col(11), col(10), ALU.subtract))
                dve.drain().then_inc(rexp_in, 1)
                me.wait(rexp_out, 3)
                for half in range(NH2):
                    r = rs[:, half, :]
                    ts(r[:, 52:53], r[:, 51:52], 1.0, None, ALU.add)
                    last = dve.reciprocal(r[:, 53:54], r[:, 8:9])
                me.link(last)
                me.link(dve.reciprocal(rs[:, :, 54:55], rs[:, :, 52:53]))
                me.link(tt(rs[:, :, 55:56], rs[:, :, 54:55], rs[:, :, 53:54], ALU.mult))
                me.link(tt(rs[:, :, 56:57], rs[:, :, 55:56], rs[:, :, 51:52], ALU.mult))
                for half in range(NH2):
                    r = rs[:, half, :]
                    me.link(tt(r[:, KEY], r[:, O1], r[:, O2], ALU.add))
                    me.link(ts(r[:, ESEL], r[:, O1], r[:, 55:56], None, ALU.mult))
                    me.link(stt(out=r[:, ESEL], in0=r[:, O2], scalar=r[:, 56:57], in1=r[:, ESEL], op0=ALU.mult, op1=ALU.add))
                    for j in range(NG):
                        ts(Mt[:, half, j * EPG:(j + 1) * EPG], r[:, KEY], r[:, 12 + j:13 + j], None, ALU.mult)
                        last = ts(Wt[:, half, j * EPG:(j + 1) * EPG], r[:, ESEL], r[:, 12 + j:13 + j], None, ALU.mult)
                me.link(last)
                dve.drain().then_inc(member_ready, 1)
                me.wait(rank_done)
                dve.memset(slot[:, :, :], 0.0)
                me.link(dve.tensor_reduce(stat[:, 100:101], PS[:, 1, 2 * NE:3 * NE], AX, ALU.max))
                ts(flag[:, layer:layer + 1], stat[:, 100:101], float(CAP), None, ALU.is_gt)
                me.link(stt(out=slot[:, :, 0:NE], in0=PS[:, 1, 0:2 * NE].rearrange("p (h e) -> p h e", e=NE), scalar=1.0, in1=Mt[:, :, :],
                            op0=ALU.add, op1=ALU.mult))
                me.link(ts(slot[:, :, :], slot[:, :, :], -1.0, None, ALU.add))
                me.link(stt(out=ovf_wt[:, :, :], in0=slot[:, :, 0:NE], scalar=float(CAP), in1=Wt[:, :, :], op0=ALU.is_ge, op1=ALU.mult))
                me.barrier()

                def one_hot(column):
                    for half in range(NH2):
                        last = ts(SS[:, half, :], slot_no[:, :], slot[:, half, column], None, ALU.is_equal)
                    last.then_inc(ss_ready, 1)

                def xe_copy():
                    me.wait(g1_done)
                    tt_copy(xe[:, 4:8, :].rearrange("p k c -> p (k c)"), PS[:, 2, :]).then_inc(xe1, 1)

                one_hot(slice(0, 1))
                dve.drain().then_inc(yl0, 1)
                dve.drain().then_inc(yl1, 1)
                xe_copy()
                n0 = me.n
                me.pump(n0 + CNV - 1)
                one = lambda *s: {q.name: 1 for q in s}
                with dve.Fori(0, NE) as e:
                    me.enter(e, {**one(t_done, g1_done, f_done, silu_done, yh0, yh1), dve_link.name: 1})

                    def convert(k):
                        n = n0 + k
                        dve.wait_ge(hi_ready, e * EXPERT_TILES + (n + 1))
                        tt(tile_view(w_lo, n % CNV, n0), tile_view(raw, n % RAW, n0), tile_view(w_hi, n % CNV, n0), ALU.subtract).then_inc(lo_ready, 1)

                    convert(3)
                    me.wait(t_done)
                    one_hot(bass.ds(e + 1, 1))
                    convert(4)
                    dve.wait_ge(w_used, e * EXPERT_TILES + (n0 + 4))
                    tt_copy(hs[:, DE:2 * DE], PS[:, 1, :]).then_inc(hs_up, 1)
                    convert(5)
                    convert(6)
                    xe_copy()
                    me.wait(f_done)
                    me.wait(silu_done)
                    me.link(tt(af[:, :, :].rearrange("p k c -> p (k c)"), sil[:, :, :].rearrange("p k c -> p (k c)"), PS[:, 3, 4 * CAP:8 * CAP], ALU.mult))
                    ahi = tt_copy(aT[:, :, 0:CAP], af[:, :, :])
                    dve.drain().then_inc(dve_half, 1)
                    dve.wait_ge(dve_half, e + (layer * NE + 1))
                    tt(aT[:, :, CAP:2 * CAP], af[:, :, :], aT[:, :, 0:CAP], ALU.subtract).then_inc(act_ready, 1)
                    me.wait(yh0)
                    stt(out=yl[:, 0:TW], in0=PS[:, 0, :], scalar=wc[:, 0:1], in1=yh[:, 0:TW], op0=ALU.mult, op1=ALU.subtract).then_inc(yl0, 1)
                    convert(7)
                    me.wait(yh1)
                    stt(out=yl[:, TW:D], in0=PS[:, 1, :], scalar=wc[:, 0:1], in1=yh[:, TW:D], op0=ALU.mult, op1=ALU.subtract).then_inc(yl1, 1)
                    convert(8)
                    me.leave(NE)
                me.n = n0 + n_moe
                me.converted = me.n + CNV
                me.wait(moe_done)
                for nb in range(2):
                    for half in range(NH2):
                        last = stt(out=x[:, half, nb * TW:(nb + 1) * TW], in0=x[:, half, nb * TW:(nb + 1) * TW], scalar=ALPHA,
                                   in1=PS[:, 4 + 2 * nb + half, :], op0=ALU.mult, op1=ALU.add)
                me.link(last)
                o = ov[layer]
                more = dve.value_load(flag[0:1, layer:layer + 1], min_val=0, max_val=1)
                with dve.If(more > 0):
                    dve.drain().then_inc(o["mm"], 1)
                    dve.drain().then_inc(o["add"], 1)
                    with dve.Fori(0, NE) as e:
                        for half in range(NH2):
                            dve.wait_ge(o["mm"], e * OVF_LOADS + (half * OVF_HALF + 2 * KT + 1))
                            dve.wait_ge(o["silu"], e * 2 + (half + 1))
                            tt(ovf_h[:, DE:2 * DE], ovf_h[:, 0:DE], PS[:, 1, :], ALU.mult).then_inc(o["link"], 1)
                            dve.wait_ge(o["link"], e * 2 + (half + 1))
                            ts(ovf_h[:, 0:DE], ovf_h[:, DE:2 * DE], ovf_wt[:, half, bass.ds(e, 1)], None, ALU.mult).then_inc(o["act"], 1)
                            dve.wait_ge(o["mm"], e * OVF_LOADS + ((half + 1) * OVF_HALF + 1))
                            for nb in range(2):
                                last = tt(x[:, half, nb * TW:(nb + 1) * TW], x[:, half, nb * TW:(nb + 1) * TW], PS[:, nb, :], ALU.add)
                            last.then_inc(o["add"], 1)
                            dve.wait_ge(o["add"], e * 2 + (half + 2))
                me.barrier()

            add_wide(ALPHA)
            layer_norm()
            rows_split()
            me.barrier()
            router_and_experts(0)
            layer_norm()
            dve.drain().then_inc(rows_ready, 1)
            split_banks(KT)
            me.barrier()

            for nb in range(6):
                g = me.gemm_pair(2, nb % 2 == 1)
                b = 2 * (g % 2)
                if nb == 1 or nb == 3:
                    dst = (qT1, kT1)[nb // 2][:, 4:8, :].rearrange("p k t -> p (k t)")
                    tt_copy(dst, PSf[:, b * 512:b * 512 + 1024]).then_inc(gemm_free[g % 2], 1)
                elif nb == 5:
                    tt_copy(v1[:, :, TW:D], PS[:, b:b + 2, :]).then_inc(gemm_free[g % 2], 1)
            me.barrier()

            for step in range(SB_HEADS + 1):
                if step < SB_HEADS:
                    h, i = step, step % 2
                    dve.wait_ge(soft_abs, h + 1)
                    if h >= 2:
                        dve.wait_ge(later_done, h - 1)
                    me.link(stt(out=sp_l[:, i, :], in0=zs[:, i, :], scalar=0.0, in1=sp_a[:, i, :], op0=ALU.max, op1=ALU.add))
                    tt(sp_l[:, i, 0:P], sp_l[:, i, 0:P], keep_t[:, :], ALU.mult)
                    tt(sp_l[:, i, T:BLK], sp_l[:, i, T:BLK], keep_t[:, :], ALU.mult).then_inc(soft_ready, 1)
                if step >= 1:
                    h, i = step - 1, (step - 1) % 2
                    dve.wait_ge(later_done, h + 1)
                    if h >= 2:
                        dve.wait_ge(sb_pv, h - 1)
                    me.link(tt(aa[:, i, :], zs[:, i, :], PS[:, 2 + i, 0:BLK], ALU.subtract))
                    tt(aa[:, i, 0:P], aa[:, i, 0:P], drop_t[:, :], ALU.add)
                    tt(aa[:, i, T:BLK], aa[:, i, T:BLK], drop_t[:, :], ALU.add).then_inc(logit_ready, 1)
            split_banks(KT, 4)
            me.barrier()

            add_wide(ALPHA)
            layer_norm()
            rows_split()
            me.barrier()
            router_and_experts(1)
            layer_norm()
            me.barrier()

            me.wait(pos_loaded, 32)
            tt_copy(posk[:, :], posi[:, :])
            me.link(tt_copy(posq[:, :], posqi[:, :]))
            for half in range(NH2):
                last = ts(ang[:, half, :], inv_freq[:, :], posq[:, half:half + 1], None, ALU.mult)
            me.link(last)
            MAGIC = 1.5 * 2.0 ** 23
            me.link(ts(angk[:, :, :], ang[:, :, :], 1.0 / (2 * math.pi), None, ALU.mult))
            me.link(ts(angk[:, :, :], angk[:, :, :], MAGIC, None, ALU.add))
            me.link(ts(angk[:, :, :], angk[:, :, :], -MAGIC, None, ALU.add))
            for part in TWO_PI_PARTS:
                me.link(stt(out=ang[:, :, :], in0=angk[:, :, :], scalar=-part, in1=ang[:, :, :], op0=ALU.mult, op1=ALU.add))
            me.link(ts(ang[:, :, :], ang[:, :, :], 3.1415925, -3.1415925, ALU.min, ALU.max))
            dve.drain().then_inc(sin_in, 1)
            for half, c0, w in ((0, 0, P), (1, P, T)):
                me.link(ts(dist[:, c0:c0 + w], posk[:, 0:w], posq[:, half:half + 1], None, ALU.subtract))
            me.link(stt(out=dist[:, :], in0=dist[:, :], scalar=-1.0, in1=dist[:, :], op0=ALU.mult, op1=ALU.max))
            for m in range(N_ALIBI):
                scale = (DIFF_HD if m < DIFF_H else HD) ** -0.5
                stt(out=alibi[:, m, :], in0=dist[:, :], scalar=-SLOPES[m] / scale, in1=causal[:, :], op0=ALU.mult, op1=ALU.add)
            for l in range(DEPTH):
                for j in range(2):
                    c = 32 + 2 * l + j
                    prod = lam_rows[:, 2 * j * DEPTH + l, :]
                    me.link(tt(prod, prod, lam_rows[:, (2 * j + 1) * DEPTH + l, :], ALU.mult))
                    me.link(dve.tensor_reduce(stat[:, c:c + 1], prod, AX, ALU.add))
            dve.drain().then_inc(lam_in, 1)
            me.wait(sin_out)
            me.link(tt(cosT[:, :, :], cosT[:, :, :], cosT[:, :, :], ALU.mult))
            me.link(ts(cosT[:, :, :], cosT[:, :, :], -2.0, 1.0, ALU.mult, ALU.add))
            me.wait(lam_out)
            for l in range(DEPTH):
                me.link(tt(stat[:, 44 + l:45 + l], stat[:, 41 + 2 * l:42 + 2 * l], stat[:, 40 + 2 * l:41 + 2 * l], ALU.subtract))
                me.link(ts(stat[:, 44 + l:45 + l], stat[:, 44 + l:45 + l], -LAM_INIT[l], None, ALU.add))
            me.barrier()

            for layer in range(DEPTH):
                row = layer * ROWS_LAYER
                rms_rows(x, xn).then_inc(rows_ready, 1)
                split_banks(KT, gain=row + ROW_ATTN)
                me.barrier()
                for j, (c0, width, channel_major) in enumerate(PROJ):
                    g = me.gemm_pair(2, j % 2 == 1)
                    b = 2 * (g % 2)
                    if j == 1:
                        tt_copy(dqT[:, :, :].rearrange("p k t -> p (k t)"), PSf[:, b * 512:b * 512 + 3 * T]).then_inc(gemm_free[g % 2], 1)
                    elif j == 3:
                        tt_copy(dv[:, :, :], PS[:, b:b + 2, 0:384]).then_inc(gemm_free[g % 2], 1)
                    elif j == 5:
                        tt_copy(mv[:, :, :], PS[:, b:b + 2, 0:256]).then_inc(gemm_free[g % 2], 1)
                me.barrier()
                me.wait(ssq_done)
                ts(stat[:, 26:28], stat[:, 12:14], 1.0 / QR, RMS_EPS, ALU.mult, ALU.add)
                me.link(ts(stat[:, 28:30], stat[:, 20:22], 1.0 / KVR, RMS_EPS, ALU.mult, ALU.add))
                dve.drain().then_inc(root_in, 1)
                me.wait(root_out)
                me.link(dve.reciprocal(stat[:, 104:108], stat[:, 22:26]))
                for half in range(NH2):
                    ts(cq[:, half, 0:QR], cq[:, half, 0:QR], stat[:, 104 + half:105 + half], None, ALU.mult)
                    last = ts(cq[:, half, QR:QR + KVR], cq[:, half, QR:QR + KVR], stat[:, 106 + half:107 + half], None, ALU.mult)
                last.then_inc(rows_ready, 1)
                split_banks(3, gain=row + ROW_Q, signal=True)
                for j in range(4):
                    g = me.gemm_pair(1 if j % 2 == 0 else 0, j % 2 == 1)
                    b = 2 * (g % 2)
                    if j == 1:
                        tt_copy(qrow[:, :, 288:576], PS[:, b:b + 2, 0:288]).then_inc(gemm_free[g % 2], 1)
                    elif j == 3:
                        for half in range(NH2):
                            kv = PS[:, b + half, 0:384].rearrange("p (h c) -> p h c", c=P)
                            tt_copy(krow[:, half, 288:576].rearrange("p (h c) -> p h c", c=MLA_QK)[:, :, 0:MLA_NOPE], kv[:, :, 0:MLA_NOPE])
                            last = tt_copy(v2[:, half, 192:384].rearrange("p (h c) -> p h c", c=64), kv[:, :, MLA_NOPE:P])
                        last.then_inc(gemm_free[g % 2], 1)
                HR = MLA_ROPE // 2
                tmp = sc[:, 0, 0:6 * HR]
                tmp2 = sc[:, 1, 0:6 * HR]

                def rotate(x1, x2, cos, sin, t1, t2):
                    tt(t1, x1, sin, ALU.mult)
                    me.link(tt(t2, x2, sin, ALU.mult))
                    tt(x1, x1, cos, ALU.mult)
                    me.link(tt(x2, x2, cos, ALU.mult))
                    tt(x1, x1, t2, ALU.subtract)
                    me.link(tt(x2, x2, t1, ALU.add))

                me.wait(qk_rows)
                for half in range(NH2):
                    q3 = qrow[:, half, :].rearrange("p (h c) -> p h c", c=MLA_QK)
                    t1 = tmp.rearrange("p (h c) -> p h c", c=HR)
                    t2 = tmp2.rearrange("p (h c) -> p h c", c=HR)
                    cos = cosT[:, half, :].unsqueeze(1).broadcast_to([P, MLA_H, HR])
                    sin = sinT[:, half, :].unsqueeze(1).broadcast_to([P, MLA_H, HR])
                    rotate(q3[:, :, MLA_NOPE:MLA_NOPE + HR], q3[:, :, MLA_NOPE + HR:MLA_QK], cos, sin, t1, t2)
                dve.drain().then_inc(rows_ready, 1)
                for half in range(NH2):
                    kr = cq[:, half, QR + KVR:QR + KVR + MLA_ROPE]
                    rotate(kr[:, 0:HR], kr[:, HR:2 * HR], cosT[:, half, :], sinT[:, half, :], tmp[:, 0:HR], tmp2[:, 0:HR])
                    k3 = krow[:, half, :].rearrange("p (h c) -> p h c", c=MLA_QK)
                    for h in range(MLA_H):
                        last = tt_copy(k3[:, h, MLA_NOPE:MLA_QK], kr)
                last.then_inc(rows_ready, 1)
                me.barrier()

                def read_group(group):
                    b = 4 + 2 * (group % 2)
                    if group == 0:
                        last = tt_copy(o2[:, :, 0:384], PS[:, b:b + 2, 0:384])
                    elif group == 1:
                        last = tt_copy(o3[:, :, :], PS[:, b:b + 2, 0:384])
                    elif group == 2:
                        last = stt(out=o3[:, :, :], in0=PS[:, b:b + 2, 0:384], scalar=stat[:, 44 + layer:45 + layer], in1=o3[:, :, :],
                                   op0=ALU.mult, op1=ALU.add)
                    else:
                        last = tt_copy(o2[:, :, 768:1024], PS[:, b:b + 2, 0:256])
                    last.then_inc(pv_read, 1)

                pv_seen = layer * N_MAPS
                for step in range(N_MAPS + 1):
                    if step < N_MAPS:
                        i = step % 2
                        me.wait(score_done)
                        if step >= 2:
                            me.wait(prob_turned)
                        bias, scale = items[step][2], items[step][3]
                        for blk, c0, w in ((0, 0, P), (1, P, T)):
                            last = dve.tensor_tensor_reduce(sc[:, i, c0:c0 + w], PS[:, i, c0:c0 + w], bias[:, c0:c0 + w], scale, -3e38,
                                                            ALU.add, ALU.max, stat[:, 60 + 2 * i + blk:61 + 2 * i + blk])
                        me.link(last)
                        dve.drain().then_inc(score_read, 1)
                        ts(stat[:, 52 + 2 * i:54 + 2 * i], stat[:, 60 + 2 * i:62 + 2 * i], -1.0, None, ALU.mult).then_inc(shifted, 1)
                    if step >= 1:
                        i = (step - 1) % 2
                        me.wait(exp_done)
                        me.link(dve.reciprocal(stat[:, 108 + 2 * i:110 + 2 * i], stat[:, 56 + 2 * i:58 + 2 * i]))
                        ts(sc[:, i, 0:P], sc[:, i, 0:P], stat[:, 108 + 2 * i:109 + 2 * i], None, ALU.mult)
                        ts(sc[:, i, P:BLK], sc[:, i, P:BLK], stat[:, 109 + 2 * i:110 + 2 * i], None, ALU.mult).then_inc(prob_ready, 1)
                    for group, end in enumerate(GROUP_ENDS):
                        if step == min(end + 3, N_MAPS):
                            dve.wait_ge(pv_done, pv_seen + end)
                            read_group(group)
                me.wait(prob_turned, 2)
                me.wait(pv_read, 4)
                sq = o2[:, :, 384:768]
                me.link(tt(sq, o3[:, :, :], o3[:, :, :], ALU.mult))
                me.link(dve.tensor_reduce(stat[:, 112:124], sq.rearrange("p h (n c) -> p h n c", c=HD), AX, ALU.add))
                me.link(ts(stat[:, 112:124], stat[:, 112:124], 1.0 / HD, RMS_EPS, ALU.mult, ALU.add))
                dve.drain().then_inc(root_in, 1)
                me.wait(root_out)
                me.link(dve.reciprocal(stat[:, 112:124], stat[:, 124:136]))
                for half in range(NH2):
                    for h in range(DIFF_H):
                        c = 112 + half * DIFF_H + h
                        last = stt(out=o2[:, half, 384 + h * HD:384 + (h + 1) * HD], in0=o3[:, half, h * HD:(h + 1) * HD], scalar=stat[:, c:c + 1],
                                   in1=subn[:, layer, :], op0=ALU.mult, op1=ALU.mult)
                me.link(last)
                me.link(ts(o2[:, :, 384:768], o2[:, :, 384:768], 1.0 - LAM_INIT[layer], None, ALU.mult))
                me.barrier()
                dve.drain().then_inc(rows_ready, 1)
                split_banks(KT, signal=True)
                add_wide(1.0)
                me.barrier()
                rms_rows(memx, memx).then_inc(rows_ready, 1)
                split_banks(KT, gain=row + ROW_MEM, signal=True)
                for nb in range(4):
                    g = me.gemm_pair(2, nb % 2 == 1)
                    b = 2 * (g % 2)
                    if nb == 1:
                        tt_copy(ckT[:, 4:8, :].rearrange("p k t -> p (k t)"), PSf[:, b * 512:b * 512 + 1024]).then_inc(gemm_free[g % 2], 1)
                    elif nb == 3:
                        tt_copy(cv[:, :, TW:D], PS[:, b:b + 2, :]).then_inc(gemm_free[g % 2], 1)
                me.barrier()
                rms_rows(x, xn).then_inc(rows_ready, 1)
                split_banks(KT, gain=row + ROW_CROSS, signal=True)
                for nb in range(2):
                    g = me.gemm_pair(2, nb == 1)
                    b = 2 * (g % 2)
                    if nb == 1:
                        tt_copy(cqT[:, 4:8, :].rearrange("p k t -> p (k t)"), PSf[:, b * 512:b * 512 + 1024]).then_inc(gemm_free[g % 2], 1)
                me.barrier()
                for step in range(CROSS_H + 1):
                    if step < CROSS_H:
                        i = step % 2
                        me.wait(x_scored)
                        me.link(dve.tensor_reduce(stat[:, 60 + 2 * i:62 + 2 * i], PS[:, i, :].rearrange("p (b m) -> p b m", b=2), AX, ALU.max))
                        ts(stat[:, 52 + 2 * i:54 + 2 * i], stat[:, 60 + 2 * i:62 + 2 * i], -CROSS_HD ** -0.5, None, ALU.mult).then_inc(x_max, 1)
                    if step >= 1:
                        i = (step - 1) % 2
                        me.wait(x_exp)
                        me.link(dve.reciprocal(stat[:, 108 + 2 * i:110 + 2 * i], stat[:, 56 + 2 * i:58 + 2 * i]))
                        ts(csc[:, i, 0:T], csc[:, i, 0:T], stat[:, 108 + 2 * i:109 + 2 * i], None, ALU.mult)
                        ts(csc[:, i, T:2 * T], csc[:, i, T:2 * T], stat[:, 109 + 2 * i:110 + 2 * i], None, ALU.mult).then_inc(x_prob, 1)
                split_banks(KT, 4)
                me.barrier()
                add_wide(1.0)
                me.barrier()
                rms_rows(x, xn).then_inc(rows_ready, 1)
                split_banks(KT, gain=row + ROW_MLP, signal=True)
                for part in range(2):
                    for nb in range(FF // 2 // TW):
                        me.gemm_pair(2, False)
                        me.wait(sq_in)
                        tt(fl[:, 4 * nb:4 * nb + 4, :].rearrange("p k t -> p (k t)"), rT[:, 1, :],
                           fh[:, 4 * nb:4 * nb + 4, :].rearrange("p k t -> p (k t)"), ALU.subtract).then_inc(fh_done, 1)
                    if part == 0:
                        for nb in range(2):
                            me.wide_half(4, False)
                add_wide.tiles = 4
                add_wide(1.0)
                add_wide.tiles = 2
                me.barrier()
            me.link(rms_rows(x, x))
            me.wait(ln_loaded, 16)
            for half in range(NH2):
                last = tt(x[:, half, :], x[:, half, :], lnp[:, 0, :], ALU.mult)
            last.then_inc(h_ready, 1)


_INS = ["x", "even_w_in", "even_conv_a", "even_conv_b_w", "even_conv_b_bias", "even_norm_b_g", "even_norm_b_b", "even_w_out",
        "odd_w_qkv", "odd_w_o", "ln_mix_g", "ln_mix_b", "ln_ffn_g", "ln_ffn_b", "router_group_w", "router_group_b",
        "router_expert_w", "router_expert_b", "expert_w_up", "expert_w_down", "mem_2", "positions_2", "attn_norm_2", "w_in_2",
        "mla_q_norm_2", "mla_w_uq_2", "mla_kv_norm_2", "mla_w_ukv_2", "diff_lambda_q1_2", "diff_lambda_k1_2", "diff_lambda_q2_2",
        "diff_lambda_k2_2", "diff_sub_norm_2", "w_out_2", "cross_norm_2", "mem_norm_2", "cross_wq_2", "cross_wkv_2", "cross_wo_2",
        "mlp_norm_2", "mlp_w1_2", "mlp_w2_2", "final_norm_2"]


def kernel(**inputs):
    import numpy as np
    import concourse.bacc as bacc
    from concourse.bass_utils import run_bass_kernel_spmd

    nc = bacc.Bacc("TRN2", target_bir_lowering=False, num_devices=1)
    arrays, aps = {}, {}

    def given(name, array):
        arrays[f"in_{name}_dram"] = array
        aps[name] = nc.dram_tensor(f"in_{name}_dram", array.shape, mybir.dt.from_np(array.dtype), kind="ExternalInput").ap()

    for name in _INS:
        given(name, np.ascontiguousarray(inputs[name]))
    half = MLA_ROPE // 2
    given("inv_freq", (10000.0 ** (-np.arange(half, dtype=np.float32) / np.float32(half))).astype(np.float32))
    out = nc.dram_tensor("out_0_dram", (1, T, D), F32, kind="ExternalOutput").ap()
    build(nc, aps, out)
    r = run_bass_kernel_spmd(nc, [arrays], core_ids=[0])
    return r.results[0]["out_0_dram"]
```

```python
import math
from contextlib import ExitStack

import concourse.bass as bass
from concourse import mybir

F32 = mybir.dt.float32
F32R = mybir.dt.float32r
I32 = mybir.dt.int32
ALU = mybir.AluOpType
ACT = mybir.ActivationFunctionType
AX = mybir.AxisListType.X

P = 128
D = 1024
KT = D // P
T = 256
NH2 = T // P
DEPTH = 2
ALPHA = (2 * DEPTH) ** 0.25
LN_EPS, RMS_EPS = 1e-5, 1e-6
NEG = -1e30

E_IN, CONV_A, CONV_B = 2560, 3, 31
IN_ORDER = (3, 4, 0, 1, 2)
SIDE_BLOCK = 3
SB_HEADS, HD = 16, 64
SB_GROUP = 4
NG, EPG = 4, 8
NE = NG * EPG
DE = 512
NR = NG + NE
CAP = 64

MLA_H, MLA_QK, MLA_NOPE, MLA_ROPE = 6, 96, 64, 32
QR, KVR = 256, 128
DIFF_H, DIFF_HD = 6, 32
MOBA_H = 4
CROSS_H, CROSS_HD = 4, 256
FF = 4096
N_ALIBI = DIFF_H + MOBA_H
SLOPES = [2.0 ** (-8.0 * (h + 1) / N_ALIBI) for h in range(N_ALIBI)]
BLK = 3 * P

TK = 2
TW = 512
KG = KT // TK
RAW = 12
CNV = 6
SIDE = (10, 12)
EXPERT_TILES = 12

ROW_ATTN, ROW_CROSS, ROW_MEM, ROW_MLP, ROW_Q, ROW_KV, ROWS_LAYER = 0, 8, 16, 24, 32, 34, 35
ROW_CONVA = DEPTH * ROWS_LAYER
ROW_BIAS = ROW_CONVA + 4 * CONV_A
ROW_NBG = ROW_BIAS + 4
ROW_NBB = ROW_NBG + 4
ROWS_A = ROW_NBB + 4

PROJ = [(0, 416, False), (416, 384, True), (800, 384, True), (1184, 384, False), (1568, 512, True), (2080, 256, False)]


class Lane:

    def __init__(self, eng, link_sem=None):
        self.e, self.link_sem = eng, link_sem
        self.seen, self.loop = {}, None

    def wait(self, sem, k=1):
        self.seen[sem.name] = self.seen.get(sem.name, 0) + k
        if self.loop is None:
            self.e.wait_ge(sem, self.seen[sem.name])
        else:
            i, per, _ = self.loop
            self.e.wait_ge(sem, self.seen[sem.name] + per[sem.name] * i)

    def link(self, ins):
        ins.then_inc(self.link_sem, 1)
        self.wait(self.link_sem)

    def enter(self, i, per):
        self.loop = (i, per, dict(self.seen))

    def leave(self, rounds):
        _, per, before = self.loop
        for name, n in per.items():
            assert self.seen.get(name, 0) - before.get(name, 0) == n, (name, n, self.seen.get(name, 0) - before.get(name, 0))
            self.seen[name] = before.get(name, 0) + n * rounds
        self.loop = None


def once(*sems):
    return {s.name: 1 for s in sems}


def weight_tiles(a):
    def cut(w, kg, c0, width, k=TK):
        return w[kg * TK * P:kg * TK * P + k * P, c0:c0 + width].rearrange("(k p) c -> p k c", p=P)

    def whole(w, kgs, width):
        return [cut(w, kg, c0, TW) for c0 in range(0, width, TW) for kg in range(kgs)]

    before = [cut(a["even_w_in"][0], kg, nb * TW, TW) for nb in IN_ORDER for kg in range(KG)] + whole(a["even_w_out"][0], KG, D)
    middle = whole(a["odd_w_qkv"][0], KG, 3 * D) + whole(a["odd_w_o"][0], KG, D)
    after = []
    for l in range(DEPTH):
        for c0, width, _ in PROJ:
            after += [cut(a["w_in_2"][l], kg, c0, width) for kg in range(KG)]
        after += [cut(a["mla_w_uq_2"][l], 0, c0, 288, 2) for c0 in (0, 288)]
        after += [cut(a["mla_w_ukv_2"][l], 0, c0, 384, 1) for c0 in (0, 384)]
        after += whole(a["w_out_2"][l], KG, D)
        after += whole(a["cross_wkv_2"][l], KG, 2 * D) + whole(a["cross_wq_2"][l], KG, D)
        after += whole(a["cross_wo_2"][l], KG, D)
        for f in range(2):
            after += whole(a["mlp_w1_2"][l][:, f * FF // 2:(f + 1) * FF // 2], KG, FF // 2)
            after += whole(a["mlp_w2_2"][l][f * FF // 2:(f + 1) * FF // 2, :], FF // 2 // (TK * P), D)
    return before, middle, after


def build(nc, a, out):
    before, middle, after = weight_tiles(a)
    n_moe = NE * EXPERT_TILES
    moe_start = [len(before), len(before) + n_moe + len(middle)]
    n_total = len(before) + len(middle) + len(after) + 2 * n_moe
    shapes = {}
    for first, tiles in ((0, before), (moe_start[0] + n_moe, middle), (moe_start[1] + n_moe, after)):
        for j, ap in enumerate(tiles):
            shapes[first + j] = (ap.shape[1], ap.shape[2])

    def shape_of(n):
        return shapes.get(n, (TK, TW))

    ctx = ExitStack()
    with ctx:
        def sb(name, shape, dt=F32, scope=ctx):
            return scope.enter_context(nc.sbuf_tensor(name, shape, dt))

        def sem(name):
            return ctx.enter_context(nc.semaphore(name))

        PS = ctx.enter_context(nc.psum_tensor("PS", [P, 8, 512], F32))
        PSf = PS[:, :, :].rearrange("p b c -> p (b c)")

        raw = sb("raw", [P, RAW, TK * TW])
        w_hi = sb("w_hi", [P, CNV, TK * TW], F32R)
        w_lo = sb("w_lo", [P, CNV, TK * TW], F32R)
        x = sb("x", [P, NH2, D])
        ah = sb("ah", [P, KT, T], F32R)
        al = sb("al", [P, KT, T], F32R)
        ident = sb("ident", [P, P])
        ones = sb("ones", [P, P])
        tri_after = sb("tri_after", [P, P])
        tri_before = sb("tri_before", [P, P])
        keep_t = sb("keep_t", [P, P])
        drop_t = sb("drop_t", [P, P])
        causal = sb("causal", [P, BLK])
        fold = sb("fold", [P, CAP])
        slot_no = sb("slot_no", [P, 2 * CAP])
        prio = sb("prio", [P, EPG])
        colA = sb("colA", [P, P])
        colB = sb("colB", [P, 4 * CONV_B])
        inv_freq = sb("inv_freq", [P, MLA_ROPE // 2])
        stat = sb("stat", [P, 256])
        subn = sb("subn", [P, DEPTH, HD])
        flag = sb("flag", [P, DEPTH], I32)
        lam_rows = sb("lam_rows", [P, DEPTH * 4, DIFF_HD])
        lnp = sb("lnp", [P, 2, D])

        def scoped(specs):
            scope = ExitStack()
            got = [sb(name, shape, dt, scope) for name, shape, dt in specs]
            scope.close()
            return got

        prmA, prmB = scoped([("prmA", [P, P], F32), ("prmB", [P, P], F32)])
        uT, pa, pb, ya, gb, tc = scoped([
            ("uT", [P, 20, T], F32), ("pa", [P, 4, CONV_A - 1 + T], F32), ("pb", [P, 4, CONV_B - 1 + T], F32),
            ("ya", [P, 4, T], F32), ("gb", [P, 4, T], F32), ("tc", [P, 4, T], F32)])
        (xT, xe, hs, sil, af, aT, yh, yl, SS, Pm, rw, rbias, lg, rs, Mt, Wt, slot, wc, ovf_w, ovf_h, ovf_a, ovf_wt) = scoped([
            ("xT", [P, KT, T], F32),
            ("xe", [P, KT, 2 * CAP], F32R), ("hs", [P, 2 * DE], F32), ("sil", [P, 4, CAP], F32),
            ("af", [P, 4, CAP], F32), ("aT", [P, 4, 2 * CAP], F32R), ("yh", [P, D], F32R), ("yl", [P, D], F32R),
            ("SS", [P, NH2, 2 * CAP], F32R), ("Pm", [P, T], F32R), ("rw", [P, KT, NR], F32), ("rbias", [P, NR], F32),
            ("lg", [P, NH2, NR], F32), ("rs", [P, NH2, 64], F32), ("Mt", [P, NH2, NE], F32), ("Wt", [P, NH2, NE], F32),
            ("slot", [P, NH2, NE + 1], F32), ("wc", [P, 1], F32),
            ("ovf_w", [P, DE], F32), ("ovf_h", [P, 2 * DE], F32), ("ovf_a", [P, 4, P], F32), ("ovf_wt", [P, NH2, NE], F32)])
        qT1, kT1, v1, zs, sp = scoped([
            ("qT1", [P, KT, T], F32), ("kT1", [P, KT, T], F32), ("v1", [P, NH2, D], F32),
            ("zs", [P, 2 * SB_GROUP, BLK], F32), ("sp", [P, 2 * SB_GROUP, BLK], F32)])
        tabs = ExitStack()
        alibi = sb("alibi", [P, N_ALIBI, BLK], F32, tabs)
        cosT = sb("cosT", [P, NH2, MLA_ROPE // 2], F32, tabs)
        sinT = sb("sinT", [P, NH2, MLA_ROPE // 2], F32, tabs)
        posq = sb("posq", [P, NH2], F32, tabs)
        posk, posi, posqi, dist, ang, angk = scoped([
            ("posk", [P, T], F32), ("posi", [P, T], I32), ("posqi", [P, NH2], I32), ("dist", [P, BLK], F32),
            ("ang", [P, NH2, 16], F32), ("angk", [P, NH2, 16], F32)])
        (cq, dqT, dkT, mqT, mkT, dv, mv, qrow, krow, v2, qa, ka, sc, o2) = scoped([
            ("cq", [P, NH2, 416], F32), ("dqT", [P, 3, T], F32), ("dkT", [P, 3, T], F32), ("mqT", [P, 2, T], F32),
            ("mkT", [P, 2, T], F32), ("dv", [P, NH2, 384], F32), ("mv", [P, NH2, 256], F32),
            ("qrow", [P, NH2, 576], F32), ("krow", [P, NH2, 576], F32), ("v2", [P, NH2, 384], F32),
            ("qa", [P, MLA_H, T], F32), ("ka", [P, MLA_H, T], F32), ("sc", [P, 3, BLK], F32),
            ("o2", [P, NH2, D], F32)])
        pT = cq[:, :, :].rearrange("p h c -> p (h c)")[:, 0:2 * BLK].rearrange("p (i c) -> p i c", i=2)
        o3 = qrow[:, :, 0:384]
        cqT, ckT, cv, csc, cpT, memx = scoped([
            ("cqT", [P, KT, T], F32), ("ckT", [P, KT, T], F32), ("cv", [P, NH2, D], F32), ("csc", [P, 2, 512], F32),
            ("cpT", [P, 2, 512], F32), ("memx", [P, NH2, D], F32)])
        rT, fh, fl = scoped([("rT", [P, 2, 1024], F32), ("fh", [P, FF // P // 2, T], F32R), ("fl", [P, FF // P // 2, T], F32R)])
        tabs.close()

        raw_loaded = [sem(f"raw_loaded{s}") for s in range(RAW)]
        hi_ready = sem("hi_ready")
        lo_ready = sem("lo_ready")
        w_used = sem("w_used")
        params = sem("params")
        consts = sem("consts")
        ln_loaded = sem("ln_loaded")
        ln_used = sem("ln_used")
        mem_loaded = sem("mem_loaded")
        pos_loaded = sem("pos_loaded")
        gemm_free = [sem("gemm_free0"), sem("gemm_free1")]
        moe_done = sem("moe_done")
        router_loaded = sem("router_loaded")
        turned = sem("turned")
        turn_hi = sem("turn_hi")
        turn_ready = sem("turn_ready")
        rows_ready = sem("rows_ready")
        root_in, root_out = sem("root_in"), sem("root_out")
        ssq_done = sem("ssq_done")
        pe_stage, act_stage, dve_stage = sem("pe_stage"), sem("act_stage"), sem("dve_stage")
        pe_link, act_link, dve_link = sem("pe_link"), sem("act_link"), sem("dve_link")
        gate_sig = sem("gate_sig")
        conv_in = sem("conv_in")
        mix_copied = sem("mix_copied")
        side_conv = sem("side_conv")
        pool_link = sem("pool_link")
        conv_b_done = sem("conv_b_done")
        chan_mean = sem("chan_mean")
        sq_ready = sem("sq_ready")
        normed = sem("normed")
        mix_hi = sem("mix_hi")
        logits_done = sem("logits_done")
        rexp_in, rexp_out = sem("rexp_in"), sem("rexp_out")
        member_ready = sem("member_ready")
        rank_done = sem("rank_done")
        ss_ready = sem("ss_ready")
        t_done = sem("t_done")
        p_copied = sem("p_copied")
        g0_done, g1_done = sem("g0_done"), sem("g1_done")
        xe_hi = [sem("xe_hi0"), sem("xe_hi1")]
        xe0, xe1 = sem("xe0"), sem("xe1")
        hs_gate, hs_up = sem("hs_gate"), sem("hs_up")
        fg_done = sem("fg_done")
        f_done = sem("f_done")
        silu_done, act_ready = sem("silu_done"), sem("act_ready")
        yh0, yh1, yl0, yl1 = sem("yh0"), sem("yh1"), sem("yl0"), sem("yl1")
        score_done = sem("score_done")
        score_read = sem("score_read")
        shifted = sem("shifted")
        exp_done = sem("exp_done")
        prob_ready = sem("prob_ready")
        prob_turned = sem("prob_turned")
        prob_copied = sem("prob_copied")
        pv_done = sem("pv_done")
        pv_read = sem("pv_read")
        soft_abs = sem("soft_abs")
        later_read = sem("later_read")
        soft_ready = sem("soft_ready")
        later_done = sem("later_done")
        logit_ready = sem("logit_ready")
        share_ready = sem("share_ready")
        sb_scored, sb_read, sb_pv = sem("sb_scored"), sem("sb_read"), sem("sb_pv")
        heads_copied = sem("heads_copied")
        x_scored, x_max, x_exp, x_prob = sem("x_scored"), sem("x_max"), sem("x_exp"), sem("x_prob")
        x_turned, x_copied, x_pv = sem("x_turned"), sem("x_copied"), sem("x_pv")
        sin_in, sin_out = sem("sin_in"), sem("sin_out")
        sq_in, fh_done = sem("sq_in"), sem("fh_done")
        qk_rows, dve_half = sem("qk_rows"), sem("dve_half")
        h_ready = sem("h_ready")
        lam_in, lam_out = sem("lam_in"), sem("lam_out")
        stored = sem("stored")
        side_split = sem("side_split")
        ov = [{k: sem(f"ov{l}_{k}") for k in ("w", "mm", "copied", "act", "turn", "tcopy", "down", "add", "link", "alink", "wt", "silu")}
              for l in range(DEPTH)]

        xn = lnp

        MAX, NEG_MAX, SUM, SHARE = 136, 142, 148, 154
        items = []
        for h in range(MLA_H):
            items.append((qa[0:MLA_QK, h, :], ka[0:MLA_QK, h, :], causal, MLA_QK ** -0.5, v2[:, :, h * HD:(h + 1) * HD], 4, h * HD))
        for j in range(2):
            for h in range(DIFF_H):
                r = slice(64 * (h % 2) + DIFF_HD * j, 64 * (h % 2) + DIFF_HD * (j + 1))
                items.append((dqT[r, h // 2, :], dkT[r, h // 2, :], alibi[:, h, :], DIFF_HD ** -0.5, dv[:, :, h * HD:(h + 1) * HD], 6 - 2 * j, h * HD))
        for h in range(MOBA_H):
            r = slice(HD * (h % 2), HD * (h % 2) + HD)
            items.append((mqT[r, h // 2, :], mkT[r, h // 2, :], alibi[:, DIFF_H + h, :], HD ** -0.5, mv[:, :, h * HD:(h + 1) * HD], 6, h * HD))
        N_MAPS = len(items)
        GROUP_ENDS = (MLA_H, MLA_H + DIFF_H, MLA_H + 2 * DIFF_H, N_MAPS)
        GROUP_REUSES = (MLA_H + DIFF_H, MLA_H + 2 * DIFF_H)
        LAM_INIT = [0.8 - 0.6 * math.exp(-0.3 * l) for l in range(DEPTH)]
        TWO_PI_PARTS = (6.28125, 0.0019350051879882812, 3.019915981956753e-07)

        def tile_view(buf, slot, n):
            kts, width = shape_of(n)
            return buf[:, slot, 0:kts * width].rearrange("p (k c) -> p k c", k=kts)

        class Engine(Lane):

            def __init__(self, eng, link_sem, own_stage, stages, convert=None):
                super().__init__(eng, link_sem)
                self.n = self.g = self.converted = 0
                self.own_stage, self.stages, self.convert = own_stage, stages, convert
                self.k = 0

            def pump(self, upto):
                while self.converted <= min(upto, n_total - 1):
                    self.convert(self.converted)
                    self.converted += 1

            def barrier(self):
                self.e.drain().then_inc(self.own_stage, 1)
                self.k += 1
                for s in self.stages:
                    if s is not self.own_stage:
                        self.e.wait_ge(s, self.k)

            def gemm_pair(self, tiles, mine, part=False):
                self.n += tiles
                self.pump(self.n - 1 + CNV - 1)
                g = self.g
                self.g += 1
                if mine:
                    self.e.wait_ge(w_used, self.n)
                return g

            def wide_half(self, tiles, mine):
                self.n += tiles
                self.pump(self.n - 1 + CNV - 1)
                if mine:
                    self.e.wait_ge(w_used, self.n)

        STAGES = (pe_stage, act_stage, dve_stage)
        PARAM_LOADS = 6 * DEPTH + 5 + 1 + 4 + 1
        OVF_HALF, OVF_LOADS = 2 * KT + 8, 2 * (2 * KT + 8)
        EXPERTS_FROM = (4, 10)
        ROUTER_FROM, POS_FROM, MEM_FROM, FINAL_FROM = (2, 8), 12, (18, 28), 33

        block = ctx.enter_context(nc.Block())

        @block.sync
        def _(sp):
            count = [0]

            def param(dst, src):
                sp.dma_start(dst, src).then_inc(params, 16)
                count[0] += 16

            sp.dma_start(x[:, :, :], a["x"][0].rearrange("(h p) d -> p h d", p=P)).then_inc(h_ready, 16)

            def load(n, src):
                slot = n % RAW
                if n >= RAW:
                    sp.wait_ge(lo_ready, n - RAW + 1)
                sp.dma_start(tile_view(raw, slot, n), src).then_inc(raw_loaded[slot], 16)

            for n in range(2):
                load(n, before[n])
            sp.wait_ge(consts, 1)
            for l in range(DEPTH):
                for row, name, k in ((ROW_ATTN, "attn_norm_2", 8), (ROW_CROSS, "cross_norm_2", 8), (ROW_MEM, "mem_norm_2", 8),
                                     (ROW_MLP, "mlp_norm_2", 8), (ROW_Q, "mla_q_norm_2", 2), (ROW_KV, "mla_kv_norm_2", 1)):
                    r = l * ROWS_LAYER + row
                    param(prmA[r:r + k, :], a[name][l].rearrange("(k p) -> k p", p=P))
            param(prmA[ROW_CONVA:ROW_CONVA + 4 * CONV_A, :], a["even_conv_a"][0].rearrange("j (k p) -> (j k) p", p=P))
            param(prmA[ROW_BIAS:ROW_BIAS + 4, :], a["even_conv_b_bias"][0].rearrange("(k p) -> k p", p=P))
            param(prmA[ROW_NBG:ROW_NBG + 4, :], a["even_norm_b_g"][0].rearrange("(k p) -> k p", p=P))
            param(prmA[ROW_NBB:ROW_NBB + 4, :], a["even_norm_b_b"][0].rearrange("(k p) -> k p", p=P))
            param(prmB[0:4 * CONV_B, :], a["even_conv_b_w"][0].rearrange("j (k p) -> (j k) p", p=P))
            param(inv_freq[:, :], a["inv_freq"].partition_broadcast(P))
            for j, name in enumerate(("q1", "k1", "q2", "k2")):
                param(lam_rows[:, j * DEPTH:(j + 1) * DEPTH, :], a[f"diff_lambda_{name}_2"].partition_broadcast(P))
            param(subn[:, :, :], a["diff_sub_norm_2"].partition_broadcast(P))
            assert count[0] == 16 * PARAM_LOADS

            for n in range(2, len(before)):
                load(n, before[n])
            for layer, rest in ((0, middle), (1, after)):
                n0 = moe_start[layer]
                w_up, w_down = a["expert_w_up"][layer], a["expert_w_down"][layer]
                with sp.Fori(0, NE) as e:
                    ups = w_up[bass.ds(e, 1)].rearrange("a (k p) c -> p (a k) c", p=P)
                    downs = w_down[bass.ds(e, 1)].rearrange("a (k p) c -> p (a k) c", p=P)
                    for k in range(EXPERT_TILES):
                        if k < 2 * KG:
                            src = ups[:, (k % KG) * TK:(k % KG + 1) * TK, (k // KG) * DE:(k // KG + 1) * DE]
                        else:
                            j = k - 2 * KG
                            kg, nb = j % (KG // 2), j // (KG // 2)
                            src = downs[:, kg * TK:(kg + 1) * TK, nb * TW:(nb + 1) * TW]
                        slot = (n0 + k) % RAW
                        sp.wait_ge(lo_ready, e * EXPERT_TILES + (n0 + k - RAW + 1))
                        sp.dma_start(tile_view(raw, slot, n0), src).then_inc(raw_loaded[slot], 16)
                for j in range(CNV):
                    load(n0 + n_moe + j, rest[j])
                o = ov[layer]
                more = sp.value_load(flag[0:1, layer:layer + 1], min_val=0, max_val=1)
                with sp.If(more > 0):
                    with sp.Fori(0, NE) as e:
                        ups = w_up[bass.ds(e, 1)].rearrange("a (k p) c -> p (a k) c", p=P)
                        downs = w_down[bass.ds(e, 1)].rearrange("a (k p) c -> p (a k) c", p=P)
                        for half in range(NH2):
                            for j in range(OVF_HALF):
                                src = ups[:, j // 2, (j % 2) * DE:(j % 2 + 1) * DE] if j < 2 * KT else \
                                    downs[:, (j - 2 * KT) // 2, (j % 2) * TW:(j % 2 + 1) * TW]
                                sp.wait_ge(o["mm"], e * OVF_LOADS + (half * OVF_HALF + j + 1))
                                sp.dma_start(ovf_w[:, :], src).then_inc(o["w"], 16)
                for j in range(CNV, len(rest)):
                    load(n0 + n_moe + j, rest[j])
            sp.wait_ge(h_ready, 16 + 1)
            sp.dma_start(out[0].rearrange("(h p) d -> p h d", p=P), x[:, :, :]).then_inc(stored, 16)
            sp.wait_ge(stored, 16)

        @block.gpsimd
        def _(pool):
            pool.memset(prmA[:, :], 0.0)
            pool.memset(prmB[:, :], 0.0).then_inc(consts, 1)
            pool.memset(ident[:, :], 0.0)
            pool.memset(ones[:, :], 1.0)
            pool.memset(tri_after[:, :], 1.0)
            pool.memset(tri_before[:, :], 1.0)
            pool.memset(keep_t[:, :], 1.0)
            pool.memset(drop_t[:, :], 0.0)
            pool.memset(causal[:, :], 0.0)
            pool.memset(fold[:, :], 0.0).then_inc(consts, 1)
            pool.wait_ge(consts, 2)
            sel = pool.affine_select
            sel(out=ident[:, :], in_=ident[:, :], pattern=[[-1, P]], compare_op=ALU.not_equal, fill=1.0, base=0, channel_multiplier=1)
            sel(out=tri_after[:, :], in_=tri_after[:, :], pattern=[[-1, P]], compare_op=ALU.is_ge, fill=0.0, base=0, channel_multiplier=1)
            sel(out=tri_before[:, :], in_=tri_before[:, :], pattern=[[1, P]], compare_op=ALU.is_gt, fill=0.0, base=0, channel_multiplier=-1)
            sel(out=keep_t[:, :], in_=keep_t[:, :], pattern=[[1, P]], compare_op=ALU.is_gt, fill=0.0, base=0, channel_multiplier=-1)
            sel(out=drop_t[:, :], in_=drop_t[:, :], pattern=[[1, P]], compare_op=ALU.is_gt, fill=NEG, base=0, channel_multiplier=-1)
            sel(out=causal[:, 0:P], in_=causal[:, 0:P], pattern=[[-1, P]], compare_op=ALU.is_ge, fill=NEG, base=0, channel_multiplier=1)
            sel(out=causal[:, P:BLK], in_=causal[:, P:BLK], pattern=[[-1, T]], compare_op=ALU.is_ge, fill=NEG, base=P, channel_multiplier=1)
            sel(out=fold[:, :], in_=fold[:, :], pattern=[[-1, CAP]], compare_op=ALU.not_equal, fill=1.0, base=0, channel_multiplier=1).then_inc(consts, 1)
            pool.wait_ge(consts, 3)
            sel(out=fold[:, :], in_=fold[:, :], pattern=[[-1, CAP]], compare_op=ALU.not_equal, fill=1.0, base=-CAP, channel_multiplier=1)
            pool.iota(slot_no[:, :], pattern=[[0, 2], [1, CAP]], base=0, channel_multiplier=0, allow_small_or_imprecise_dtypes=True)
            pool.iota(prio[:, :], pattern=[[-1, EPG]], base=EPG, channel_multiplier=0, allow_small_or_imprecise_dtypes=True).then_inc(consts, 1)

            def norm_params(k, names, layer):
                if k:
                    pool.wait_ge(ln_used, k)
                for j, name in enumerate(names):
                    src = a[name][layer] if layer is not None else a[name]
                    pool.dma_start(lnp[:, j, :], src.partition_broadcast(P)).then_inc(ln_loaded, 16)

            lane = Lane(pool, pool_link)
            for layer in range(DEPTH):
                norm_params(2 * layer, ("ln_mix_g", "ln_mix_b"), layer)
                if layer == 0:
                    pool.wait_ge(dve_stage, 1)
                    pool.wait_ge(conv_in, 1)
                    c = SIDE_BLOCK
                    term = uT[:, 12:14, :]

                    def tap(j):
                        w = colB[:, 4 * j + c:4 * j + c + 1]
                        return pool.tensor_scalar(term[:, j % 2, :], pb[:, c, j:j + T], w, None, ALU.mult)

                    pool.tensor_scalar(gb[:, c, :], pb[:, c, 0:T], colB[:, c:c + 1], colA[:, ROW_BIAS + c:ROW_BIAS + c + 1], ALU.mult, ALU.add)
                    lane.link(tap(1))
                    for j in range(1, CONV_B):
                        if j + 1 < CONV_B:
                            tap(j + 1)
                        lane.link(pool.tensor_tensor(gb[:, c, :], gb[:, c, :], term[:, j % 2, :], ALU.add))
                    pool.drain().then_inc(side_conv, 1)
                    pool.wait_ge(mix_copied, 1)
                    lane.link(pool.tensor_tensor(pa[:, :, CONV_A - 1:], uT[:, 4:8, :], uT[:, 8:12, :], ALU.mult))
                    for j in range(CONV_A):
                        dst = ya if j == 0 else uT[:, 4 * j:4 * j + 4, :]
                        for c in range(4):
                            w = colA[:, ROW_CONVA + 4 * j + c:ROW_CONVA + 4 * j + c + 1]
                            last = pool.tensor_scalar(dst[:, c, :], pa[:, c, j:j + T], w, None, ALU.mult)
                    lane.link(last)
                    for j in range(1, CONV_A):
                        lane.link(pool.tensor_tensor(ya[:, :, :], ya[:, :, :], uT[:, 4 * j:4 * j + 4, :], ALU.add))
                    pool.tensor_tensor(ya[:, :, :], ya[:, :, :], uT[:, 0:4, :], ALU.mult).then_inc(side_conv, 1)
                pool.wait_ge(dve_stage, ROUTER_FROM[layer])
                pool.wait_ge(act_stage, ROUTER_FROM[layer])
                pool.wait_ge(pe_stage, ROUTER_FROM[layer])
                pool.dma_start(rw[:, :, 0:NG], a["router_group_w"][layer].rearrange("(k p) n -> p k n", p=P)).then_inc(router_loaded, 16)
                pool.dma_start(rw[:, :, NG:NR], a["router_expert_w"][layer].rearrange("(k p) n -> p k n", p=P)).then_inc(router_loaded, 16)
                pool.dma_start(rbias[:, 0:NG], a["router_group_b"][layer].partition_broadcast(P)).then_inc(router_loaded, 16)
                pool.dma_start(rbias[:, NG:NR], a["router_expert_b"][layer].partition_broadcast(P)).then_inc(router_loaded, 16)
                norm_params(2 * layer + 1, ("ln_ffn_g", "ln_ffn_b"), layer)
                for s in STAGES:
                    pool.wait_ge(s, EXPERTS_FROM[layer])
                n0 = moe_start[layer]
                with pool.Fori(0, NE) as e:
                    for k in SIDE:
                        n = n0 + k
                        pool.wait_ge(hi_ready, e * EXPERT_TILES + (n + 1))
                        pool.tensor_tensor(tile_view(w_lo, n % CNV, n0), tile_view(raw, n % RAW, n0), tile_view(w_hi, n % CNV, n0),
                                           ALU.subtract).then_inc(side_split, 1)
            pool.wait_ge(ln_used, 4)
            pool.wait_ge(dve_stage, POS_FROM)
            pool.wait_ge(act_stage, POS_FROM)
            pool.wait_ge(pe_stage, POS_FROM)
            pool.dma_start(posi[:, :], a["positions_2"][0].partition_broadcast(P)).then_inc(pos_loaded, 16)
            pool.dma_start(posqi[:, :], a["positions_2"][0].rearrange("(h p) -> p h", p=P), allow_slow_non_contiguous=True).then_inc(pos_loaded, 16)
            for layer in range(DEPTH):
                for s in STAGES:
                    pool.wait_ge(s, MEM_FROM[layer])
                pool.dma_start(memx[:, :, :], a["mem_2"][0].rearrange("(h p) d -> p h d", p=P)).then_inc(mem_loaded, 16)
            for s in STAGES:
                pool.wait_ge(s, FINAL_FROM)
            pool.dma_start(lnp[:, 0, :], a["final_norm_2"].partition_broadcast(P)).then_inc(ln_loaded, 16)

        @block.tensor
        def _(pe):
            me = Engine(pe, pe_link, pe_stage, STAGES)
            me.pump = lambda upto: None

            def mm(outp, lhsT, rhs, start, stop):
                return pe.matmul(outp, lhsT, rhs, start=start, stop=stop, skip_group_check=True)

            def tile(width_only=None):
                n = me.n
                pe.wait_ge(lo_ready, n + 1)
                me.n += 1
                return tile_view(w_hi, n % CNV, n), tile_view(w_lo, n % CNV, n)

            def three(outp, lh, ll, rh, rl, start, stop):
                mm(outp, lh, rh, start, False)
                mm(outp, ll, rh, False, False)
                return mm(outp, lh, rl, False, stop)

            def open_pair():
                g = me.g
                if g >= 2:
                    pe.wait_ge(gemm_free[g % 2], g // 2)
                me.g += 1
                return 2 * (g % 2)

            def rows_pair(kts, width, halves_cols=None, k0=0):
                b = open_pair()
                for kg in range(0, kts, TK):
                    wh, wl = tile()
                    for half in range(NH2):
                        tok = slice(half * P, half * P + P)
                        for k in range(min(TK, kts - kg)):
                            kt = kg + k
                            last = three(PS[:, b + half, 0:width], ah[:, k0 + kt, tok], al[:, k0 + kt, tok], wh[:, k, :], wl[:, k, :],
                                         kt == 0, kt == kts - 1)
                    last.then_inc(w_used, 1)

            def cols_pair(width, kts=KT):
                b = open_pair()
                for kg in range(0, kts, TK):
                    wh, wl = tile()
                    for k in range(TK):
                        kt = kg + k
                        for eb in range(width // P):
                            ch = slice(eb * P, eb * P + P)
                            o = PS[:, b + eb // 2, (eb % 2) * T:(eb % 2 + 1) * T]
                            first, stop = kt == 0 and eb % 2 == 0, kt == kts - 1
                            mm(o, wh[:, k, ch], ah[:, kt, :], first, False)
                            mm(o, wh[:, k, ch], al[:, kt, :], False, False)
                            last = mm(o, wl[:, k, ch], ah[:, kt, :], False, stop)
                    last.then_inc(w_used, 1)

            def wide(actsh, actsl, kts, first=True, final=True):
                for nb in range(2):
                    for kg in range(0, kts, TK):
                        wh, wl = tile()
                        for half in range(NH2):
                            tok = slice(half * P, half * P + P)
                            for k in range(TK):
                                kt = kg + k
                                last = three(PS[:, 4 + 2 * nb + half, :], actsh[:, kt, tok], actsl[:, kt, tok], wh[:, k, :], wl[:, k, :],
                                             first and kt == 0, final and kt == kts - 1)
                        last.then_inc(w_used, 1)

            def turn(src, kts=KT, wait=True, c0=0):
                if wait:
                    me.wait(rows_ready)
                for b in range((kts + 1) // 2):
                    for kt in range(2 * b, min(2 * b + 2, kts)):
                        for half in range(NH2):
                            c = (kt % 2) * T + half * P
                            last = pe.transpose(PS[:, b, c:c + P], src[:, half, c0 + kt * P:c0 + (kt + 1) * P], ident[:, :])
                    last.then_inc(turned, 1)

            pe.wait_ge(consts, 4)
            pe.wait_ge(params, 16 * PARAM_LOADS)
            pe.wait_ge(h_ready, 16)
            pe.transpose(PS[:, 7, 0:P], prmA[:, :], ident[:, :])
            pe.transpose(PS[:, 7, P:2 * P], prmB[:, :], ident[:, :]).then_inc(turned, 1)
            turn(x, wait=False)
            me.barrier()

            for nb in range(E_IN // TW):
                cols_pair(TW)
            me.wait(conv_b_done)
            me.wait(side_conv)
            for blk in range(4):
                last = mm(PS[:, 4, 0:T], ones[:, :], gb[:, blk, :], blk == 0, blk == 3)
            last.then_inc(chan_mean, 1)
            me.wait(sq_ready)
            for blk in range(4):
                last = mm(PS[:, 5, 0:T], ones[:, :], tc[:, blk, :], blk == 0, blk == 3)
            last.then_inc(chan_mean, 1)
            me.barrier()

            def router_and_experts(layer):
                me.wait(router_loaded, 64)
                for half in range(NH2):
                    for kt in range(KT):
                        last = mm(PS[:, 0, half * 64:half * 64 + NR], xT[:, kt, half * P:half * P + P], rw[:, kt, :], kt == 0, kt == KT - 1)
                last.then_inc(logits_done, 1)
                me.wait(member_ready)
                mm(PS[:, 1, 0:NE], tri_before[:, :], Mt[:, 0, :], True, True)
                mm(PS[:, 1, NE:2 * NE], tri_before[:, :], Mt[:, 1, :], True, False)
                mm(PS[:, 1, NE:2 * NE], ones[:, :], Mt[:, 0, :], False, True)
                mm(PS[:, 1, 2 * NE:3 * NE], ones[:, :], Mt[:, 0, :], True, False)
                mm(PS[:, 1, 2 * NE:3 * NE], ones[:, :], Mt[:, 1, :], False, True).then_inc(rank_done, 1)
                me.barrier()

                def gather(kts, bank):
                    for k in kts:
                        for half in range(NH2):
                            last = mm(PS[:, bank, (k % 4) * CAP:(k % 4 + 1) * CAP], x[:, half, k * P:(k + 1) * P],
                                      SS[:, half, 0:CAP].bitcast(F32), half == 0, half == 1)
                    return last

                def combine(outputs=range(2 * NH2)):
                    for o in outputs:
                        nb, half = o // NH2, o % NH2
                        for part in (yh, yl):
                            last = mm(PS[:, 4 + o, :], Pm[:, half * P:half * P + P], part[:, nb * TW:(nb + 1) * TW], False, False)
                    return last

                me.wait(ss_ready)
                for nb in range(2):
                    for half in range(NH2):
                        mm(PS[:, 4 + 2 * nb + half, :], Pm[:, half * P:half * P + P], yh[:, nb * TW:(nb + 1) * TW], True, False)
                gather(range(0, 4), 1).then_inc(g0_done, 1)
                gather(range(4, 8), 3).then_inc(g1_done, 1)
                n0 = me.n
                with pe.Fori(0, NE) as e:
                    me.enter(e, once(xe0, xe1, yl0, yl1, p_copied, ss_ready, hs_gate, hs_up, act_ready))

                    def product(bank, k0, kts, operand, from_kt=0, to_kt=None):
                        for kt in range(from_kt, kts if to_kt is None else to_kt):
                            slot, q = (n0 + k0 + kt // TK) % CNV, kt % TK
                            if q == 0:
                                pe.wait_ge(lo_ready, e * EXPERT_TILES + (n0 + k0 + kt // TK + 1))
                            mm(PS[:, bank, :], operand[:, kt, :], w_hi[:, slot, q * TW:(q + 1) * TW], kt == 0, False)
                            last = mm(PS[:, bank, :], operand[:, kt, :], w_lo[:, slot, q * TW:(q + 1) * TW], False, kt == kts - 1)
                            if q == TK - 1:
                                last.then_inc(w_used, 1)

                    me.wait(yl0)
                    me.wait(xe0)
                    product(0, 0, KT, xe, to_kt=KT // 2)
                    me.wait(xe1)
                    product(0, 0, KT, xe, from_kt=KT // 2)
                    product(1, KG, KT, xe)
                    me.wait(yl1)
                    me.wait(hs_gate)
                    for c in range(DE // P):
                        last = mm(PS[:, 3, c * CAP:(c + 1) * CAP], hs[:, c * P:(c + 1) * P], fold[:, :], True, True)
                    last.then_inc(fg_done, 1)
                    combine(range(0, 1))
                    me.wait(hs_up)
                    for c in range(DE // P):
                        last = mm(PS[:, 2, c * CAP:(c + 1) * CAP], hs[:, DE + c * P:DE + (c + 1) * P], fold[:, :], True, True)
                    last.then_inc(f_done, 1)
                    combine(range(1, 2 * NH2))
                    pe.transpose(PS[:, 1, 0:P], SS[:, 0, :].bitcast(F32), ident[:, :])
                    pe.transpose(PS[:, 1, P:2 * P], SS[:, 1, :].bitcast(F32), ident[:, :])
                    for half in range(NH2):
                        last = mm(PS[:, 1, 2 * P:2 * P + NE], SS[:, half, :].bitcast(F32), Wt[:, half, :], half == 0, half == 1)
                    last.then_inc(t_done, 1)
                    me.wait(act_ready)
                    product(0, 2 * KG, DE // P, aT)
                    product(2, 2 * KG + KG // 2, DE // P, aT)
                    me.wait(p_copied)
                    me.wait(ss_ready)
                    gather(range(0, 4), 1).then_inc(g0_done, 1)
                    gather(range(4, 8), 3).then_inc(g1_done, 1)
                    me.leave(NE)
                me.n = n0 + n_moe
                me.wait(yl0)
                me.wait(yl1)
                me.wait(xe0)
                me.wait(xe1)
                combine().then_inc(moe_done, 1)
                overflow(layer)
                me.barrier()

            def overflow(layer):
                o = ov[layer]
                more = pe.value_load(flag[0:1, layer:layer + 1], min_val=0, max_val=1)
                with pe.If(more > 0):
                    with pe.Fori(0, NE) as e:
                        for half in range(NH2):
                            tok = slice(half * P, half * P + P)
                            if half == 0:
                                pe.wait_ge(o["add"], e * 2 + 1)
                            else:
                                pe.wait_ge(o["add"], e * 2 + 2)
                            for j in range(2 * KT):
                                pe.wait_ge(o["w"], e * (16 * OVF_LOADS) + 16 * (half * OVF_HALF + j + 1))
                                mm(PS[:, j % 2, :], xT[:, j // 2, tok], ovf_w[:, :], j // 2 == 0, j // 2 == KT - 1).then_inc(o["mm"], 1)
                            pe.wait_ge(o["act"], e * 2 + (half + 1))
                            for c in range(4):
                                last = pe.transpose(PS[:, 2, c * P:(c + 1) * P], ovf_h[:, c * P:(c + 1) * P], ident[:, :])
                            last.then_inc(o["turn"], 1)
                            pe.wait_ge(o["tcopy"], e * 2 + (half + 1))
                            for j in range(8):
                                pe.wait_ge(o["w"], e * (16 * OVF_LOADS) + 16 * (half * OVF_HALF + 2 * KT + j + 1))
                                mm(PS[:, j % 2, :], ovf_a[:, j // 2, :], ovf_w[:, :], j // 2 == 0, j // 2 == 3).then_inc(o["mm"], 1)

            wide(ah, al, KT)
            turn(x)
            me.barrier()
            router_and_experts(0)
            turn(x)
            me.barrier()

            for nb in range(4):
                cols_pair(TW)
            for nb in range(2):
                rows_pair(KT, TW)
            me.barrier()

            def rows_of(h):
                return slice(HD * (h % 2), HD * (h % 2) + HD)

            def sb_scores(h):
                if h >= 2:
                    pe.wait_ge(sb_read, h - 1)
                r, kt = rows_of(h), h // 2
                mm(PS[:, h % 2, 0:T], kT1[r, kt, 0:P], qT1[r, kt, :], True, True)
                mm(PS[:, h % 2, T:BLK], kT1[r, kt, P:T], qT1[r, kt, P:T], True, True).then_inc(sb_scored, 1)

            def sb_later(h):
                if h % SB_GROUP == 0:
                    pe.wait_ge(soft_ready, h // SB_GROUP + 1)
                if h >= 2:
                    pe.wait_ge(later_read, h - 1)
                b, l = 2 + h % 2, sp[:, h % (2 * SB_GROUP), :]
                mm(PS[:, b, 0:T], tri_after[:, :], l[:, 0:T], True, False)
                mm(PS[:, b, P:T], ones[:, :], l[:, T:BLK], False, True)
                mm(PS[:, b, T:BLK], tri_after[:, :], l[:, T:BLK], True, True).then_inc(later_done, 1)

            def sb_values(h):
                if h % SB_GROUP == 0:
                    pe.wait_ge(share_ready, h // SB_GROUP + 1)
                r, kt = rows_of(h), h // 2
                b, c0 = 4 + kt // 2, (kt % 2) * T
                v, share = v1[:, :, h * HD:(h + 1) * HD], zs[:, h % (2 * SB_GROUP), :]
                mm(PS[r, b, c0:c0 + T], v[:, 0, :], share[:, 0:T], True, False)
                mm(PS[r, b, c0 + P:c0 + T], v[:, 1, :], share[:, T:BLK], False, True).then_inc(sb_pv, 1)

            for step in range(SB_HEADS // SB_GROUP + 2):
                for stage, lag in ((sb_values, 2), (sb_scores, 0), (sb_later, 1)):
                    if 0 <= step - lag < SB_HEADS // SB_GROUP:
                        for h in range((step - lag) * SB_GROUP, (step - lag + 1) * SB_GROUP):
                            stage(h)
            me.barrier()

            wide(ah, al, KT)
            turn(x)
            me.barrier()
            router_and_experts(1)
            me.barrier()
            me.barrier()

            for layer in range(DEPTH):
                turn(xn)
                me.barrier()
                for c0, width, channel_major in PROJ:
                    cols_pair(width) if channel_major else rows_pair(KT, width)
                me.barrier()
                turn(cq, 3)
                me.wait(turn_ready)
                for kts, width, k0 in ((2, 288, 0), (2, 288, 0), (1, 384, 2), (1, 384, 2)):
                    rows_pair(kts, width, k0=k0)
                for rows in (qrow, krow):
                    me.wait(rows_ready)
                    for b in range(3):
                        for h in (2 * b, 2 * b + 1):
                            for half in range(NH2):
                                last = pe.transpose(PS[0:MLA_QK, 4 + b, (h % 2) * T + half * P:(h % 2) * T + half * P + P],
                                                    rows[:, half, h * MLA_QK:(h + 1) * MLA_QK], ident[:, :])
                    last.then_inc(turned, 1)
                    me.wait(heads_copied)
                me.barrier()

                def scores(i):
                    if i >= 2:
                        me.wait(score_read)
                    q, k = items[i][0], items[i][1]
                    mm(PS[:, i % 2, 0:P], q[:, 0:P], k[:, 0:P], True, True)
                    mm(PS[:, i % 2, P:BLK], q[:, P:T], k[:, :], True, True).then_inc(score_done, 1)

                def values(i):
                    v, b, c0 = items[i][4], items[i][5], items[i][6]
                    mm(PS[:, b, c0:c0 + HD], pT[:, i % 2, 0:P], v[:, 0, :], True, True)
                    mm(PS[:, b + 1, c0:c0 + HD], pT[:, i % 2, P:2 * P], v[:, 0, :], True, False)
                    mm(PS[:, b + 1, c0:c0 + HD], pT[:, i % 2, 2 * P:BLK], v[:, 1, :], False, True).then_inc(pv_done, 1)

                for step in range(N_MAPS + 3):
                    if step < N_MAPS:
                        scores(step)
                    if step >= 3:
                        if step - 3 in GROUP_REUSES:
                            me.wait(pv_read)
                        me.wait(prob_copied)
                        values(step - 3)
                    if 2 <= step <= N_MAPS + 1:
                        me.wait(prob_ready)
                        i = step - 2
                        for c in range(3):
                            last = pe.transpose(PS[:, 2 + i % 2, c * P:(c + 1) * P], sc[:, i % 3, c * P:(c + 1) * P], ident[:, :])
                        last.then_inc(prob_turned, 1)
                me.wait(score_read, 2)
                me.wait(pv_read, 4 - len(GROUP_REUSES))
                me.barrier()

                turn(o2)
                me.wait(turn_ready)
                wide(ah, al, KT)
                me.barrier()
                turn(memx)
                me.wait(turn_ready)
                for nb in range(2):
                    cols_pair(TW)
                for nb in range(2):
                    rows_pair(KT, TW)
                me.barrier()
                turn(xn)
                me.wait(turn_ready)
                for nb in range(2):
                    cols_pair(TW)
                me.barrier()
                for step in range(CROSS_H + 1):
                    if step < CROSS_H:
                        h = step
                        if h >= 2:
                            me.wait(x_exp)
                        for half in range(NH2):
                            for q in range(2):
                                last = mm(PS[:, h % 2, half * T:(half + 1) * T], cqT[:, 2 * h + q, half * P:half * P + P], ckT[:, 2 * h + q, :], q == 0, q == 1)
                        last.then_inc(x_scored, 1)
                    if step >= 1:
                        h = step - 1
                        me.wait(x_prob)
                        for m in range(2):
                            for half in range(NH2):
                                last = pe.transpose(PS[:, 2 + h % 2, m * T + half * P:m * T + half * P + P],
                                                    csc[:, h % 2, half * T + m * P:half * T + m * P + P], ident[:, :])
                        last.then_inc(x_turned, 1)
                        me.wait(x_copied)
                        for q in range(2):
                            for m in range(2):
                                c = h * CROSS_HD + q * P
                                last = mm(PS[:, 4 + h, q * T:(q + 1) * T], cv[:, m, c:c + P], cpT[:, h % 2, m * T:(m + 1) * T], m == 0, m == 1)
                last.then_inc(x_pv, 1)
                me.wait(x_exp, 2)
                me.barrier()
                wide(ah, al, KT)
                me.barrier()
                turn(xn)
                me.wait(turn_ready)
                for f in range(2):
                    for nb in range(FF // 2 // TW):
                        cols_pair(TW)
                    me.wait(fh_done, FF // 2 // TW)
                    wide(fh, fl, FF // 2 // P, first=f == 0, final=f == 1)
                me.barrier()


        @block.scalar
        def _(act):
            def round_tile(n):
                act.wait_ge(raw_loaded[n % RAW], 16 * (n // RAW + 1))
                if n >= CNV:
                    act.wait_ge(w_used, n - CNV + 1)
                act.activation(tile_view(w_hi, n % CNV, n), tile_view(raw, n % RAW, n), ACT.Copy).then_inc(hi_ready, 1)

            me = Engine(act, act_link, act_stage, STAGES, round_tile)

            def f(out_, in_, func, **kw):
                return act.activation(out_, in_, func, **kw)

            def root():
                me.wait(root_in)
                f(stat[:, 16:18], stat[:, 14:16], ACT.Sqrt).then_inc(root_out, 1)

            def split_banks(kts, b0=0, gain=None, wait=True, k0=0):
                for b in range((kts + 1) // 2):
                    if wait:
                        me.wait(turned)
                    for kt in range(2 * b, min(2 * b + 2, kts)) if gain is not None else (2 * b,):
                        if gain is None:
                            m = min(2, kts - kt)
                            last = f(ah[:, k0 + kt:k0 + kt + m, :].rearrange("p k t -> p (k t)"), PS[:, b0 + b, 0:m * T], ACT.Copy)
                        else:
                            last = f(ah[:, k0 + kt, :], PS[:, b0 + b, (kt % 2) * T:(kt % 2 + 1) * T], ACT.Copy, scale=colA[:, gain + kt:gain + kt + 1])
                    last.then_inc(turn_hi, 1)

            def squares(src):
                for half in range(NH2):
                    last = f(PSf[:, half * D:half * D + D], src[:, half, :], ACT.Square, accum_out=stat[:, 12 + half:13 + half])
                last.then_inc(ssq_done, 1)

            me.pump(CNV - 1)
            me.wait(turned)
            split_banks(KT)
            me.barrier()

            for j, nb in enumerate(IN_ORDER):
                g = me.gemm_pair(KG, True)
                b = 2 * (g % 2)
                if nb == 4:
                    last = f(gb[:, :, :].rearrange("p k t -> p (k t)"), PSf[:, b * 512:b * 512 + 1024], ACT.Sigmoid)
                else:
                    last = f(uT[:, 4 * nb:4 * nb + 4, :].rearrange("p k t -> p (k t)"), PSf[:, b * 512:b * 512 + 1024], ACT.Copy)
                last.then_inc(gemm_free[g % 2], 1)
                if j == 1:
                    act.drain().then_inc(gate_sig, 1)
            act.drain().then_inc(mix_copied, 1)
            me.pump(me.n + CNV - 1)
            me.wait(root_in)
            f(tc[:, 0, :], tc[:, 1, :], ACT.Sqrt).then_inc(root_out, 1)
            me.wait(normed)
            for blk in range(4):
                last = f(gb[:, blk, :], gb[:, blk, :], ACT.Silu, scale=colA[:, ROW_NBG + blk:ROW_NBG + blk + 1],
                         bias=colA[:, ROW_NBB + blk:ROW_NBB + blk + 1])
            me.link(last)
            me.wait(side_conv, 2)
            f(ah[:, 0:4, :], ya[:, :, :], ACT.Copy)
            f(ah[:, 4:8, :], gb[:, :, :], ACT.Copy).then_inc(mix_hi, 1)
            me.barrier()

            def rows_split():
                me.wait(rows_ready)
                for b in range(4):
                    me.wait(turned)
                    last = f(xT[:, 2 * b:2 * b + 2, :].rearrange("p k t -> p (k t)"), PS[:, b, :], ACT.Copy)

            def router_and_experts(layer):
                me.wait(rexp_in)
                for half in range(NH2):
                    last = f(rs[:, half, 4:8], rs[:, half, 0:4], ACT.Exp, accum_out=rs[:, half, 8:9])
                last.then_inc(rexp_out, 1)
                me.wait(rexp_in)
                f(rs[:, :, 51:52], rs[:, :, 50:51], ACT.Exp).then_inc(rexp_out, 1)
                me.barrier()

                def xe_copies(*parts):
                    for part in parts:
                        me.wait((g0_done, g1_done)[part])
                        f(xe[:, 4 * part:4 * part + 4, 0:CAP], PS[:, 1 + 2 * part, 0:4 * CAP].rearrange("p (k c) -> p k c", k=4), ACT.Copy).then_inc(xe_hi[part], 1)

                xe_copies(0, 1)
                n0 = me.n
                me.pump(n0 + CNV - 1)
                f(sil[:, 0, 0:1], ident[:, 0:1], ACT.Silu)
                with act.Fori(0, NE) as e:
                    me.enter(e, once(t_done, g0_done, g1_done, fg_done, p_copied))

                    def convert(*tiles):
                        for k in tiles:
                            n = n0 + k
                            act.wait_ge(raw_loaded[n % RAW], e * 16 + 16 * (n // RAW + 1))
                            act.wait_ge(w_used, e * EXPERT_TILES + (n - CNV + 1))
                            act.activation(tile_view(w_hi, n % CNV, n0), tile_view(raw, n % RAW, n0), ACT.Copy).then_inc(hi_ready, 1)

                    def used(k):
                        act.wait_ge(w_used, e * EXPERT_TILES + (n0 + k))

                    convert(6, 7, 8)
                    used(KG)
                    f(hs[:, 0:DE], PS[:, 0, :], ACT.Copy).then_inc(hs_gate, 1)
                    convert(9, 10, 11)
                    used(2 * KG)
                    f(hs[:, DE:2 * DE], PS[:, 1, :], ACT.Copy).then_inc(hs_up, 1)
                    me.wait(fg_done)
                    f(sil[:, :, :].rearrange("p k c -> p (k c)"), PS[:, 3, 0:4 * CAP], ACT.Silu).then_inc(silu_done, 1)
                    convert(12, 13)
                    me.wait(t_done)
                    f(Pm[:, :], PS[:, 1, 0:T], ACT.Copy)
                    f(wc[:, :], PS[:, 1, bass.ds(e + T, 1)], ACT.Copy).then_inc(p_copied, 1)
                    convert(14, 15)
                    me.wait(p_copied)
                    used(2 * KG + KG // 2)
                    f(yh[:, 0:TW], PS[:, 0, :], ACT.Copy, scale=wc[:, 0:1]).then_inc(yh0, 1)
                    convert(16)
                    xe_copies(0)
                    used(3 * KG)
                    f(yh[:, TW:D], PS[:, 2, :], ACT.Copy, scale=wc[:, 0:1]).then_inc(yh1, 1)
                    xe_copies(1)
                    convert(17)
                    me.leave(NE)
                me.n = n0 + n_moe
                me.converted = me.n + CNV
                o = ov[layer]
                more = act.value_load(flag[0:1, layer:layer + 1], min_val=0, max_val=1)
                with act.If(more > 0):
                    with act.Fori(0, NE) as e:
                        for half in range(NH2):
                            act.wait_ge(o["mm"], e * OVF_LOADS + (half * OVF_HALF + 2 * KT + 1))
                            f(ovf_h[:, 0:DE], PS[:, 0, :], ACT.Silu).then_inc(o["silu"], 1)
                            act.wait_ge(o["turn"], e * 2 + (half + 1))
                            f(ovf_a[:, :, :].rearrange("p k t -> p (k t)"), PS[:, 2, :], ACT.Copy).then_inc(o["tcopy"], 1)
                me.barrier()

            for nb in range(2):
                me.wide_half(KG, False)
            root()
            rows_split()
            me.barrier()
            router_and_experts(0)
            root()
            me.wait(rows_ready)
            split_banks(KT)
            me.barrier()

            for nb in range(6):
                g = me.gemm_pair(KG, nb % 2 == 0)
                b = 2 * (g % 2)
                if nb == 0 or nb == 2:
                    dst = (qT1, kT1)[nb // 2][:, 0:4, :].rearrange("p k t -> p (k t)")
                    f(dst, PSf[:, b * 512:b * 512 + 1024], ACT.Copy).then_inc(gemm_free[g % 2], 1)
                elif nb == 4:
                    f(v1[:, :, 0:TW], PS[:, b:b + 2, :], ACT.Copy).then_inc(gemm_free[g % 2], 1)
            me.barrier()

            for step in range(SB_HEADS // SB_GROUP + 1):
                if step < SB_HEADS // SB_GROUP:
                    g = slice((step % 2) * SB_GROUP, (step % 2 + 1) * SB_GROUP)
                    act.wait_ge(sb_read, (step + 1) * SB_GROUP)
                    if step >= 2:
                        act.wait_ge(later_done, (step - 1) * SB_GROUP)
                    me.link(f(sp[:, g, :], zs[:, g, :], ACT.Abs))
                    me.link(f(sp[:, g, :], sp[:, g, :], ACT.Exp, scale=-1.0))
                    f(sp[:, g, :], sp[:, g, :], ACT.Ln, bias=1.0).then_inc(soft_abs, 1)
                if step >= 1:
                    g = slice(((step - 1) % 2) * SB_GROUP, ((step - 1) % 2 + 1) * SB_GROUP)
                    act.wait_ge(logit_ready, step)
                    f(zs[:, g, :], zs[:, g, :], ACT.Exp).then_inc(share_ready, 1)
            act.wait_ge(sb_pv, SB_HEADS)
            split_banks(KT, 4, wait=False)
            me.barrier()

            for nb in range(2):
                me.wide_half(KG, False)
            root()
            rows_split()
            me.barrier()
            router_and_experts(1)
            root()
            me.barrier()
            me.wait(sin_in)
            f(sinT[:, :, :], ang[:, :, :], ACT.Sin)
            f(cosT[:, :, :], ang[:, :, :], ACT.Sin, scale=0.5).then_inc(sin_out, 1)
            me.wait(lam_in)
            f(stat[:, 40:40 + 2 * DEPTH], stat[:, 32:32 + 2 * DEPTH], ACT.Exp).then_inc(lam_out, 1)
            me.barrier()

            for layer in range(DEPTH):
                row = layer * ROWS_LAYER
                squares(x)
                root()
                split_banks(KT, gain=row + ROW_ATTN)
                me.barrier()
                for j, (c0, width, channel_major) in enumerate(PROJ):
                    g = me.gemm_pair(KG, j % 2 == 0)
                    b = 2 * (g % 2)
                    if j == 0:
                        f(cq[:, :, :], PS[:, b:b + 2, 0:416], ACT.Copy).then_inc(gemm_free[g % 2], 1)
                    elif j == 2:
                        f(dkT[:, :, :].rearrange("p k t -> p (k t)"), PSf[:, b * 512:b * 512 + 3 * T], ACT.Copy).then_inc(gemm_free[g % 2], 1)
                    elif j == 4:
                        f(mqT[:, :, :].rearrange("p k t -> p (k t)"), PS[:, b, :], ACT.Copy)
                        f(mkT[:, :, :].rearrange("p k t -> p (k t)"), PS[:, b + 1, :], ACT.Copy).then_inc(gemm_free[g % 2], 1)
                me.barrier()
                for half in range(NH2):
                    f(PSf[:, 6 * 512 + half * 256:6 * 512 + half * 256 + QR], cq[:, half, 0:QR], ACT.Square, accum_out=stat[:, 12 + half:13 + half])
                    last = f(PSf[:, 7 * 512 + half * 256:7 * 512 + half * 256 + KVR], cq[:, half, QR:QR + KVR], ACT.Square,
                             accum_out=stat[:, 20 + half:21 + half])
                last.then_inc(ssq_done, 1)
                me.wait(root_in)
                f(stat[:, 22:26], stat[:, 26:30], ACT.Sqrt).then_inc(root_out, 1)
                split_banks(3, gain=row + ROW_Q)
                for j in range(4):
                    if j % 2 == 0:
                        g = me.gemm_pair(1, True)
                        b = 2 * (g % 2)
                        if j == 0:
                            f(qrow[:, :, 0:288], PS[:, b:b + 2, 0:288], ACT.Copy).then_inc(gemm_free[g % 2], 1)
                        else:
                            for half in range(NH2):
                                kv = PS[:, b + half, 0:384].rearrange("p (h c) -> p h c", c=P)
                                f(krow[:, half, 0:288].rearrange("p (h c) -> p h c", c=MLA_QK)[:, :, 0:MLA_NOPE], kv[:, :, 0:MLA_NOPE], ACT.Copy)
                                last = f(v2[:, half, 0:192].rearrange("p (h c) -> p h c", c=64), kv[:, :, MLA_NOPE:P], ACT.Copy)
                            last.then_inc(gemm_free[g % 2], 1)
                    else:
                        me.gemm_pair(1, False)
                act.drain().then_inc(qk_rows, 1)
                for dst in (qa, ka):
                    me.wait(turned)
                    for b in range(3):
                        last = f(dst[0:MLA_QK, 2 * b:2 * b + 2, :].rearrange("p h t -> p (h t)"), PS[0:MLA_QK, 4 + b, :], ACT.Copy)
                    last.then_inc(heads_copied, 1)
                me.barrier()
                for step in range(N_MAPS + 2):
                    if step < N_MAPS:
                        i = step % 3
                        me.wait(shifted)
                        f(sc[:, i, 0:P], sc[:, i, 0:P], ACT.Exp, bias=stat[:, NEG_MAX + 2 * i:NEG_MAX + 2 * i + 1],
                          accum_out=stat[:, SUM + 2 * i:SUM + 2 * i + 1])
                        f(sc[:, i, P:BLK], sc[:, i, P:BLK], ACT.Exp, bias=stat[:, NEG_MAX + 2 * i + 1:NEG_MAX + 2 * i + 2],
                          accum_out=stat[:, SUM + 2 * i + 1:SUM + 2 * i + 2]).then_inc(exp_done, 1)
                    if step >= 2:
                        i = (step - 2) % 2
                        me.wait(prob_turned)
                        if step - 2 >= 2:
                            me.wait(pv_done)
                        f(pT[:, i, :], PS[:, 2 + i, 0:BLK], ACT.Copy).then_inc(prob_copied, 1)
                me.wait(pv_done, 2)
                me.wait(root_in)
                f(stat[:, 124:136], stat[:, 112:124], ACT.Sqrt).then_inc(root_out, 1)
                me.barrier()
                split_banks(KT)
                for nb in range(2):
                    me.wide_half(KG, False)
                me.barrier()
                me.wait(mem_loaded, 16)
                squares(memx)
                root()
                split_banks(KT, gain=row + ROW_MEM)
                for nb in range(4):
                    g = me.gemm_pair(KG, nb % 2 == 0)
                    b = 2 * (g % 2)
                    if nb == 0:
                        f(ckT[:, 0:4, :].rearrange("p k t -> p (k t)"), PSf[:, b * 512:b * 512 + 1024], ACT.Copy).then_inc(gemm_free[g % 2], 1)
                    elif nb == 2:
                        f(cv[:, :, 0:TW], PS[:, b:b + 2, :], ACT.Copy).then_inc(gemm_free[g % 2], 1)
                me.barrier()
                squares(x)
                root()
                split_banks(KT, gain=row + ROW_CROSS)
                for nb in range(2):
                    g = me.gemm_pair(KG, nb == 0)
                    b = 2 * (g % 2)
                    if nb == 0:
                        f(cqT[:, 0:4, :].rearrange("p k t -> p (k t)"), PSf[:, b * 512:b * 512 + 1024], ACT.Copy).then_inc(gemm_free[g % 2], 1)
                me.barrier()
                for step in range(CROSS_H + 1):
                    if step < CROSS_H:
                        i = step % 2
                        me.wait(x_max)
                        for half in range(NH2):
                            last = f(csc[:, i, half * T:(half + 1) * T], PS[:, i, half * T:(half + 1) * T], ACT.Exp, scale=CROSS_HD ** -0.5,
                                     bias=stat[:, 52 + 2 * i + half:53 + 2 * i + half], accum_out=stat[:, 56 + 2 * i + half:57 + 2 * i + half])
                        last.then_inc(x_exp, 1)
                    if step >= 1:
                        i = (step - 1) % 2
                        me.wait(x_turned)
                        f(cpT[:, i, :], PS[:, 2 + i, :], ACT.Copy).then_inc(x_copied, 1)
                me.wait(x_pv)
                split_banks(KT, 4, wait=False)
                me.barrier()
                for nb in range(2):
                    me.wide_half(KG, False)
                me.barrier()
                squares(x)
                root()
                split_banks(KT, gain=row + ROW_MLP)
                for part in range(2):
                    for nb in range(FF // 2 // TW):
                        g = me.gemm_pair(KG, True)
                        b = 2 * (g % 2)
                        me.link(f(rT[:, 0, :], PSf[:, b * 512:b * 512 + 1024], ACT.Relu))
                        act.drain().then_inc(gemm_free[g % 2], 1)
                        if nb + part >= 1:
                            me.wait(fh_done)
                        me.link(f(rT[:, 1, :], rT[:, 0, :], ACT.Square))
                        f(fh[:, 4 * nb:4 * nb + 4, :].rearrange("p k t -> p (k t)"), rT[:, 1, :], ACT.Copy).then_inc(sq_in, 1)
                    for nb in range(2):
                        me.wide_half(2 * KG, False)
                me.wait(fh_done)
                me.barrier()
            squares(x)
            root()

        @block.vector
        def _(dve):
            def split_tile(n):
                dve.wait_ge(hi_ready, n + 1)
                dve.tensor_tensor(tile_view(w_lo, n % CNV, n), tile_view(raw, n % RAW, n), tile_view(w_hi, n % CNV, n),
                                  ALU.subtract).then_inc(lo_ready, 1)

            me = Engine(dve, dve_link, dve_stage, STAGES, split_tile)
            tt, ts, stt = dve.tensor_tensor, dve.tensor_scalar, dve.scalar_tensor_tensor

            def root():
                dve.drain().then_inc(root_in, 1)
                me.wait(root_out)
                me.link(dve.reciprocal(stat[:, 18:20], stat[:, 16:18]))

            def split_banks(kts, b0=0, gain=None, k0=0, signal=False):
                for b in range((kts + 1) // 2):
                    me.wait(turn_hi)
                    for kt in range(2 * b, min(2 * b + 2, kts)) if gain is not None else (2 * b,):
                        if gain is None:
                            m = min(2, kts - kt)
                            last = tt(al[:, k0 + kt:k0 + kt + m, :].rearrange("p k t -> p (k t)"), PS[:, b0 + b, 0:m * T],
                                      ah[:, k0 + kt:k0 + kt + m, :].rearrange("p k t -> p (k t)"), ALU.subtract)
                        else:
                            last = stt(out=al[:, k0 + kt, :], in0=PS[:, b0 + b, (kt % 2) * T:(kt % 2 + 1) * T],
                                       scalar=colA[:, gain + kt:gain + kt + 1], in1=ah[:, k0 + kt, :], op0=ALU.mult, op1=ALU.subtract)
                if signal:
                    last.then_inc(turn_ready, 1)

            def add_wide(factor):
                for nb in range(2):
                    me.wide_half(add_wide.tiles, True)
                    for half in range(NH2):
                        last = stt(out=x[:, half, nb * TW:(nb + 1) * TW], in0=x[:, half, nb * TW:(nb + 1) * TW], scalar=factor,
                                   in1=PS[:, 4 + 2 * nb + half, :], op0=ALU.mult, op1=ALU.add)
                me.link(last)
            add_wide.tiles = KG

            def layer_norm():
                for half in range(NH2):
                    for c in range(2):
                        last = dve.bn_stats(stat[:, 64 + 12 * half + 6 * c:70 + 12 * half + 6 * c], x[:, half, c * TW:(c + 1) * TW])
                me.link(last)
                for half in range(NH2):
                    last = dve.bn_aggr(stat[:, 88 + 2 * half:90 + 2 * half], stat[:, 64 + 12 * half:76 + 12 * half])
                me.link(last)
                for half in range(NH2):
                    last = ts(stat[:, 14 + half:15 + half], stat[:, 89 + 2 * half:90 + 2 * half], LN_EPS, None, ALU.add)
                me.link(last)
                dve.drain().then_inc(root_in, 1)
                me.wait(ln_loaded, 32)
                for half in range(NH2):
                    last = stt(out=x[:, half, :], in0=x[:, half, :], scalar=stat[:, 88 + 2 * half:89 + 2 * half], in1=lnp[:, 0, :],
                               op0=ALU.subtract, op1=ALU.mult)
                me.link(last)
                me.wait(root_out)
                me.link(dve.reciprocal(stat[:, 18:20], stat[:, 16:18]))
                for half in range(NH2):
                    last = stt(out=x[:, half, :], in0=x[:, half, :], scalar=stat[:, 18 + half:19 + half], in1=lnp[:, 1, :],
                               op0=ALU.mult, op1=ALU.add)
                me.link(last)
                dve.drain().then_inc(ln_used, 1)

            def rms_rows(src, dst):
                me.wait(ssq_done)
                me.link(ts(stat[:, 14:16], stat[:, 12:14], 1.0 / D, RMS_EPS, ALU.mult, ALU.add))
                root()
                for half in range(NH2):
                    last = ts(dst[:, half, :], src[:, half, :], stat[:, 18 + half:19 + half], None, ALU.mult)
                return last

            me.pump(CNV - 1)
            me.wait(turned)
            tt_copy = dve.tensor_copy
            tt_copy(colA[:, :], PS[:, 7, 0:P])
            tt_copy(colB[:, :], PS[:, 7, P:P + 4 * CONV_B])
            split_banks(KT)
            me.barrier()

            dve.memset(pa[:, :, 0:CONV_A - 1], 0.0)
            dve.memset(pb[:, :, 0:CONV_B - 1], 0.0)
            me.gemm_pair(KG, False)
            me.gemm_pair(KG, False)
            me.wait(gate_sig)
            me.link(tt(pb[:, :, CONV_B - 1:], uT[:, 12:16, :], gb[:, :, :], ALU.mult))
            dve.drain().then_inc(conv_in, 1)
            mine = [c for c in range(4) if c != SIDE_BLOCK]
            tiles_ahead = me.n + 3 * KG + CNV - 1
            for j in range(CONV_B):
                for c in mine:
                    w = colB[:, 4 * j + c:4 * j + c + 1]
                    if j == 0:
                        last = ts(gb[:, c, :], pb[:, c, 0:T], w, colA[:, ROW_BIAS + c:ROW_BIAS + c + 1], ALU.mult, ALU.add)
                    else:
                        last = stt(out=gb[:, c, :], in0=pb[:, c, j:j + T], scalar=w, in1=gb[:, c, :], op0=ALU.mult, op1=ALU.add)
                me.link(last)
                if j % 2 == 1 and me.converted <= tiles_ahead:
                    me.pump(me.converted)
            dve.drain().then_inc(conv_b_done, 1)
            for _ in range(3):
                me.gemm_pair(KG, False)
            me.pump(me.n + CNV - 1)
            me.wait(side_conv)
            me.wait(chan_mean)
            for blk in range(4):
                last = stt(out=gb[:, blk, :], in0=PS[:, 4, 0:T], scalar=-1.0 / 512, in1=gb[:, blk, :], op0=ALU.mult, op1=ALU.add)
            me.link(last)
            tt(tc[:, :, :], gb[:, :, :], gb[:, :, :], ALU.mult).then_inc(sq_ready, 1)
            me.wait(chan_mean)
            me.link(ts(tc[:, 1, :], PS[:, 5, 0:T], 1.0 / 512, LN_EPS, ALU.mult, ALU.add))
            dve.drain().then_inc(root_in, 1)
            me.wait(root_out)
            me.link(dve.reciprocal(tc[:, 2, :], tc[:, 0, :]))
            for blk in range(4):
                last = tt(gb[:, blk, :], gb[:, blk, :], tc[:, 2, :], ALU.mult)
            last.then_inc(normed, 1)
            me.wait(mix_hi)
            me.wait(side_conv)
            tt(al[:, 0:4, :], ya[:, :, :], ah[:, 0:4, :], ALU.subtract)
            tt(al[:, 4:8, :], gb[:, :, :], ah[:, 4:8, :], ALU.subtract)
            me.barrier()

            def rows_split():
                dve.drain().then_inc(rows_ready, 1)

            def router_and_experts(layer):
                dve.memset(Pm[:, :].bitcast(F32), 0.0)
                dve.memset(yh[:, :].bitcast(F32), 0.0)
                dve.memset(yl[:, :].bitcast(F32), 0.0)
                me.wait(logits_done)
                for half in range(NH2):
                    last = tt(lg[:, half, :], PS[:, 0, half * 64:half * 64 + NR], rbias[:, :], ALU.add)
                me.link(last)
                GD, GO, ESEL, KEY, O1, O2 = slice(0, 4), slice(12, 16), slice(16, 24), slice(24, 32), slice(32, 40), slice(40, 48)
                def both(op):
                    for half in range(NH2):
                        last = op(rs[:, half, :], lg[:, half, 0:NG], lg[:, half, NG:NR])
                    me.link(last)

                def reduce_max(c, val):
                    both(lambda r, g4, e32: dve.tensor_reduce(r[:, c:c + 1], val(r, g4), AX, ALU.max))

                def first_max(oh, val, top, n):
                    both(lambda r, g4, e32: stt(out=r[:, KEY][:, 0:n], in0=val(r, g4), scalar=r[:, top:top + 1], in1=prio[:, EPG - n:EPG],
                                                op0=ALU.is_equal, op1=ALU.mult))
                    reduce_max(49, lambda r, g4: r[:, KEY][:, 0:n])
                    both(lambda r, g4, e32: ts(r[:, oh], r[:, KEY][:, 0:n], r[:, 49:50], None, ALU.is_equal))

                groups, chosen = (lambda r, g4: g4), (lambda r, g4: r[:, ESEL])
                reduce_max(9, groups)
                both(lambda r, g4, e32: ts(r[:, GD], g4, r[:, 9:10], None, ALU.subtract))
                dve.drain().then_inc(rexp_in, 1)
                first_max(GO, groups, 9, NG)
                both(lambda r, g4, e32: ts(r[:, ESEL], e32[:, 0:EPG], r[:, 12:13], None, ALU.mult))
                for j in range(1, NG):
                    both(lambda r, g4, e32: stt(out=r[:, ESEL], in0=e32[:, j * EPG:(j + 1) * EPG], scalar=r[:, 12 + j:13 + j], in1=r[:, ESEL],
                                                op0=ALU.mult, op1=ALU.add))
                reduce_max(10, chosen)
                first_max(O1, chosen, 10, EPG)
                both(lambda r, g4, e32: stt(out=r[:, ESEL], in0=r[:, O1], scalar=NEG, in1=r[:, ESEL], op0=ALU.mult, op1=ALU.add))
                reduce_max(11, chosen)
                first_max(O2, chosen, 11, EPG)
                both(lambda r, g4, e32: tt(r[:, 50:51], r[:, 11:12], r[:, 10:11], ALU.subtract))
                dve.drain().then_inc(rexp_in, 1)
                me.wait(rexp_out, 2)
                for half in range(NH2):
                    r = rs[:, half, :]
                    ts(r[:, 52:53], r[:, 51:52], 1.0, None, ALU.add)
                    last = dve.reciprocal(r[:, 53:54], r[:, 8:9])
                me.link(last)
                me.link(dve.reciprocal(rs[:, :, 54:55], rs[:, :, 52:53]))
                me.link(tt(rs[:, :, 55:56], rs[:, :, 54:55], rs[:, :, 53:54], ALU.mult))
                me.link(tt(rs[:, :, 56:57], rs[:, :, 55:56], rs[:, :, 51:52], ALU.mult))
                both(lambda r, g4, e32: tt(r[:, KEY], r[:, O1], r[:, O2], ALU.add))
                both(lambda r, g4, e32: ts(r[:, ESEL], r[:, O1], r[:, 55:56], None, ALU.mult))
                both(lambda r, g4, e32: stt(out=r[:, ESEL], in0=r[:, O2], scalar=r[:, 56:57], in1=r[:, ESEL], op0=ALU.mult, op1=ALU.add))
                for half in range(NH2):
                    r = rs[:, half, :]
                    for j in range(NG):
                        ts(Mt[:, half, j * EPG:(j + 1) * EPG], r[:, KEY], r[:, 12 + j:13 + j], None, ALU.mult)
                        last = ts(Wt[:, half, j * EPG:(j + 1) * EPG], r[:, ESEL], r[:, 12 + j:13 + j], None, ALU.mult)
                me.link(last)
                dve.drain().then_inc(member_ready, 1)
                me.wait(rank_done)
                dve.memset(slot[:, :, :], 0.0)
                me.link(dve.tensor_reduce(stat[:, 100:101], PS[:, 1, 2 * NE:3 * NE], AX, ALU.max))
                ts(flag[:, layer:layer + 1], stat[:, 100:101], float(CAP), None, ALU.is_gt)
                me.link(stt(out=slot[:, :, 0:NE], in0=PS[:, 1, 0:2 * NE].rearrange("p (h e) -> p h e", e=NE), scalar=1.0, in1=Mt[:, :, :],
                            op0=ALU.add, op1=ALU.mult))
                me.link(ts(slot[:, :, :], slot[:, :, :], -1.0, None, ALU.add))
                me.link(stt(out=ovf_wt[:, :, :], in0=slot[:, :, 0:NE], scalar=float(CAP), in1=Wt[:, :, :], op0=ALU.is_ge, op1=ALU.mult))
                me.barrier()

                dve.drain().then_inc(yl0, 1)
                dve.drain().then_inc(yl1, 1)
                def one_hot(column):
                    for half in range(NH2):
                        last = ts(SS[:, half, :], slot_no[:, :], slot[:, half, column], None, ALU.is_equal)
                    last.then_inc(ss_ready, 1)

                def xe_split(*parts):
                    for part in parts:
                        me.wait(xe_hi[part])
                        e_hi, e_lo = xe[:, 4 * part:4 * part + 4, 0:CAP], xe[:, 4 * part:4 * part + 4, CAP:2 * CAP]
                        tt(e_lo, PS[:, 1 + 2 * part, 0:4 * CAP].rearrange("p (k c) -> p k c", k=4), e_hi, ALU.subtract).then_inc((xe0, xe1)[part], 1)

                one_hot(slice(0, 1))
                n0 = me.n
                xe_split(0, 1)
                me.pump(n0 + CNV - 1)
                with dve.Fori(0, NE) as e:
                    me.enter(e, {**once(xe_hi[0], xe_hi[1], t_done, f_done, silu_done, yh0, yh1), dve_link.name: 1, side_split.name: len(SIDE)})

                    def convert(*tiles):
                        for k in tiles:
                            if k in SIDE:
                                continue
                            n = n0 + k
                            done = 1
                            if k - 1 in SIDE:
                                me.wait(side_split)
                                done = 2
                            dve.wait_ge(hi_ready, e * EXPERT_TILES + (n + 1))
                            tt(tile_view(w_lo, n % CNV, n0), tile_view(raw, n % RAW, n0), tile_view(w_hi, n % CNV, n0), ALU.subtract).then_inc(lo_ready, done)

                    convert(6, 7, 8, 9)
                    me.wait(f_done)
                    me.wait(silu_done)
                    me.link(tt(af[:, :, :].rearrange("p k c -> p (k c)"), sil[:, :, :].rearrange("p k c -> p (k c)"), PS[:, 2, 0:4 * CAP], ALU.mult))
                    tt_copy(aT[:, :, 0:CAP], af[:, :, :])
                    dve.drain().then_inc(dve_half, 1)
                    dve.wait_ge(dve_half, e + (layer * NE + 1))
                    tt(aT[:, :, CAP:2 * CAP], af[:, :, :], aT[:, :, 0:CAP], ALU.subtract).then_inc(act_ready, 1)
                    convert(10, 11, 12, 13)
                    me.wait(t_done)
                    one_hot(bass.ds(e + 1, 1))
                    convert(14, 15)
                    me.wait(yh0)
                    stt(out=yl[:, 0:TW], in0=PS[:, 0, :], scalar=wc[:, 0:1], in1=yh[:, 0:TW], op0=ALU.mult, op1=ALU.subtract).then_inc(yl0, 1)
                    convert(16)
                    xe_split(0, 1)
                    me.wait(yh1)
                    stt(out=yl[:, TW:D], in0=PS[:, 2, :], scalar=wc[:, 0:1], in1=yh[:, TW:D], op0=ALU.mult, op1=ALU.subtract).then_inc(yl1, 1)
                    convert(17)
                    me.leave(NE)
                me.n = n0 + n_moe
                me.converted = me.n + CNV
                me.wait(moe_done)
                for nb in range(2):
                    for half in range(NH2):
                        last = stt(out=x[:, half, nb * TW:(nb + 1) * TW], in0=x[:, half, nb * TW:(nb + 1) * TW], scalar=ALPHA,
                                   in1=PS[:, 4 + 2 * nb + half, :], op0=ALU.mult, op1=ALU.add)
                me.link(last)
                o = ov[layer]
                more = dve.value_load(flag[0:1, layer:layer + 1], min_val=0, max_val=1)
                with dve.If(more > 0):
                    dve.drain().then_inc(o["mm"], 1)
                    dve.drain().then_inc(o["add"], 1)
                    with dve.Fori(0, NE) as e:
                        for half in range(NH2):
                            dve.wait_ge(o["mm"], e * OVF_LOADS + (half * OVF_HALF + 2 * KT + 1))
                            dve.wait_ge(o["silu"], e * 2 + (half + 1))
                            tt(ovf_h[:, DE:2 * DE], ovf_h[:, 0:DE], PS[:, 1, :], ALU.mult).then_inc(o["link"], 1)
                            dve.wait_ge(o["link"], e * 2 + (half + 1))
                            ts(ovf_h[:, 0:DE], ovf_h[:, DE:2 * DE], ovf_wt[:, half, bass.ds(e, 1)], None, ALU.mult).then_inc(o["act"], 1)
                            dve.wait_ge(o["mm"], e * OVF_LOADS + ((half + 1) * OVF_HALF + 1))
                            for nb in range(2):
                                last = tt(x[:, half, nb * TW:(nb + 1) * TW], x[:, half, nb * TW:(nb + 1) * TW], PS[:, nb, :], ALU.add)
                            last.then_inc(o["add"], 1)
                            dve.wait_ge(o["add"], e * 2 + (half + 2))
                me.barrier()

            add_wide(ALPHA)
            layer_norm()
            rows_split()
            me.barrier()
            router_and_experts(0)
            layer_norm()
            dve.drain().then_inc(rows_ready, 1)
            split_banks(KT)
            me.barrier()

            for nb in range(6):
                g = me.gemm_pair(KG, nb % 2 == 1)
                b = 2 * (g % 2)
                if nb == 1 or nb == 3:
                    dst = (qT1, kT1)[nb // 2][:, 4:8, :].rearrange("p k t -> p (k t)")
                    tt_copy(dst, PSf[:, b * 512:b * 512 + 1024]).then_inc(gemm_free[g % 2], 1)
                elif nb == 5:
                    tt_copy(v1[:, :, TW:D], PS[:, b:b + 2, :]).then_inc(gemm_free[g % 2], 1)
            me.barrier()

            keep_g = keep_t[:, :].unsqueeze(1).broadcast_to([P, SB_GROUP, P])
            drop_g = drop_t[:, :].unsqueeze(1).broadcast_to([P, SB_GROUP, P])
            for step in range(SB_HEADS // SB_GROUP + 1):
                if step < SB_HEADS // SB_GROUP:
                    if step >= 2:
                        dve.wait_ge(sb_pv, (step - 1) * SB_GROUP)
                    for h in range(step * SB_GROUP, (step + 1) * SB_GROUP):
                        dve.wait_ge(sb_scored, h + 1)
                        ts(zs[:, h % (2 * SB_GROUP), :], PS[:, h % 2, 0:BLK], HD ** -0.5, None, ALU.mult).then_inc(sb_read, 1)
                if step >= 1:
                    for h in range((step - 1) * SB_GROUP, step * SB_GROUP):
                        z = zs[:, h % (2 * SB_GROUP), :]
                        dve.wait_ge(later_done, h + 1)
                        tt(z, z, PS[:, 2 + h % 2, 0:BLK], ALU.subtract).then_inc(later_read, 1)
                    dve.wait_ge(later_read, step * SB_GROUP)
                    g = slice(((step - 1) % 2) * SB_GROUP, ((step - 1) % 2 + 1) * SB_GROUP)
                    tt(zs[:, g, 0:P], zs[:, g, 0:P], drop_g, ALU.add)
                    tt(zs[:, g, T:BLK], zs[:, g, T:BLK], drop_g, ALU.add).then_inc(logit_ready, 1)
                if step < SB_HEADS // SB_GROUP:
                    g = slice((step % 2) * SB_GROUP, (step % 2 + 1) * SB_GROUP)
                    dve.wait_ge(sb_read, (step + 1) * SB_GROUP)
                    dve.wait_ge(soft_abs, step + 1)
                    me.link(stt(out=sp[:, g, :], in0=zs[:, g, :], scalar=0.0, in1=sp[:, g, :], op0=ALU.max, op1=ALU.add))
                    tt(sp[:, g, 0:P], sp[:, g, 0:P], keep_g, ALU.mult)
                    tt(sp[:, g, T:BLK], sp[:, g, T:BLK], keep_g, ALU.mult).then_inc(soft_ready, 1)
            split_banks(KT, 4)
            me.barrier()

            add_wide(ALPHA)
            layer_norm()
            rows_split()
            me.barrier()
            router_and_experts(1)
            layer_norm()
            me.barrier()

            me.wait(pos_loaded, 32)
            tt_copy(posk[:, :], posi[:, :])
            me.link(tt_copy(posq[:, :], posqi[:, :]))
            for half in range(NH2):
                last = ts(ang[:, half, :], inv_freq[:, :], posq[:, half:half + 1], None, ALU.mult)
            me.link(last)
            MAGIC = 1.5 * 2.0 ** 23
            me.link(ts(angk[:, :, :], ang[:, :, :], 1.0 / (2 * math.pi), None, ALU.mult))
            me.link(ts(angk[:, :, :], angk[:, :, :], MAGIC, None, ALU.add))
            me.link(ts(angk[:, :, :], angk[:, :, :], -MAGIC, None, ALU.add))
            for part in TWO_PI_PARTS:
                me.link(stt(out=ang[:, :, :], in0=angk[:, :, :], scalar=-part, in1=ang[:, :, :], op0=ALU.mult, op1=ALU.add))
            me.link(ts(ang[:, :, :], ang[:, :, :], 3.1415925, -3.1415925, ALU.min, ALU.max))
            dve.drain().then_inc(sin_in, 1)
            for half, c0, w in ((0, 0, P), (1, P, T)):
                me.link(ts(dist[:, c0:c0 + w], posk[:, 0:w], posq[:, half:half + 1], None, ALU.subtract))
            me.link(stt(out=dist[:, :], in0=dist[:, :], scalar=-1.0, in1=dist[:, :], op0=ALU.mult, op1=ALU.max))
            for m in range(N_ALIBI):
                scale = (DIFF_HD if m < DIFF_H else HD) ** -0.5
                stt(out=alibi[:, m, :], in0=dist[:, :], scalar=-SLOPES[m] / scale, in1=causal[:, :], op0=ALU.mult, op1=ALU.add)
            for l in range(DEPTH):
                for j in range(2):
                    c = 32 + 2 * l + j
                    prod = lam_rows[:, 2 * j * DEPTH + l, :]
                    me.link(tt(prod, prod, lam_rows[:, (2 * j + 1) * DEPTH + l, :], ALU.mult))
                    me.link(dve.tensor_reduce(stat[:, c:c + 1], prod, AX, ALU.add))
            dve.drain().then_inc(lam_in, 1)
            me.wait(sin_out)
            me.link(tt(cosT[:, :, :], cosT[:, :, :], cosT[:, :, :], ALU.mult))
            me.link(ts(cosT[:, :, :], cosT[:, :, :], -2.0, 1.0, ALU.mult, ALU.add))
            me.wait(lam_out)
            for l in range(DEPTH):
                me.link(tt(stat[:, 44 + l:45 + l], stat[:, 41 + 2 * l:42 + 2 * l], stat[:, 40 + 2 * l:41 + 2 * l], ALU.subtract))
                me.link(ts(stat[:, 44 + l:45 + l], stat[:, 44 + l:45 + l], -LAM_INIT[l], None, ALU.add))
            me.barrier()

            for layer in range(DEPTH):
                row = layer * ROWS_LAYER
                rms_rows(x, xn).then_inc(rows_ready, 1)
                split_banks(KT, gain=row + ROW_ATTN)
                me.barrier()
                for j, (c0, width, channel_major) in enumerate(PROJ):
                    g = me.gemm_pair(KG, j % 2 == 1)
                    b = 2 * (g % 2)
                    if j == 1:
                        tt_copy(dqT[:, :, :].rearrange("p k t -> p (k t)"), PSf[:, b * 512:b * 512 + 3 * T]).then_inc(gemm_free[g % 2], 1)
                    elif j == 3:
                        tt_copy(dv[:, :, :], PS[:, b:b + 2, 0:384]).then_inc(gemm_free[g % 2], 1)
                    elif j == 5:
                        tt_copy(mv[:, :, :], PS[:, b:b + 2, 0:256]).then_inc(gemm_free[g % 2], 1)
                me.barrier()
                me.wait(ssq_done)
                ts(stat[:, 26:28], stat[:, 12:14], 1.0 / QR, RMS_EPS, ALU.mult, ALU.add)
                me.link(ts(stat[:, 28:30], stat[:, 20:22], 1.0 / KVR, RMS_EPS, ALU.mult, ALU.add))
                dve.drain().then_inc(root_in, 1)
                me.wait(root_out)
                me.link(dve.reciprocal(stat[:, 104:108], stat[:, 22:26]))
                for half in range(NH2):
                    ts(cq[:, half, 0:QR], cq[:, half, 0:QR], stat[:, 104 + half:105 + half], None, ALU.mult)
                    last = ts(cq[:, half, QR:QR + KVR], cq[:, half, QR:QR + KVR], stat[:, 106 + half:107 + half], None, ALU.mult)
                last.then_inc(rows_ready, 1)
                split_banks(3, gain=row + ROW_Q, signal=True)
                for j in range(4):
                    g = me.gemm_pair(1, j % 2 == 1)
                    b = 2 * (g % 2)
                    if j == 1:
                        tt_copy(qrow[:, :, 288:576], PS[:, b:b + 2, 0:288]).then_inc(gemm_free[g % 2], 1)
                    elif j == 3:
                        for half in range(NH2):
                            kv = PS[:, b + half, 0:384].rearrange("p (h c) -> p h c", c=P)
                            tt_copy(krow[:, half, 288:576].rearrange("p (h c) -> p h c", c=MLA_QK)[:, :, 0:MLA_NOPE], kv[:, :, 0:MLA_NOPE])
                            last = tt_copy(v2[:, half, 192:384].rearrange("p (h c) -> p h c", c=64), kv[:, :, MLA_NOPE:P])
                        last.then_inc(gemm_free[g % 2], 1)
                HR = MLA_ROPE // 2
                tmp = sc[:, 0, 0:6 * HR]
                tmp2 = sc[:, 1, 0:6 * HR]

                def rotate(x1, x2, cos, sin, t1, t2):
                    tt(t1, x1, sin, ALU.mult)
                    me.link(tt(t2, x2, sin, ALU.mult))
                    tt(x1, x1, cos, ALU.mult)
                    me.link(tt(x2, x2, cos, ALU.mult))
                    tt(x1, x1, t2, ALU.subtract)
                    me.link(tt(x2, x2, t1, ALU.add))

                me.wait(qk_rows)
                for half in range(NH2):
                    q3 = qrow[:, half, :].rearrange("p (h c) -> p h c", c=MLA_QK)
                    t1 = tmp.rearrange("p (h c) -> p h c", c=HR)
                    t2 = tmp2.rearrange("p (h c) -> p h c", c=HR)
                    cos = cosT[:, half, :].unsqueeze(1).broadcast_to([P, MLA_H, HR])
                    sin = sinT[:, half, :].unsqueeze(1).broadcast_to([P, MLA_H, HR])
                    rotate(q3[:, :, MLA_NOPE:MLA_NOPE + HR], q3[:, :, MLA_NOPE + HR:MLA_QK], cos, sin, t1, t2)
                dve.drain().then_inc(rows_ready, 1)
                for half in range(NH2):
                    kr = cq[:, half, QR + KVR:QR + KVR + MLA_ROPE]
                    rotate(kr[:, 0:HR], kr[:, HR:2 * HR], cosT[:, half, :], sinT[:, half, :], tmp[:, 0:HR], tmp2[:, 0:HR])
                    k3 = krow[:, half, :].rearrange("p (h c) -> p h c", c=MLA_QK)
                    for h in range(MLA_H):
                        last = tt_copy(k3[:, h, MLA_NOPE:MLA_QK], kr)
                last.then_inc(rows_ready, 1)
                me.barrier()

                def read_group(group):
                    b = 4 + 2 * (group % 2)
                    if group == 0:
                        last = tt_copy(o2[:, :, 0:384], PS[:, b:b + 2, 0:384])
                    elif group == 1:
                        last = tt_copy(o3[:, :, :], PS[:, b:b + 2, 0:384])
                    elif group == 2:
                        last = stt(out=o3[:, :, :], in0=PS[:, b:b + 2, 0:384], scalar=stat[:, 44 + layer:45 + layer], in1=o3[:, :, :],
                                   op0=ALU.mult, op1=ALU.add)
                    else:
                        last = tt_copy(o2[:, :, 768:1024], PS[:, b:b + 2, 0:256])
                    last.then_inc(pv_read, 1)

                pv_seen = layer * N_MAPS
                for step in range(N_MAPS + 1):
                    if step < N_MAPS:
                        i = step % 3
                        me.wait(score_done)
                        if step >= 3:
                            me.wait(prob_turned)
                        bias, scale = items[step][2], items[step][3]
                        for blk, c0, w in ((0, 0, P), (1, P, T)):
                            last = dve.tensor_tensor_reduce(sc[:, i, c0:c0 + w], PS[:, step % 2, c0:c0 + w], bias[:, c0:c0 + w], scale, -3e38,
                                                            ALU.add, ALU.max, stat[:, MAX + 2 * i + blk:MAX + 2 * i + blk + 1])
                        me.link(last)
                        dve.drain().then_inc(score_read, 1)
                        ts(stat[:, NEG_MAX + 2 * i:NEG_MAX + 2 * i + 2], stat[:, MAX + 2 * i:MAX + 2 * i + 2], -1.0, None, ALU.mult).then_inc(shifted, 1)
                    if step >= 1:
                        i = (step - 1) % 3
                        me.wait(exp_done)
                        me.link(dve.reciprocal(stat[:, SHARE + 2 * i:SHARE + 2 * i + 2], stat[:, SUM + 2 * i:SUM + 2 * i + 2]))
                        ts(sc[:, i, 0:P], sc[:, i, 0:P], stat[:, SHARE + 2 * i:SHARE + 2 * i + 1], None, ALU.mult)
                        ts(sc[:, i, P:BLK], sc[:, i, P:BLK], stat[:, SHARE + 2 * i + 1:SHARE + 2 * i + 2], None, ALU.mult).then_inc(prob_ready, 1)
                    for group, end in enumerate(GROUP_ENDS):
                        if step == min(end + 4, N_MAPS):
                            dve.wait_ge(pv_done, pv_seen + end)
                            read_group(group)
                me.wait(prob_turned, 3)
                me.wait(pv_read, 4)
                sq = o2[:, :, 384:768]
                me.link(tt(sq, o3[:, :, :], o3[:, :, :], ALU.mult))
                me.link(dve.tensor_reduce(stat[:, 112:124], sq.rearrange("p h (n c) -> p h n c", c=HD), AX, ALU.add))
                me.link(ts(stat[:, 112:124], stat[:, 112:124], 1.0 / HD, RMS_EPS, ALU.mult, ALU.add))
                dve.drain().then_inc(root_in, 1)
                me.wait(root_out)
                me.link(dve.reciprocal(stat[:, 112:124], stat[:, 124:136]))
                for half in range(NH2):
                    for h in range(DIFF_H):
                        c = 112 + half * DIFF_H + h
                        last = stt(out=o2[:, half, 384 + h * HD:384 + (h + 1) * HD], in0=o3[:, half, h * HD:(h + 1) * HD], scalar=stat[:, c:c + 1],
                                   in1=subn[:, layer, :], op0=ALU.mult, op1=ALU.mult)
                me.link(last)
                me.link(ts(o2[:, :, 384:768], o2[:, :, 384:768], 1.0 - LAM_INIT[layer], None, ALU.mult))
                me.barrier()
                dve.drain().then_inc(rows_ready, 1)
                split_banks(KT, signal=True)
                add_wide(1.0)
                me.barrier()
                rms_rows(memx, memx).then_inc(rows_ready, 1)
                split_banks(KT, gain=row + ROW_MEM, signal=True)
                for nb in range(4):
                    g = me.gemm_pair(KG, nb % 2 == 1)
                    b = 2 * (g % 2)
                    if nb == 1:
                        tt_copy(ckT[:, 4:8, :].rearrange("p k t -> p (k t)"), PSf[:, b * 512:b * 512 + 1024]).then_inc(gemm_free[g % 2], 1)
                    elif nb == 3:
                        tt_copy(cv[:, :, TW:D], PS[:, b:b + 2, :]).then_inc(gemm_free[g % 2], 1)
                me.barrier()
                rms_rows(x, xn).then_inc(rows_ready, 1)
                split_banks(KT, gain=row + ROW_CROSS, signal=True)
                for nb in range(2):
                    g = me.gemm_pair(KG, nb == 1)
                    b = 2 * (g % 2)
                    if nb == 1:
                        tt_copy(cqT[:, 4:8, :].rearrange("p k t -> p (k t)"), PSf[:, b * 512:b * 512 + 1024]).then_inc(gemm_free[g % 2], 1)
                me.barrier()
                for step in range(CROSS_H + 1):
                    if step < CROSS_H:
                        i = step % 2
                        me.wait(x_scored)
                        me.link(dve.tensor_reduce(stat[:, 60 + 2 * i:62 + 2 * i], PS[:, i, :].rearrange("p (b m) -> p b m", b=2), AX, ALU.max))
                        ts(stat[:, 52 + 2 * i:54 + 2 * i], stat[:, 60 + 2 * i:62 + 2 * i], -CROSS_HD ** -0.5, None, ALU.mult).then_inc(x_max, 1)
                    if step >= 1:
                        i = (step - 1) % 2
                        me.wait(x_exp)
                        me.link(dve.reciprocal(stat[:, 108 + 2 * i:110 + 2 * i], stat[:, 56 + 2 * i:58 + 2 * i]))
                        ts(csc[:, i, 0:T], csc[:, i, 0:T], stat[:, 108 + 2 * i:109 + 2 * i], None, ALU.mult)
                        ts(csc[:, i, T:2 * T], csc[:, i, T:2 * T], stat[:, 109 + 2 * i:110 + 2 * i], None, ALU.mult).then_inc(x_prob, 1)
                split_banks(KT, 4)
                me.barrier()
                add_wide(1.0)
                me.barrier()
                rms_rows(x, xn).then_inc(rows_ready, 1)
                split_banks(KT, gain=row + ROW_MLP, signal=True)
                for part in range(2):
                    for nb in range(FF // 2 // TW):
                        me.gemm_pair(KG, False)
                        me.wait(sq_in)
                        tt(fl[:, 4 * nb:4 * nb + 4, :].rearrange("p k t -> p (k t)"), rT[:, 1, :],
                           fh[:, 4 * nb:4 * nb + 4, :].rearrange("p k t -> p (k t)"), ALU.subtract).then_inc(fh_done, 1)
                    if part == 0:
                        for nb in range(2):
                            me.wide_half(2 * KG, False)
                add_wide.tiles = 2 * KG
                add_wide(1.0)
                add_wide.tiles = KG
                me.barrier()
            me.link(rms_rows(x, x))
            me.wait(ln_loaded, 16)
            for half in range(NH2):
                last = tt(x[:, half, :], x[:, half, :], lnp[:, 0, :], ALU.mult)
            last.then_inc(h_ready, 1)


_INS = ["x", "even_w_in", "even_conv_a", "even_conv_b_w", "even_conv_b_bias", "even_norm_b_g", "even_norm_b_b", "even_w_out",
        "odd_w_qkv", "odd_w_o", "ln_mix_g", "ln_mix_b", "ln_ffn_g", "ln_ffn_b", "router_group_w", "router_group_b",
        "router_expert_w", "router_expert_b", "expert_w_up", "expert_w_down", "mem_2", "positions_2", "attn_norm_2", "w_in_2",
        "mla_q_norm_2", "mla_w_uq_2", "mla_kv_norm_2", "mla_w_ukv_2", "diff_lambda_q1_2", "diff_lambda_k1_2", "diff_lambda_q2_2",
        "diff_lambda_k2_2", "diff_sub_norm_2", "w_out_2", "cross_norm_2", "mem_norm_2", "cross_wq_2", "cross_wkv_2", "cross_wo_2",
        "mlp_norm_2", "mlp_w1_2", "mlp_w2_2", "final_norm_2"]


def kernel(**inputs):
    import numpy as np
    import concourse.bacc as bacc
    from concourse.bass_utils import run_bass_kernel_spmd

    nc = bacc.Bacc("TRN2", target_bir_lowering=False, num_devices=1)
    arrays, aps = {}, {}

    def given(name, array):
        arrays[f"in_{name}_dram"] = array
        aps[name] = nc.dram_tensor(f"in_{name}_dram", array.shape, mybir.dt.from_np(array.dtype), kind="ExternalInput").ap()

    for name in _INS:
        given(name, np.ascontiguousarray(inputs[name]))
    half = MLA_ROPE // 2
    given("inv_freq", (10000.0 ** (-np.arange(half, dtype=np.float32) / np.float32(half))).astype(np.float32))
    out = nc.dram_tensor("out_0_dram", (1, T, D), F32, kind="ExternalOutput").ap()
    build(nc, aps, out)
    r = run_bass_kernel_spmd(nc, [arrays], core_ids=[0])
    return r.results[0]["out_0_dram"]
```
